# Optimizing a Trainium2 kernel written in Bass

```python
import jax, jax.numpy as jnp
from jax import lax
import numpy as np

D_MODEL = 1024
BATCH = 1
SEQ = 256
DEPTH = 1

D_MIX = D_MODEL
D_CONV = D_MIX // 2
D_RET = D_MIX - D_CONV
N_RET_HEADS = 4
RET_HEAD_DIM = D_RET // N_RET_HEADS
CONV_WIDTH = 31
CHUNK = 128
D_FF = ((8 * D_MODEL // 3 + 255) // 256) * 256
D_PLE = 256
ROPE_BASE = 10000.0
EPS = 1e-6
D_IN = 2 * D_CONV + 4 * D_RET


def rmsnorm(x, w):
    xf = x.astype(jnp.float32)
    y = xf * lax.rsqrt(jnp.mean(xf * xf, axis=-1, keepdims=True) + EPS)
    return (y * w.astype(jnp.float32)).astype(x.dtype)

def layernorm(x, w, b):
    xf = x.astype(jnp.float32)
    mu = jnp.mean(xf, axis=-1, keepdims=True)
    var = jnp.mean(jnp.square(xf - mu), axis=-1, keepdims=True)
    y = (xf - mu) * lax.rsqrt(var + EPS)
    return (y * w.astype(jnp.float32) + b.astype(jnp.float32)).astype(x.dtype)

def rotary(t, pos):
    half = t.shape[-1] // 2
    freqs = ROPE_BASE ** (-jnp.arange(half, dtype=jnp.float32) / half)
    ang = pos[:, None] * freqs[None, :]
    cos = jnp.cos(ang)[None, :, None, :]
    sin = jnp.sin(ang)[None, :, None, :]
    t1, t2 = t[..., :half], t[..., half:]
    return jnp.concatenate([t1 * cos - t2 * sin, t1 * sin + t2 * cos], axis=-1)

def conformer_conv(u_a, u_b, dw_w, dw_b, ln_w, ln_b):
    u = u_a * jax.nn.sigmoid(u_b)
    y = lax.conv_general_dilated(
        u, dw_w[:, None, :].astype(u.dtype), window_strides=(1,),
        padding=[(CONV_WIDTH - 1, 0)],
        dimension_numbers=("NWC", "WIO", "NWC"),
        feature_group_count=D_CONV)
    y = y + dw_b
    y = layernorm(y, ln_w, ln_b)
    return jax.nn.silu(y)

def chunkwise_retention(q, k, v):
    b, s, h, dh = q.shape
    nc = s // CHUNK
    log_g = jnp.log(1.0 - 2.0 ** (-5.0 - jnp.arange(h, dtype=jnp.float32)))
    idx = jnp.arange(CHUNK, dtype=jnp.float32)
    rel = idx[:, None] - idx[None, :]
    decay_in = jnp.where(rel >= 0, jnp.exp(log_g[:, None, None] * jnp.maximum(rel, 0.0)), 0.0)
    q_decay = jnp.exp(log_g[:, None] * (idx + 1.0))[None, :, :, None]
    k_decay = jnp.exp(log_g[:, None] * (CHUNK - 1.0 - idx))[None, :, :, None]
    chunk_decay = jnp.exp(log_g * CHUNK)[None, :, None, None]

    def to_chunks(t):
        return t.reshape(b, nc, CHUNK, h, dh).transpose(1, 0, 3, 2, 4)

    def step(state, qkv):
        qc, kc, vc = qkv
        scores = jnp.einsum("bhid,bhjd->bhij", qc, kc) * decay_in[None]
        inner = jnp.einsum("bhij,bhjd->bhid", scores, vc)
        cross = jnp.einsum("bhid,bhde->bhie", qc, state) * q_decay
        new_state = state * chunk_decay + jnp.einsum("bhjd,bhje->bhde", kc * k_decay, vc)
        return new_state, inner + cross

    state0 = jnp.zeros((b, h, dh, dh), jnp.float32)
    _, out = lax.scan(step, state0, (to_chunks(q), to_chunks(k), to_chunks(v)))
    return out.transpose(1, 0, 3, 2, 4).reshape(b, s, h, dh)

def retention_group(hq, hk, hv, hg):
    b, s, _ = hq.shape
    shp = (b, s, N_RET_HEADS, RET_HEAD_DIM)
    pos = jnp.arange(s, dtype=jnp.float32)
    q = rotary(hq.reshape(shp).astype(jnp.float32), pos)
    k = rotary(hk.reshape(shp).astype(jnp.float32), pos) * (RET_HEAD_DIM ** -0.5)
    v = hv.reshape(shp).astype(jnp.float32)
    o = chunkwise_retention(q, k, v)
    o = o * lax.rsqrt(jnp.mean(o * o, axis=-1, keepdims=True) + EPS)
    o = o.reshape(b, s, D_RET).astype(hg.dtype)
    return jax.nn.silu(hg) * o

def first_inputs(seed: int = 0) -> dict:
    key = jax.random.key(seed)
    ks = jax.random.split(key, 20)
    f32 = jnp.float32

    def nrm(k, shape, scale):
        return jax.random.normal(k, shape, f32) * scale

    def gain(k, shape):
        return 1.0 + 0.01 * jax.random.normal(k, shape, f32)

    L = DEPTH
    return {
        "x": nrm(ks[0], (BATCH, SEQ, D_MODEL), 1.0),
        "p": nrm(ks[1], (DEPTH, BATCH, SEQ, D_PLE), 1.0),
        "mix_pre_norm": gain(ks[2], (L, D_MODEL)),
        "w_in": nrm(ks[3], (L, D_MODEL, D_IN), D_MODEL ** -0.5),
        "conv_dw_w": nrm(ks[4], (L, CONV_WIDTH, D_CONV), CONV_WIDTH ** -0.5),
        "conv_dw_b": nrm(ks[5], (L, D_CONV), 0.01),
        "conv_ln_w": gain(ks[6], (L, D_CONV)),
        "conv_ln_b": nrm(ks[7], (L, D_CONV), 0.01),
        "w_out": nrm(ks[8], (L, D_MIX, D_MODEL), D_MIX ** -0.5),
        "mix_post_norm": gain(ks[9], (L, D_MODEL)),
        "ffn_pre_norm": gain(ks[10], (L, D_MODEL)),
        "w_ffn_gate": nrm(ks[11], (L, D_MODEL, D_FF), D_MODEL ** -0.5),
        "w_ffn_up": nrm(ks[12], (L, D_MODEL, D_FF), D_MODEL ** -0.5),
        "w_ffn_down": nrm(ks[13], (L, D_FF, D_MODEL), D_FF ** -0.5),
        "ffn_post_norm": gain(ks[14], (L, D_MODEL)),
        "w_ple_gate": nrm(ks[15], (L, D_MODEL, D_MODEL), D_MODEL ** -0.5),
        "w_ple_proj": nrm(ks[16], (L, D_PLE, D_MODEL), D_PLE ** -0.5),
        "ple_post_norm": gain(ks[17], (L, D_MODEL)),
    }

def first_block(x, p, mix_pre_norm, w_in, conv_dw_w, conv_dw_b, conv_ln_w, conv_ln_b,
              w_out, mix_post_norm, ffn_pre_norm, w_ffn_gate, w_ffn_up, w_ffn_down,
              ffn_post_norm, w_ple_gate, w_ple_proj, ple_post_norm):
    for i in range(DEPTH):
        h = rmsnorm(x, mix_pre_norm[i])
        u = h @ w_in[i]
        c0, c1 = D_CONV, 2 * D_CONV
        u_a, u_b = u[..., :c0], u[..., c0:c1]
        hq = u[..., c1:c1 + D_RET]
        hk = u[..., c1 + D_RET:c1 + 2 * D_RET]
        hv = u[..., c1 + 2 * D_RET:c1 + 3 * D_RET]
        hg = u[..., c1 + 3 * D_RET:]
        y_conv = conformer_conv(u_a, u_b, conv_dw_w[i], conv_dw_b[i], conv_ln_w[i], conv_ln_b[i])
        y_ret = retention_group(hq, hk, hv, hg)
        y = jnp.concatenate([y_conv, y_ret], axis=-1) @ w_out[i]
        x = x + rmsnorm(y, mix_post_norm[i])
        h = rmsnorm(x, ffn_pre_norm[i])
        f = (jax.nn.silu(h @ w_ffn_gate[i]) * (h @ w_ffn_up[i])) @ w_ffn_down[i]
        x = x + rmsnorm(f, ffn_post_norm[i])
        e = jax.nn.sigmoid(x @ w_ple_gate[i]) * (p[i].astype(x.dtype) @ w_ple_proj[i])
        x = x + rmsnorm(e, ple_post_norm[i])
    return x


DEPTH_2 = 2

GRID_W = 64
CTX_LEN = 256
N_MIXERS = 2
HEAD_DIM = 64
DA_HEADS = D_MODEL // (2 * HEAD_DIM)
NA_HEADS = D_MODEL // HEAD_DIM
NA_WIN_ROWS = 8
NA_WIN_COLS = 16
D_FF_2 = ((8 * D_MODEL + 3 * 256 - 1) // (3 * 256)) * 256
ROPE_THETA = 10000.0
Q_BLOCK = 128


def rmsnorm_2(x, g):
    xf = x.astype(jnp.float32)
    y = xf * lax.rsqrt(jnp.mean(xf * xf, axis=-1, keepdims=True) + EPS)
    return (y * g.astype(jnp.float32)).astype(x.dtype)

def adaln(cond, w, b):
    mod = jax.nn.silu(cond) @ w + b
    return jnp.split(mod, 6, axis=-1)

def modulate(xn, shift, scale):
    return xn * (1 + scale) + shift

def swiglu(h, w_gate_up, w_down):
    gu = h @ w_gate_up
    g, u = jnp.split(gu, 2, axis=-1)
    return (jax.nn.silu(g) * u) @ w_down

def axial_rope_tables(n):
    t = jnp.arange(n)
    row = (t // GRID_W).astype(jnp.float32)
    col = (t % GRID_W).astype(jnp.float32)
    half = HEAD_DIM // 2
    freqs = 1.0 / (ROPE_THETA ** (jnp.arange(0, half, 2, dtype=jnp.float32) / half))
    ar = row[:, None] * freqs
    ac = col[:, None] * freqs
    ang = jnp.concatenate([ar, ar, ac, ac], axis=-1)
    return jnp.cos(ang), jnp.sin(ang)

def rotate_half(x):
    x1, x2 = jnp.split(x, 2, axis=-1)
    return jnp.concatenate([-x2, x1], axis=-1)

def apply_rope(t, cos, sin):
    half = t.shape[-1] // 2
    rot = jnp.concatenate([rotate_half(t[..., :half]), rotate_half(t[..., half:])], axis=-1)
    shape = (t.shape[1],) + (1,) * (t.ndim - 3) + (t.shape[-1],)
    return t * cos.reshape(shape).astype(t.dtype) + rot * sin.reshape(shape).astype(t.dtype)

def diff_attention(h_lat, h_ctx, wqkv, lq1, lk1, lq2, lk2, subln, wo, lam_init, need_ctx_out):
    B, N, _ = h_lat.shape
    L = h_ctx.shape[1]
    scale = HEAD_DIM ** -0.5

    def proj(h):
        n = h.shape[1]
        q, k, v = jnp.split(h @ wqkv, 3, axis=-1)
        return (q.reshape(B, n, DA_HEADS, 2, HEAD_DIM),
                k.reshape(B, n, DA_HEADS, 2, HEAD_DIM),
                v.reshape(B, n, DA_HEADS, 2 * HEAD_DIM))

    q_l, k_l, v_l = proj(h_lat)
    q_c, k_c, v_c = proj(h_ctx)
    cos, sin = axial_rope_tables(N)
    q_l = apply_rope(q_l, cos, sin)
    k_l = apply_rope(k_l, cos, sin)

    f32 = jnp.float32
    lam = (jnp.exp(jnp.sum(lq1.astype(f32) * lk1.astype(f32)))
           - jnp.exp(jnp.sum(lq2.astype(f32) * lk2.astype(f32))) + lam_init)

    def attend(q_blk, k, v):
        s = jnp.einsum('bqhmd,bkhmd->bhmqk', q_blk, k).astype(f32) * scale
        p = jax.nn.softmax(s, axis=-1)
        p = p[:, :, 0] - lam * p[:, :, 1]
        return jnp.einsum('bhqk,bkhe->bqhe', p.astype(v.dtype), v)

    k_all = jnp.concatenate([k_c, k_l], axis=1)
    v_all = jnp.concatenate([v_c, v_l], axis=1)
    nblk = N // Q_BLOCK
    q_blocks = q_l.reshape(B, nblk, Q_BLOCK, DA_HEADS, 2, HEAD_DIM).transpose(1, 0, 2, 3, 4, 5)
    o_l = lax.map(lambda qb: attend(qb, k_all, v_all), q_blocks)
    o_l = o_l.transpose(1, 0, 2, 3, 4).reshape(B, N, DA_HEADS, 2 * HEAD_DIM)

    def finish(o, n):
        o = rmsnorm_2(o, subln) * (1.0 - lam_init)
        return o.reshape(B, n, D_MODEL) @ wo

    y_l = finish(o_l, N)
    y_c = finish(attend(q_c, k_c, v_c), L) if need_ctx_out else None
    return y_l, y_c

def neighbourhood_attention(h_lat, h_ctx, wqkv, rpb, wo, need_ctx_out):
    B, N, _ = h_lat.shape
    L = h_ctx.shape[1]
    rows = N // GRID_W
    wr = min(NA_WIN_ROWS, rows)
    scale = HEAD_DIM ** -0.5
    f32 = jnp.float32

    def proj(h):
        n = h.shape[1]
        q, k, v = jnp.split(h @ wqkv, 3, axis=-1)
        return tuple(t.reshape(B, n, NA_HEADS, HEAD_DIM) for t in (q, k, v))

    q_l, k_l, v_l = proj(h_lat)
    q_c, k_c, v_c = proj(h_ctx)
    kg = k_l.reshape(B, rows, GRID_W, NA_HEADS, HEAD_DIM)
    vg = v_l.reshape(B, rows, GRID_W, NA_HEADS, HEAD_DIM)
    qg = q_l.reshape(B, rows, GRID_W, NA_HEADS, HEAD_DIM).transpose(1, 0, 2, 3, 4)

    qc = np.arange(GRID_W)
    col_start = np.clip(qc - NA_WIN_COLS // 2, 0, GRID_W - NA_WIN_COLS)
    col_mask = (qc[None, :] >= col_start[:, None]) & (qc[None, :] < col_start[:, None] + NA_WIN_COLS)
    dc_idx = np.clip(qc[None, :] - qc[:, None] + NA_WIN_COLS - 1, 0, 2 * NA_WIN_COLS - 2)
    rpb_cols = rpb[:, :, dc_idx]
    col_mask = jnp.asarray(col_mask)[None, None, :, None, :]

    def row_block(args):
        q_row, r = args
        rs = jnp.clip(r - NA_WIN_ROWS // 2, 0, rows - wr)
        kb = lax.dynamic_slice_in_dim(kg, rs, wr, axis=1)
        vb = lax.dynamic_slice_in_dim(vg, rs, wr, axis=1)
        dr_idx = rs + jnp.arange(wr) - r + NA_WIN_ROWS - 1
        bias = rpb_cols[:, dr_idx].transpose(0, 2, 1, 3)
        s_band = jnp.einsum('bqhd,brkhd->bhqrk', q_row, kb).astype(f32) * scale + bias.astype(f32)
        s_band = jnp.where(col_mask, s_band, -jnp.inf)
        s_ctx = jnp.einsum('bqhd,bchd->bhqc', q_row, k_c).astype(f32) * scale
        s = jnp.concatenate([s_band.reshape(B, NA_HEADS, GRID_W, wr * GRID_W), s_ctx], axis=-1)
        p = jax.nn.softmax(s, axis=-1).astype(v_c.dtype)
        p_band = p[..., :wr * GRID_W].reshape(B, NA_HEADS, GRID_W, wr, GRID_W)
        p_ctx = p[..., wr * GRID_W:]
        return (jnp.einsum('bhqrk,brkhd->bqhd', p_band, vb)
                + jnp.einsum('bhqc,bchd->bqhd', p_ctx, v_c))

    o_l = lax.map(row_block, (qg, jnp.arange(rows)))
    y_l = o_l.transpose(1, 0, 2, 3, 4).reshape(B, N, D_MODEL) @ wo

    y_c = None
    if need_ctx_out:
        s = jnp.einsum('bqhd,bkhd->bhqk', q_c, k_c).astype(f32) * scale
        p = jax.nn.softmax(s, axis=-1).astype(v_c.dtype)
        y_c = jnp.einsum('bhqk,bkhd->bqhd', p, v_c).reshape(B, L, D_MODEL) @ wo
    return y_l, y_c

def second_inputs(seed: int = 0) -> dict:
    key = jax.random.key(seed)
    ks = jax.random.split(key, 24)
    D, F = D_MODEL, D_FF_2
    n_a = (DEPTH_2 + 1) // 2
    n_b = DEPTH_2 // 2
    nrm = jax.random.normal
    f32 = jnp.float32
    return {
        "x": nrm(ks[0], (BATCH, SEQ, D), f32),
        "c": nrm(ks[1], (BATCH, D), f32),
        "ctx": nrm(ks[2], (BATCH, CTX_LEN, D), f32),
        "c_ctx": nrm(ks[3], (D,), f32),
        "ada_w": nrm(ks[4], (DEPTH_2, D, 6 * D), f32) * D ** -0.5,
        "ada_b": nrm(ks[5], (DEPTH_2, 6 * D), f32) * 0.01,
        "norm_mix": 1.0 + 0.02 * nrm(ks[6], (DEPTH_2, D), f32),
        "norm_ffn": 1.0 + 0.02 * nrm(ks[7], (DEPTH_2, D), f32),
        "da_wqkv": nrm(ks[8], (n_a, D, 3 * D), f32) * D ** -0.5,
        "da_lambda_q1": nrm(ks[9], (n_a, HEAD_DIM), f32) * 0.1,
        "da_lambda_k1": nrm(ks[10], (n_a, HEAD_DIM), f32) * 0.1,
        "da_lambda_q2": nrm(ks[11], (n_a, HEAD_DIM), f32) * 0.1,
        "da_lambda_k2": nrm(ks[12], (n_a, HEAD_DIM), f32) * 0.1,
        "da_subln": 1.0 + 0.02 * nrm(ks[13], (n_a, 2 * HEAD_DIM), f32),
        "da_wo": nrm(ks[14], (n_a, D, D), f32) * D ** -0.5,
        "na_wqkv": nrm(ks[15], (n_b, D, 3 * D), f32) * D ** -0.5,
        "na_rpb": nrm(ks[16], (n_b, NA_HEADS, 2 * NA_WIN_ROWS - 1, 2 * NA_WIN_COLS - 1), f32) * 0.02,
        "na_wo": nrm(ks[17], (n_b, D, D), f32) * D ** -0.5,
        "ffn_w_gate_up": nrm(ks[18], (DEPTH_2, D, 2 * F), f32) * D ** -0.5,
        "ffn_w_down": nrm(ks[19], (DEPTH_2, F, D), f32) * F ** -0.5,
        "norm_final": 1.0 + 0.02 * nrm(ks[20], (D,), f32),
    }

def second_block(x, c, ctx, c_ctx, ada_w, ada_b, norm_mix, norm_ffn,
              da_wqkv, da_lambda_q1, da_lambda_k1, da_lambda_q2, da_lambda_k2, da_subln, da_wo,
              na_wqkv, na_rpb, na_wo, ffn_w_gate_up, ffn_w_down, norm_final):
    h, hc = x, ctx
    for i in range(DEPTH_2):
        last = i == DEPTH_2 - 1
        sh_m, sc_m, g_m, sh_f, sc_f, g_f = (t[:, None, :] for t in adaln(c, ada_w[i], ada_b[i]))
        csh_m, csc_m, cg_m, csh_f, csc_f, cg_f = adaln(c_ctx, ada_w[i], ada_b[i])

        xn = modulate(rmsnorm_2(h, norm_mix[i]), sh_m, sc_m)
        xc = modulate(rmsnorm_2(hc, norm_mix[i]), csh_m, csc_m)
        j = i // N_MIXERS
        if i % N_MIXERS == 0:
            lam_init = 0.8 - 0.6 * float(np.exp(-0.3 * i))
            y, yc = diff_attention(xn, xc, da_wqkv[j], da_lambda_q1[j], da_lambda_k1[j],
                                   da_lambda_q2[j], da_lambda_k2[j], da_subln[j], da_wo[j],
                                   lam_init, not last)
        else:
            y, yc = neighbourhood_attention(xn, xc, na_wqkv[j], na_rpb[j], na_wo[j], not last)

        h = h + g_m * y
        h = h + g_f * swiglu(modulate(rmsnorm_2(h, norm_ffn[i]), sh_f, sc_f),
                             ffn_w_gate_up[i], ffn_w_down[i])
        if not last:
            hc = hc + cg_m * yc
            hc = hc + cg_f * swiglu(modulate(rmsnorm_2(hc, norm_ffn[i]), csh_f, csc_f),
                                    ffn_w_gate_up[i], ffn_w_down[i])
    return rmsnorm_2(h, norm_final)


def setup_inputs(seed=0):
    out = dict(first_inputs(seed))
    for name, value in second_inputs(seed + 1).items():
        if name != "x":
            out[name + "_2"] = value
    return out


def reference(
    x, p, mix_pre_norm, w_in, conv_dw_w, conv_dw_b, conv_ln_w, conv_ln_b, w_out, mix_post_norm,
    ffn_pre_norm, w_ffn_gate, w_ffn_up, w_ffn_down, ffn_post_norm, w_ple_gate, w_ple_proj,
    ple_post_norm, c_2, ctx_2, c_ctx_2, ada_w_2, ada_b_2, norm_mix_2, norm_ffn_2, da_wqkv_2,
    da_lambda_q1_2, da_lambda_k1_2, da_lambda_q2_2, da_lambda_k2_2, da_subln_2, da_wo_2,
    na_wqkv_2, na_rpb_2, na_wo_2, ffn_w_gate_up_2, ffn_w_down_2, norm_final_2,
):
    x = first_block(
        x, p, mix_pre_norm, w_in, conv_dw_w, conv_dw_b, conv_ln_w, conv_ln_b, w_out,
        mix_post_norm, ffn_pre_norm, w_ffn_gate, w_ffn_up, w_ffn_down, ffn_post_norm,
        w_ple_gate, w_ple_proj, ple_post_norm,
    )
    return second_block(
        x, c_2, ctx_2, c_ctx_2, ada_w_2, ada_b_2, norm_mix_2, norm_ffn_2, da_wqkv_2,
        da_lambda_q1_2, da_lambda_k1_2, da_lambda_q2_2, da_lambda_k2_2, da_subln_2, da_wo_2,
        na_wqkv_2, na_rpb_2, na_wo_2, ffn_w_gate_up_2, ffn_w_down_2, norm_final_2,
    )


_drawn_inputs = setup_inputs


def setup_inputs(seed=0):
    import zlib

    import numpy as np

    out = dict(_drawn_inputs(seed))
    spreads = {}
    factors = {'mix_pre_norm': 4.377,
     'conv_dw_b': 4.599,
     'conv_ln_w': 8.0,
     'conv_ln_b': 8.0,
     'mix_post_norm': 7.416,
     'ffn_pre_norm': 7.502,
     'ffn_post_norm': 8.0,
     'ple_post_norm': 8.0,
     'ada_b_2': 4.408,
     'norm_mix_2': 8.0,
     'norm_ffn_2': 5.067,
     'da_lambda_q1_2': 7.526,
     'da_lambda_k1_2': 8.0,
     'da_subln_2': 8.0,
     'na_rpb_2': 200.0,
     'norm_final_2': 23.274}
    for name, (base, spread) in spreads.items():
        noise = np.random.default_rng([zlib.crc32(name.encode()), seed]).standard_normal(out[name].shape)
        drawn = base * np.exp(spread * noise) if base else spread * noise
        out[name] = __import__('jax').numpy.asarray(drawn.astype(out[name].dtype))
    for name, factor in factors.items():
        out[name] = (out[name] * factor).astype(out[name].dtype)
    return out
```

```python
from contextlib import ExitStack

import numpy as np

import concourse.bass as bass
from concourse import mybir

F32 = mybir.dt.float32
F32R = mybir.dt.float32r
ALU = mybir.AluOpType
ACT = mybir.ActivationFunctionType
AX_X = mybir.AxisListType.X

P = 128
D = 1024
KT = D // P
SEQ = 256
NT = 2 * SEQ
FF = 2816
FT = FF // P
EPS = 1e-6
HALF = 4
UNIT = HALF * 256
SLOTS = 4
CONV_W = 31
CONV_T = 4
RET_H = 4
DA_H = 8
NA_H = 16
LAM_INIT = 0.2
NEG = -1.0e37

PHASES = [("ada", 48), ("in_f", 10), ("in_v", 2), ("out", 4), ("gu", 22), ("dn", 12), ("pp", 1), ("pg", 4)]
for _l in range(2):
    PHASES += [(f"q{_l}", 4), (f"k{_l}", 4), (f"v{_l}", 4), (f"wo{_l}", 4), (f"gu{_l}", 22), (f"dn{_l}", 12)]


class Phase:

    def __init__(self, name, step0, steps, pair0):
        self.name, self.step0, self.steps, self.pair0 = name, step0, steps, pair0
        self.per_pair = 3 if name.startswith("dn") else 1
        self.body = 1 if name == "pp" else 2 * self.per_pair
        self.iters = steps // self.body
        self.pairs = 4 if name == "pp" else steps // self.per_pair


def plan():
    out, step, pair = {}, 0, 0
    for name, steps in PHASES:
        out[name] = ph = Phase(name, step, steps, pair)
        step += steps
        pair += ph.pairs
    return out, step


PH, STEPS = plan()
UNITS = 2 * STEPS
XL_COUNT = {"m0": 6 * KT, "f0": 8 * KT, "m1": 10 * KT, "f1": 11 * KT}
NORMS = ["pre1", "post1", "fpre1", "fpost1", "ple1", "m0", "f0", "m1", "f1", "final"]

PCOLS = [("mix_pre", KT), ("mix_post", KT), ("ffn_pre", KT), ("ffn_post", KT), ("ple_post", KT), ("final", KT),
         ("n_mix", 2 * KT), ("n_ffn", 2 * KT), ("ada_b", 96), ("conv_w", CONV_T * CONV_W), ("conv_b", CONV_T),
         ("ln_w", CONV_T), ("ln_b", CONV_T), ("cond", 2 * KT), ("subln", 1), ("lam", 256)]
PAT = {}
_at = 0
for _n, _w in PCOLS:
    PAT[_n] = (_at, _w)
    _at += _w
NPAR = _at


def build(nc, wall, xin, pin, par, tab, tab_ret, tab_rope, tab_mask, rpb, out):
    with ExitStack() as ctx:
        sems = {}

        def S(name):
            if name not in sems:
                sems[name] = ctx.enter_context(nc.semaphore(name))
            return sems[name]

        base = nc.sbuf_base
        base = (base + 31) // 32 * 32
        limit = nc.sbuf_usable_end
        arena_bytes = (limit - base) // 32 * 32
        ctx.enter_context(nc.sbuf_tensor("arena", [P, arena_bytes // 4], F32))
        cursor = [base]

        def at(name, shape, offset, dt=F32):
            size = 4 * int(np.prod(shape[1:]))
            assert offset + size <= base + arena_bytes, (name, offset + size - base - arena_bytes)
            return nc.alloc_sbuf_tensor_at(name, shape, dt, offset=offset)

        def sb(name, shape, dt=F32):
            o = cursor[0]
            cursor[0] = (o + 4 * int(np.prod(shape[1:])) + 31) // 32 * 32
            return at(name, shape, o, dt)

        class Region:

            def __init__(self, offset, size):
                self.o, self.end = offset, offset + size

            def take(self, name, shape, dt=F32):
                o = self.o
                self.o = (o + 4 * int(np.prod(shape[1:])) + 31) // 32 * 32
                assert self.o <= self.end, (name, self.o - self.end)
                return at(name, shape, o, dt)

        h = sb("h", [P, KT, NT])
        xs_at = cursor[0]
        xh = sb("xh", [P, KT, NT], F32R)
        xl = sb("xl", [P, KT, NT], F32R)
        y = sb("y", [P, KT, NT])
        y_at = cursor[0] - 4 * KT * NT
        raw = sb("raw", [P, SLOTS, HALF, 256])
        wh = sb("wh", [P, SLOTS, HALF, 256], F32R)
        wl = sb("wl", [P, SLOTS, HALF, 256], F32R)
        rstd = sb("rstd", [P, NT])
        prm = sb("prm", [P, NPAR])
        ones = sb("ones", [P, P])
        ident = sb("ident", [P, P])
        mod = sb("mod", [P, 2, 48, 2])
        gsc = sb("gsc", [P, 2, 2, KT, 2])
        lam4 = sb("lam4", [P, 8])
        eps = sb("eps", [P, 1])
        big_at = cursor[0]
        BIG = 4 * FT * NT * 2
        assert big_at + BIG <= base + arena_bytes, big_at + BIG - base - arena_bytes

        sq = at("sq", [P, KT, NT], xs_at)
        fh = {SEQ: at("fh1", [P, FT, SEQ], big_at, F32R), NT: at("fh2", [P, FT, NT], big_at, F32R)}
        fl = {SEQ: at("fl1", [P, FT, SEQ], big_at + 4 * FT * SEQ, F32R),
              NT: at("fl2", [P, FT, NT], big_at + 4 * FT * NT, F32R)}
        sil = at("sil", [P, 2, NT], y_at)
        ft = at("ft", [P, 2, NT], y_at + 8 * NT)

        r = Region(big_at, BIG)
        u = r.take("u", [P, 20, SEQ])
        vb = r.take("vb", [P, 2, 512])
        up = r.take("up", [P, CONV_T, CONV_W - 1 + SEQ])
        cy = r.take("cy", [P, CONV_T, SEQ])
        sw = r.take("sw", [P, 8, SEQ])
        st = r.take("st", [P, RET_H, 384])
        on = r.take("on", [P, 2, RET_H, P])
        dt_ = r.take("dt_", [P, RET_H, 384])
        rcs = r.take("rcs", [P, 2, SEQ])
        ssq = r.take("ssq", [P, 8])
        cs = r.take("cs", [P, KT, P], F32R)
        csf = r.take("csf", [P, KT, 2])
        row = r.take("row", [4, 2, 256])
        sel = r.take("sel", [4, 2])
        mix = at("mix", [P, KT, SEQ], y_at)
        r = Region(big_at, BIG)
        ptf = r.take("ptf", [P, 2, SEQ])
        pth = r.take("pth", [P, 2, SEQ], F32R)
        ptl = r.take("ptl", [P, 2, SEQ], F32R)
        ppo = r.take("ppo", [P, KT, SEQ])
        r = Region(big_at, BIG)
        qk = r.take("qk", [P, 2, KT, NT])
        vv = r.take("vv", [P, 4, D])
        e2 = r.take("e2", [P, 2, 2, 512])
        pt = r.take("pt", [P, 2, 4, P])
        rtmp = r.take("rtmp", [P, 2, 2, SEQ])
        qkr = r.take("qkr", [P, 2, 2, NT])
        sm = r.take("sm", [P, 2, 16])
        ort = r.take("ort", [P, 4, DA_H])
        rope = r.take("rope", [P, 2, SEQ])
        sww = at("sww", [P, 2, KT, SEQ], y_at)
        osq = at("osq", [P, 4, DA_H, P], y_at)
        r = Region(big_at, BIG)
        q1 = r.take("q1", [P, KT, SEQ])
        k1 = r.take("k1", [P, KT, NT])
        v1 = r.take("v1", [P, 4, D])
        bias = r.take("bias", [P, 2, NA_H, SEQ])
        e1 = r.take("e1", [P, 2, 512])
        pt1 = r.take("pt1", [P, 2, 4, P])
        sm1 = r.take("sm1", [P, 4, 8])
        qks = r.take("qks", [P, 2, SEQ + NT])
        o1 = at("o1", [P, 2, D], y_at)
        s1 = at("s1", [P, 2, 512], y_at + 8 * D)
        mask = at("mask", [P, SEQ], y_at + 12 * D)

        ps = ctx.enter_context(nc.psum_tensor("ps", [P, 8, 512], F32))

        def par_ap(name, a=0, n=None):
            o, w = PAT[name]
            n = w - a if n is None else n
            return prm[:, o + a:o + a + n]

        landed = [S(f"landed{k}") for k in range(SLOTS)]
        hi_ready, lo_ready = S("hi_ready"), S("lo_ready")
        units_done = S("units_done")
        bank_free = S("bank_free")

        def par_ap(name, a=0, n=None):
            o, w = PAT[name]
            n = w - a if n is None else n
            return prm[:, o + a:o + a + n]

        def run(eng, ph, body, peel=0):
            if ph.iters - peel > 1:
                with eng.Fori(0, ph.iters - peel) as i:
                    body(i)
            elif ph.iters - peel == 1:
                body(0)
            for i in range(ph.iters - peel, ph.iters):
                body(i)

        def pair_done(eng, ph, i, pair):
            eng.wait_ge(units_done, i * (2 * ph.body) + (2 * ph.step0 + 2 * ph.per_pair * (pair + 1) + SLOTS))

        def settled(eng):
            eng.wait_ge(S("x_in"), 16)

        class Link:

            def __init__(self, eng, name):
                self.eng, self.sem, self.n, self.off = eng, S(name), 0, 0

            def __call__(self, ins):
                self.n += 1
                ins.then_inc(self.sem, 1)
                self.eng.wait_ge(self.sem, self.off + self.n)

            def begin(self, i, per):
                self.off, self.per, self.n0 = i * per, per, self.n

            def end(self, iters):
                assert self.n - self.n0 == self.per, (self.n - self.n0, self.per)
                self.n, self.off = self.n0 + self.per * iters, 0

        block = ctx.enter_context(nc.Block())

        @block.sync
        def _(sp):
            def load(u_, slot):
                sp.wait_ge(lo_ready, u_ + 1)
                sp.dma_start(raw[:, slot, :, :], wall[u_, :, :, :]).then_inc(landed[slot], 16)

            sp.dma_start(prm[:], par).then_inc(S("prm_in"), 16)
            sp.dma_start(ident[:], tab[:, 0:P]).then_inc(S("tab_in"), 16)
            sp.dma_start(sel[:], tab[0:4, P:P + 2]).then_inc(S("tab_in"), 16)
            for s in range(SLOTS):
                load(s, s)
            sp.dma_start(h[:], xin).then_inc(S("x_in"), 16)
            sp.dma_start(dt_[:], tab_ret[:, 0:RET_H * 384].rearrange("p (a b) -> p a b", a=RET_H))\
                .then_inc(S("ret_in"), 16)
            sp.dma_start(rcs[:], tab_ret[:, RET_H * 384:].rearrange("p (a b) -> p a b", a=2))\
                .then_inc(S("ret_in"), 16)
            with sp.Fori(1, UNITS // SLOTS) as i:
                for s in range(SLOTS):
                    load(i * SLOTS + s, s)
            for u_ in range(UNITS // SLOTS * SLOTS, UNITS):
                load(u_, u_ % SLOTS)
            sp.wait_ge(S("final_ready"), KT)
            sp.dma_start(out, y[:, :, 0:SEQ]).then_inc(S("stored"), 16)
            sp.wait_ge(S("stored"), 16)

        @block.gpsimd
        def _(pool):
            def low(u_, slot):
                pool.wait_ge(hi_ready, u_ + 1)
                nc.gpsimd.tensor_tensor(wl[:, slot, :, :], raw[:, slot, :, :], wh[:, slot, :, :].bitcast(F32),
                                        ALU.subtract).then_inc(lo_ready, 1)

            pool.sem_inc(lo_ready, SLOTS)
            nc.gpsimd.memset(eps[:], EPS).then_inc(S("consts"), 1)
            nc.gpsimd.memset(ones[:], 1.0).then_inc(S("consts"), 1)
            with pool.Fori(0, UNITS // SLOTS) as i:
                for s in range(SLOTS):
                    low(i * SLOTS + s, s)
            for u_ in range(UNITS // SLOTS * SLOTS, UNITS):
                low(u_, u_ % SLOTS)

        @block.scalar
        def _(act):
            def high(u_, n, slot):
                act.wait_ge(landed[slot], n * 16)
                act.wait_ge(units_done, u_ + 1)
                nc.scalar.activation(wh[:, slot, :, :], raw[:, slot, :, :], ACT.Copy).then_inc(hi_ready, 1)

            def high_step(ph, i, j):
                for half in range(2):
                    c = 2 * (ph.step0 + j + 1) + half
                    if isinstance(i, int) and c + 2 * ph.body * i >= UNITS:
                        return
                    high(i * (2 * ph.body) + c, i * (2 * ph.body // SLOTS) + (c // SLOTS + 1), c % SLOTS)

            def stream_only(ph, peel=0):
                def body(i):
                    for j in range(ph.body):
                        high_step(ph, i, j)
                run(act, ph, body, peel)

            def norm(name, src, n):
                for k in range(0, KT, 2):
                    nc.scalar.activation(sq[:, k:k + 2, 0:n], src[:, k:k + 2, 0:n], ACT.Square)\
                        .then_inc(S("sq_ready"), 1)
                act.wait_ge(S("sum_ready"), NORMS.index(name) + 1)
                nc.scalar.activation(rstd[:, 0:n], ps[:, 4, 0:n], ACT.Sqrt, scale=1.0 / D, bias=eps[:, 0:1])\
                    .then_inc(S("root_ready"), 1)

            def split(sem, count0, src, n, scale=None):
                for k in range(KT):
                    act.wait_ge(S(sem), count0 + k + 1)
                    nc.scalar.activation(xh[:, k, 0:n], src[:, k, 0:n], ACT.Copy,
                                         scale=1.0 if scale is None else scale[:, k:k + 1]).then_inc(S("xh_ready"), 1)

            def split_shifted(count0, l, shift, n):
                for k in range(KT):
                    act.wait_ge(S("xr_ready"), count0 + k + 1)
                    for c in range(n // SEQ):
                        t = slice(c * SEQ, c * SEQ + SEQ)
                        nc.scalar.activation(xh[:, k, t], y[:, k, t], ACT.Identity,
                                             bias=mod[:, l, 8 * shift + k, c:c + 1]).then_inc(S("xh_ready"), 1)

            act.sem_inc(S("ne_ready"), 2)
            act.wait_ge(S("prm_in"), 16)
            nc.scalar.activation(csf[:], par_ap("cond").rearrange("p (t c) -> p t c", c=2), ACT.Silu)\
                .then_inc(S("cond_ready"), 1)
            act.wait_ge(S("cond_ready"), 1)
            act.wait_ge(S("cs_zero"), 1)
            nc.scalar.activation(cs[:, :, 0:2], csf[:], ACT.Copy).then_inc(S("cond_hi"), 1)
            for u_ in range(2):
                high(u_, 1, u_)
            act.wait_ge(S("lam_dot"), 1)
            nc.scalar.activation(lam4[:, 2:4], lam4[:, 0:2], ACT.Exp).then_inc(S("lam_exp"), 1)
            stream_only(PH["ada"])

            act.wait_ge(S("x_in"), 16)
            act.wait_ge(S("consts"), 2)
            norm("pre1", h, SEQ)
            split("xr_ready", 0, y, SEQ, par_ap("mix_pre"))
            stream_only(PH["in_f"])
            act.wait_ge(bank_free, PH["in_v"].pair0 + 2)
            for half in range(2):
                a, b = slice(64 * half, 64 * half + 64), slice(64 - 64 * half, 128 - 64 * half)
                act.dma_start(sw[a, :, :], u[b, 8:16, :]).then_inc(S("ret_swap"), 16)
            stream_only(PH["in_v"])
            nc.scalar.activation(u[:, 4:8, :], u[:, 4:8, :], ACT.Sigmoid).then_inc(S("sig_ready"), 1)
            nc.scalar.activation(u[:, 16:20, :], u[:, 16:20, :], ACT.Silu).then_inc(S("gate_ready"), 1)
            act.wait_ge(S("ret_o"), 1)
            nc.scalar.activation(on[:], ps[:, 2:4, :].rearrange("p a (b c) -> p a b c", b=RET_H), ACT.Square)\
                .then_inc(S("ret_sq"), 1)
            act.wait_ge(S("ret_ssq"), 1)
            nc.scalar.activation(ssq[:], ssq[:], ACT.Sqrt, scale=1.0 / P, bias=eps[:, 0:1]).then_inc(S("ret_root"), 1)
            act.wait_ge(S("dev_ready"), 1)
            nc.scalar.activation(sq[:, 0:4, 0:SEQ], cy[:], ACT.Square).then_inc(S("dev_sq"), 1)
            act.wait_ge(S("ln_sum"), 2)
            nc.scalar.activation(rstd[:, 0:SEQ], ps[:, 5, 0:SEQ], ACT.Sqrt, scale=1.0 / 512, bias=eps[:, 0:1])\
                .then_inc(S("ln_root"), 1)
            act.wait_ge(S("ln_scaled"), 1)
            for c in range(CONV_T):
                nc.scalar.activation(mix[:, c, :], cy[:, c, :], ACT.Silu, scale=par_ap("ln_w", c, 1),
                                     bias=par_ap("ln_b", c, 1)).then_inc(S("mix_conv"), 1)
            act.wait_ge(S("mix_conv"), CONV_T)
            split("mix_ret", 0, mix, SEQ)
            stream_only(PH["out"])
            act.wait_ge(bank_free, PH["gu"].pair0 + 2)
            norm("post1", y, SEQ)
            act.wait_ge(S("h_ready"), KT)
            norm("fpre1", h, SEQ)
            split("xr_ready", KT, y, SEQ, par_ap("ffn_pre"))

            def gate_up(ph, n, f0):
                def body(i):
                    for j in range(2):
                        high_step(ph, i, j)
                        pair_done(act, ph, i, j)
                        act.wait_ge(S("f_lo"), i * 2 + (f0 + j + 1))
                        nc.scalar.activation(sil[:, j, 0:n], ps[:, 2 * j, 0:n], ACT.Silu).then_inc(S("silu_ready"), 1)
                        act.wait_ge(bank_free, i * 2 + (ph.pair0 + j + 3))
                        settled(act)
                        nc.scalar.activation(fh[n][:, i * 2 + j, :], ft[:, j, 0:n], ACT.Copy).then_inc(S("f_hi"), 1)
                run(act, ph, body)

            gate_up(PH["gu"], SEQ, 0)
            stream_only(PH["dn"])
            act.wait_ge(bank_free, PH["pp"].pair0 + 2)
            act.dma_start(ptf[:], pin).then_inc(S("p_in"), 16)
            norm("fpost1", y, SEQ)
            act.wait_ge(S("p_in"), 16)
            nc.scalar.activation(pth[:], ptf[:], ACT.Copy).then_inc(S("p_hi"), 1)
            high_step(PH["pp"], 0, 0)
            split("h_ready", KT, h, SEQ)

            def gate_e(i):
                ph = PH["pg"]
                for j in range(2):
                    high_step(ph, i, j)
                    pair_done(act, ph, i, j)
                    act.wait_ge(bank_free, i * 2 + (ph.pair0 + j + 1))
                    nc.scalar.activation(sil[:, j, :].rearrange("p (a b) -> p a b", a=2),
                                         ps[:, 2 * j:2 * j + 2, 0:SEQ], ACT.Sigmoid).then_inc(S("sigm_ready"), 1)
            run(act, PH["pg"], gate_e)
            act.wait_ge(bank_free, PH["q0"].pair0 + 2)
            norm("ple1", ppo, SEQ)
            act.wait_ge(S("h_ready"), 3 * KT)
            act.dma_start(rope[:], tab_rope).then_inc(S("rope_in"), 16)

            for l in range(2):
                norm(f"m{l}", h, NT)
                split_shifted((2 + 2 * l) * KT, l, 0, NT)
                stream_only(PH[f"q{l}"])
                if l == 1:
                    act.wait_ge(S("xl_ready"), XL_COUNT["m1"])
                    act.dma_start(mask[:], tab_mask).then_inc(S("mask_in"), 16)
                    for t in range(2):
                        for rr in range(2):
                            row0 = 2 * t + rr
                            for kr in range(4):
                                src = bass.AP(rpb.tensor, (kr + 7 - row0) * 31 + 15 - 63, [[1, 64], [15 * 31, NA_H], [1, 64]])
                                act.dma_start(bias[64 * rr:64 * rr + 64, t, :, 64 * kr:64 * kr + 64], src)\
                                    .then_inc(S("bias_in"), 16)
                stream_only(PH[f"k{l}"])
                if l == 0:
                    act.wait_ge(bank_free, PH["v0"].pair0 + 2)
                    for b in range(4):
                        src, dst = slice(32 * b, 32 * b + 32), slice(32 * (b ^ 1), 32 * (b ^ 1) + 32)
                        for m in range(2):
                            act.dma_start(sww[dst, m, :, :], qk[src, m, :, 0:SEQ]).then_inc(S("swap_in"), 16)
                stream_only(PH[f"v{l}"])
                if l == 0:
                    def exps(v, q, k3):
                        act.wait_ge(S("pt_psum"), v + 1)
                        for m in range(2):
                            act.wait_ge(S("s_max"), v + 1)
                            for t in range(1 if k3 < 2 else 2):
                                c = slice(0, 512) if k3 < 2 else slice(t * 256, t * 256 + 256)
                                nc.scalar.activation(e2[:, q, m, c], ps[:, 2 * q + m, c], ACT.Exp, scale=0.125,
                                                     bias=sm[:, q, 2 * t + m:2 * t + m + 1],
                                                     accum_out=sm[:, q, 4 + 2 * t + m:5 + 2 * t + m])\
                                    .then_inc(S("e_ready"), 2 if k3 < 2 else 1)

                    def probs(v, q):
                        act.wait_ge(S("pt_psum"), v + 3)
                        act.wait_ge(S("pv_done"), v + 1)
                        nc.scalar.activation(pt[:, q, :, :], ps[:, 4 + q, :].rearrange("p (a b) -> p a b", a=4), ACT.Copy)\
                            .then_inc(S("pt_ready"), 1)

                    with act.Fori(0, DA_H // 2) as i:
                        for w in range(6):
                            if w % 3 == 0:
                                act.wait_ge(S("s_ready"), i * 6 + (w + 3))
                                settled(act)
                                nc.scalar.activation(qkr[:, w // 3, :, SEQ:NT], qk[:, :, i * 2 + w // 3, SEQ:NT], ACT.Copy)\
                                    .then_inc(S("qkr_ctx"), 1)
                            exps(i * 6 + w, w % 2, w % 3)
                            if w:
                                probs(i * 6 + w - 1, (w - 1) % 2)
                        probs(i * 6 + 5, 1)
                    act.wait_ge(S("o_taken"), 2 + 3 * DA_H)
                    for t in range(4):
                        nc.scalar.activation(osq[:, t, :, :], qk[:, 0, :, t * P:t * P + P], ACT.Square)\
                            .then_inc(S("da_sq"), 1)
                    act.wait_ge(S("da_ssq"), 1)
                    nc.scalar.activation(ort[:], ort[:], ACT.Sqrt, scale=1.0 / P, bias=eps[:, 0:1]).then_inc(S("da_root"), 1)
                    for t in range(4):
                        for b in range(2):
                            act.wait_ge(S("o_t"), 2 * t + b + 1)
                            nc.scalar.activation(xh[:, 4 * b:4 * b + 4, t * P:t * P + P],
                                                 ps[:, b + 2 * (t % 2), :].rearrange("p (a b) -> p a b", a=4), ACT.Copy,
                                                 scale=par_ap("subln")).then_inc(S("oh_ready"), 1)
                else:
                    def nprobs(v, q):
                        act.wait_ge(S("npt_psum"), v + 3)
                        act.wait_ge(S("npv_done"), v + 1)
                        nc.scalar.activation(pt1[:, q, :, :], ps[:, 4 + q, :].rearrange("p (a b) -> p a b", a=4), ACT.Copy)\
                            .then_inc(S("npt_ready"), 1)

                    act.wait_ge(bank_free, PH["wo1"].pair0 + 2)
                    with act.Fori(0, KT // 2) as i:
                        for w in range(8):
                            q, b = w % 2, w // 4
                            if w % 4 == 0:
                                act.wait_ge(S("ns_ready"), i * 8 + (w + 4))
                                settled(act)
                                nc.scalar.activation(qks[:, b, 0:SEQ], q1[:, i * 2 + b, :], ACT.Copy)
                                nc.scalar.activation(qks[:, b, SEQ:], k1[:, i * 2 + b, :], ACT.Copy).then_inc(S("qks_ready"), 1)
                            act.wait_ge(S("npt_psum"), i * 8 + (w + 1))
                            act.wait_ge(S("ns_max"), i * 8 + (w + 1))
                            nc.scalar.activation(e1[:, q, :], s1[:, q, :], ACT.Exp, bias=sm1[:, w % 4, 1:2],
                                                 accum_out=sm1[:, w % 4, 2:3]).then_inc(S("ne_ready"), 1)
                            if w:
                                nprobs(i * 8 + w - 1, (w - 1) % 2)
                        nprobs(i * 8 + 7, 1)
                    for t in range(2):
                        for b in range(2):
                            act.wait_ge(S("no_t"), 2 * t + b + 1)
                            nc.scalar.activation(xh[:, 4 * b:4 * b + 4, t * P:t * P + P].rearrange("p a (r c) -> p a r c", c=64),
                                                 ps[:, b + 2 * t, :].rearrange("p (a r c) -> p a r c", a=4, c=64)[:, :, :, ::-1],
                                                 ACT.Copy)\
                                .then_inc(S("oh_ready"), 1)
                n = NT if l == 0 else SEQ
                stream_only(PH[f"wo{l}"])
                act.wait_ge(bank_free, PH[f"gu{l}"].pair0 + 2)
                norm(f"f{l}", h, n)
                split_shifted((3 + 2 * l) * KT, l, 3, n)
                gate_up(PH[f"gu{l}"], n, FT * (l + 1))
                stream_only(PH[f"dn{l}"], peel=l)
                act.wait_ge(bank_free, PH[f"dn{l}"].pair0 + PH[f"dn{l}"].pairs + 2)
            norm("final", h, SEQ)

        @block.tensor
        def _(pe):
            def unit_ready(ph, i, j, half):
                c = 2 * (ph.step0 + j) + half
                pe.wait_ge(lo_ready, i * (2 * ph.body) + (c + 1 + SLOTS))
                return c % SLOTS

            def banks_ready(ph, i, pair):
                pe.wait_ge(bank_free, i * 2 + (ph.pair0 + pair + 1))

            def three(o, wa, wb, xa, xb, start, stop):
                nc.tensor.matmul(o, wa, xa, start=start, stop=False)
                nc.tensor.matmul(o, wa, xb, start=False, stop=False)
                return nc.tensor.matmul(o, wb, xa, start=False, stop=stop)

            def features(ph, n, a=xh, b=xl, ktiles=KT):
                def body(i):
                    for j in range(ph.body):
                        pair = j // ph.per_pair
                        if j % ph.per_pair == 0:
                            banks_ready(ph, i, pair)
                        for half in range(2):
                            slot = unit_ready(ph, i, j, half)
                            k0 = 2 * HALF * (j % ph.per_pair) + HALF * half
                            for o in range(2):
                                c = slice(o * P, o * P + P)
                                for kk in range(min(HALF, ktiles - k0)):
                                    k = k0 + kk
                                    mm = three(ps[:, 2 * pair + o, 0:n], wh[:, slot, kk, c], wl[:, slot, kk, c],
                                               a[:, k, 0:n], b[:, k, 0:n], k == 0, k == ktiles - 1)
                            mm.then_inc(units_done, 1)
                run(pe, ph, body)

            def tokens(ph, tiles):
                def body(i):
                    for j in range(2):
                        banks_ready(ph, i, j)
                        for half in range(2):
                            slot = unit_ready(ph, i, j, half)
                            for t in range(tiles):
                                o = ps[:, 2 * j + t // 2, (t % 2) * 256:(t % 2) * 256 + 256]
                                for kk in range(HALF):
                                    k = HALF * half + kk
                                    xa, xb = xh[:, k, t * P:t * P + P], xl[:, k, t * P:t * P + P]
                                    s0, s1_ = k == 0 and t % 2 == 0, k == KT - 1
                                    nc.tensor.matmul(o, xa, wh[:, slot, kk, :], start=s0, stop=False, skip_group_check=True)
                                    nc.tensor.matmul(o, xb, wh[:, slot, kk, :], start=False, stop=False, skip_group_check=True)
                                    mm = nc.tensor.matmul(o, xa, wl[:, slot, kk, :], start=False, stop=s1_,
                                                          skip_group_check=True)
                            mm.then_inc(units_done, 1)
                run(pe, ph, body)

            def norm_sum(name, n):
                m = NORMS.index(name)
                if m:
                    pe.wait_ge(S("root_ready"), m)
                for k in range(KT):
                    if k % 2 == 0:
                        pe.wait_ge(S("sq_ready"), 4 * m + k // 2 + 1)
                    mm = nc.tensor.matmul(ps[:, 4, 0:n], ones[:], sq[:, k, 0:n], start=k == 0, stop=k == KT - 1)
                mm.then_inc(S("sum_ready"), 1)

            pe.sem_inc(units_done, SLOTS)
            for name, n in (("mod_psum", 2), ("s_ready", 6), ("pt_psum", 2), ("pv_done", 2), ("ns_ready", 8),
                            ("npt_psum", 2), ("npv_done", 2)):
                pe.sem_inc(S(name), n)
            pe.wait_ge(S("consts"), 2)
            pe.wait_ge(S("tab_in"), 32)

            ph = PH["ada"]
            pe.wait_ge(S("cond_lo"), 1)
            with pe.Fori(0, ph.iters) as i:
                for j in range(2):
                    banks_ready(ph, i, j)
                    for half in range(2):
                        slot = unit_ready(ph, i, j, half)
                        for kk in range(HALF):
                            k = HALF * half + kk
                            nc.tensor.matmul(ps[:, j, 0:256], cs[:, k, :], wh[:, slot, kk, :], start=k == 0, stop=False)
                            mm = nc.tensor.matmul(ps[:, j, 0:256], cs[:, k, :], wl[:, slot, kk, :], start=False,
                                                  stop=k == KT - 1)
                        mm.then_inc(units_done, 1)
                for j in range(2):
                    pe.wait_ge(bank_free, i * 2 + (j + 3))
                    for c in range(2):
                        mm = nc.tensor.matmul(ps[:, 7, bass.ds(i * 8 + (4 * j + 2 * c), 2)],
                                              row[:, j, c * P:c * P + P], sel[:], start=True, stop=True)
                    mm.then_inc(S("mod_psum"), 1)

            norm_sum("pre1", SEQ)
            pe.wait_ge(S("xl_ready"), KT)
            features(PH["in_f"], SEQ)
            tokens(PH["in_v"], 2)
            pe.wait_ge(S("ret_roped"), 1)
            pe.wait_ge(bank_free, PH["out"].pair0 + 2)
            for hd in range(RET_H):
                b = hd % 2
                if hd >= 2:
                    pe.wait_ge(S("ret_s"), hd - 1)
                q_, k_ = u[:, 8 + hd, :], u[:, 12 + hd, :]
                nc.tensor.matmul(ps[:, b, 0:256], k_[:, 0:P], q_, start=True, stop=True)
                nc.tensor.matmul(ps[:, b, 256:384], k_[:, P:256], q_[:, P:256], start=True, stop=True)\
                    .then_inc(S("ret_sc"), 1)
            for hd in range(RET_H):
                pe.wait_ge(S("ret_s"), hd + 1)
                c = slice(hd * P, hd * P + P)
                nc.tensor.matmul(ps[:, 2, c], st[:, hd, 0:P], vb[:, 0, c], start=True, stop=True)
                nc.tensor.matmul(ps[:, 3, c], st[:, hd, P:256], vb[:, 0, c], start=True, stop=False)
                mm = nc.tensor.matmul(ps[:, 3, c], st[:, hd, 256:384], vb[:, 1, c], start=False, stop=True)
            mm.then_inc(S("ret_o"), 1)
            pe.wait_ge(S("ret_on"), 1)
            for hd in range(RET_H):
                for t in range(2):
                    mm = nc.tensor.transpose(ps[:, hd // 2, (hd % 2) * 256 + t * P:(hd % 2) * 256 + t * P + P],
                                             on[:, t, hd, :], ident[:])
            mm.then_inc(S("ret_t"), 1)
            pe.wait_ge(S("conv_tap"), CONV_T * CONV_W)
            for c in range(CONV_T):
                mm = nc.tensor.matmul(ps[:, 4, 0:SEQ], ones[:], cy[:, c, :], start=c == 0, stop=c == CONV_T - 1)
            mm.then_inc(S("ln_sum"), 1)
            pe.wait_ge(S("dev_sq"), 1)
            for c in range(CONV_T):
                mm = nc.tensor.matmul(ps[:, 5, 0:SEQ], ones[:], sq[:, c, 0:SEQ], start=c == 0, stop=c == CONV_T - 1)
            mm.then_inc(S("ln_sum"), 1)
            pe.wait_ge(S("xl_ready"), 2 * KT)
            features(PH["out"], SEQ)
            norm_sum("post1", SEQ)
            norm_sum("fpre1", SEQ)
            pe.wait_ge(S("xl_ready"), 3 * KT)
            features(PH["gu"], SEQ)
            pe.wait_ge(S("f_lo"), 2 + FT)
            features(PH["dn"], SEQ, fh[SEQ], fl[SEQ], FT)
            norm_sum("fpost1", SEQ)
            ph = PH["pp"]
            pe.wait_ge(S("p_lo"), 1)
            slots = [unit_ready(ph, 0, 0, half) for half in range(2)]
            flat = [(wh[:, s, :, :].rearrange("p a b -> p (a b)"), wl[:, s, :, :].rearrange("p a b -> p (a b)")) for s in slots]
            for pair in range(4):
                pe.wait_ge(bank_free, ph.pair0 + pair + 1)
                for o in range(2 * pair, 2 * pair + 2):
                    for k in range(2):
                        mm = three(ps[:, 2 * (pair % 2) + o % 2, 0:SEQ], flat[k][0][:, o * P:o * P + P],
                                   flat[k][1][:, o * P:o * P + P], pth[:, k, :], ptl[:, k, :], k == 0, k == 1)
                if pair < 3:
                    mm.then_inc(S("pp_ready"), 1)
            mm.then_inc(units_done, 2)
            pe.wait_ge(S("xl_ready"), 4 * KT)
            features(PH["pg"], SEQ)
            norm_sum("ple1", SEQ)

            for l in range(2):
                n = NT if l == 0 else SEQ
                norm_sum(f"m{l}", NT)
                pe.wait_ge(S("xl_ready"), XL_COUNT[f"m{l}"])
                features(PH[f"q{l}"], n)
                features(PH[f"k{l}"], NT)
                tokens(PH[f"v{l}"], 4)
                pe.wait_ge(bank_free, PH[f"wo{l}"].pair0 + 2)
                if l == 0:
                    def scores(v, hh, k3, q):
                        pe.wait_ge(S("e_ready"), v * 4 + 4)
                        for m in range(2):
                            rows = slice(64 * m, 64 * m + 64)
                            if k3 < 2:
                                mm = nc.tensor.matmul(ps[:, 2 * q + m, :], qkr[rows, hh, 0, k3 * P:k3 * P + P],
                                                      qkr[rows, hh, 1, :], start=True, stop=True)
                            else:
                                for t in range(2):
                                    mm = nc.tensor.matmul(ps[:, 2 * q + m, t * 256:t * 256 + 256],
                                                          qkr[rows, hh, 0, SEQ + t * P:SEQ + t * P + P],
                                                          qkr[rows, hh, 1, SEQ:NT], start=True, stop=True)
                        mm.then_inc(S("s_ready"), 1)

                    def values(v, head, k3, q):
                        pe.wait_ge(S("p_ready"), v + 1)
                        pe.wait_ge(S("pt_ready"), v + 1)
                        for t in range(4):
                            mm = nc.tensor.transpose(ps[:, 4 + q, t * P:t * P + P], e2[:, q, 0, t * P:t * P + P], ident[:])
                        mm.then_inc(S("pt_psum"), 1)
                        pe.wait_ge(S("pt_ready"), v + 3)
                        pe.wait_ge(S("o_taken"), v + 1)
                        for t in range(1 if k3 < 2 else 2):
                            for c in range(4 if k3 < 2 else 2):
                                mm = nc.tensor.matmul(ps[:, 6 + q, t * P:t * P + P], pt[:, q, 2 * t + c, :],
                                                      vv[:, c if k3 < 2 else 2 + c, bass.ds(head * P, P)], start=c == 0,
                                                      stop=c == (3 if k3 < 2 else 1))
                        mm.then_inc(S("pv_done"), 1)

                    with pe.Fori(0, DA_H // 2) as i:
                        for w in range(6):
                            if w % 3 == 0:
                                pe.wait_ge(S("qkr_ready"), i * 2 + (w // 3 + 1))
                                pe.wait_ge(S("qkr_ctx"), i * 2 + (w // 3 + 1))
                            scores(i * 6 + w, w // 3, w % 3, w % 2)
                            if w:
                                values(i * 6 + w - 1, i * 2 + (w - 1) // 3, (w - 1) % 3, (w - 1) % 2)
                        values(i * 6 + 5, i * 2 + 1, 2, 1)
                    for t in range(4):
                        pe.wait_ge(S("da_scaled"), t + 1)
                        for b in range(2):
                            if t >= 2:
                                pe.wait_ge(S("ol_ready"), 2 * (t - 2) + b + 1)
                            for hd in range(4):
                                mm = nc.tensor.transpose(ps[:, b + 2 * (t % 2), hd * P:hd * P + P],
                                                         qk[:, 0, 4 * b + hd, t * P:t * P + P], ident[:])
                            mm.then_inc(S("o_t"), 1)
                    pe.wait_ge(S("ol_ready"), 8)
                else:
                    def nvalues(v, tile, hh, q):
                        pe.wait_ge(S("ne_ready"), v + 3)
                        pe.wait_ge(S("npt_ready"), v + 1)
                        for c in range(4):
                            mm = nc.tensor.transpose(ps[:, 4 + q, c * P:c * P + P], e1[:, q, c * P:c * P + P], ident[:])
                        mm.then_inc(S("npt_psum"), 1)
                        pe.wait_ge(S("npt_ready"), v + 3)
                        pe.wait_ge(S("no_taken"), v + 1)
                        for c in range(4):
                            mm = nc.tensor.matmul(ps[:, 6 + q, 0:64], pt1[:, q, c, :],
                                                  v1[:, c, bass.ds(tile * P + hh * 64, 64)], start=c == 0, stop=c == 3)
                        mm.then_inc(S("npv_done"), 1)

                    with pe.Fori(0, KT // 2) as i:
                        for w in range(8):
                            hh, t, b, q = w // 2 % 2, w % 2, w // 4, w % 2
                            if w % 4 == 0:
                                pe.wait_ge(S("qks_ready"), i * 2 + (b + 1))
                            pe.wait_ge(S("ns_taken"), i * 8 + (w + 1))
                            rows = slice(64 * hh, 64 * hh + 64)
                            nc.tensor.matmul(ps[:, q, :], qks[rows, b, t * P:t * P + P], qks[rows, b, SEQ:],
                                             start=True, stop=True).then_inc(S("ns_ready"), 1)
                            if w:
                                nvalues(i * 8 + w - 1, i * 2 + (w - 1) // 4, (w - 1) // 2 % 2, (w - 1) % 2)
                        nvalues(i * 8 + 7, i * 2 + 1, 1, 1)
                    pe.wait_ge(S("no_taken"), 2 + 2 * NA_H)
                    for t in range(2):
                        for b in range(2):
                            for hd in range(4):
                                c = (4 * b + hd) * P
                                mm = nc.tensor.transpose(ps[:, b + 2 * t, hd * P:hd * P + P], o1[:, t, c:c + P], ident[:])
                            mm.then_inc(S("no_t"), 1)
                    pe.wait_ge(S("nol_ready"), 4)
                features(PH[f"wo{l}"], n)
                norm_sum(f"f{l}", n)
                pe.wait_ge(S("xl_ready"), XL_COUNT[f"f{l}"])
                features(PH[f"gu{l}"], n)
                pe.wait_ge(S("f_lo"), 2 + FT * (l + 2))
                features(PH[f"dn{l}"], n, fh[n], fl[n], FT)
            norm_sum("final", SEQ)

        @block.vector
        def _(dve):
            link = Link(dve, "dve_link")
            V = nc.vector

            for name, n in (("bank_free", 2), ("f_lo", 2), ("e_ready", 8), ("pt_ready", 2), ("o_taken", 2),
                            ("npt_ready", 2), ("no_taken", 2), ("ns_taken", 2)):
                dve.sem_inc(S(name), n)
            V.memset(cs[:].bitcast(mybir.dt.uint32), 0).then_inc(S("cs_zero"), 1)
            V.memset(up[:, :, 0:CONV_W - 1], 0.0)
            dve.wait_ge(S("cond_hi"), 1)
            V.tensor_tensor(cs[:, :, 2:4], csf[:], cs[:, :, 0:2].bitcast(F32), ALU.subtract).then_inc(S("cond_lo"), 1)
            dve.wait_ge(S("prm_in"), 16)
            for m in range(2):
                V.tensor_tensor(y[:, m, 0:64], par_ap("lam", 128 * m, 64), par_ap("lam", 128 * m + 64, 64), ALU.mult)\
                    .then_inc(S("lam_mul"), 1)
            dve.wait_ge(S("lam_mul"), 2)
            V.tensor_reduce(lam4[:, 0:2], y[:, 0:2, 0:64], AX_X, ALU.add).then_inc(S("lam_dot"), 1)

            ph = PH["ada"]
            with dve.Fori(0, ph.iters) as i:
                for j in range(2):
                    dve.wait_ge(S("mod_psum"), i * 2 + (j + 1))
                    pair_done(dve, ph, i, j)
                    V.tensor_copy(row[:, j, :], ps[0:4, j, 0:256]).then_inc(bank_free, 1)
            dve.wait_ge(S("mod_psum"), 2 + 48)
            link(V.tensor_tensor(mod[:].rearrange("p l t c -> p (l t) c"), ps[:, 7, 0:192].rearrange("p (t c) -> p t c", c=2),
                                 par_ap("ada_b").unsqueeze(2).to_broadcast([P, 96, 2]), ALU.add))
            for l in range(2):
                for w, name in enumerate(("n_mix", "n_ffn")):
                    V.scalar_tensor_tensor(gsc[:, l, w, :, :], mod[:, l, 8 + 24 * w:16 + 24 * w, :], 1.0,
                                           par_ap(name, l * KT, KT).unsqueeze(2).to_broadcast([P, KT, 2]),
                                           ALU.add, ALU.mult).then_inc(S("gsc_ready"), 1)
            dve.wait_ge(S("gsc_ready"), 4)
            dve.wait_ge(S("lam_exp"), 1)
            link(V.tensor_tensor(lam4[:, 4:5], lam4[:, 3:4], lam4[:, 2:3], ALU.subtract))
            link(V.tensor_scalar(lam4[:, 5:6], lam4[:, 4:5], -LAM_INIT, None, ALU.add))

            xl_count, xh_count, xr_count = [0], [0], [0]

            def recip(name, n):
                dve.wait_ge(S("root_ready"), NORMS.index(name) + 1)
                link(V.reciprocal(rstd[:, 0:n], rstd[:, 0:n]))

            def scale_in(src, n, gain):
                for k in range(KT):
                    V.tensor_tensor(y[:, k, 0:n], src[:, k, 0:n], rstd[:, 0:n], ALU.mult).then_inc(S("xr_ready"), 1)
                xr_count[0] += KT
                for k in range(KT):
                    xh_count[0] += 1
                    dve.wait_ge(S("xh_ready"), xh_count[0])
                    V.scalar_tensor_tensor(xl[:, k, 0:n], y[:, k, 0:n], gain[:, k:k + 1], xh[:, k, 0:n].bitcast(F32),
                                           ALU.mult, ALU.subtract).then_inc(S("xl_ready"), 1)

            def modulate(l, w, n):
                parts = [slice(c * SEQ, c * SEQ + SEQ) for c in range(n // SEQ)]
                for k in range(KT):
                    for c, t in enumerate(parts):
                        ins = V.scalar_tensor_tensor(y[:, k, t], h[:, k, t], gsc[:, l, w, k, c:c + 1], rstd[:, t],
                                                     ALU.mult, ALU.mult)
                    ins.then_inc(S("xr_ready"), 1)
                for k in range(KT):
                    for c, t in enumerate(parts):
                        xh_count[0] += 1
                        dve.wait_ge(S("xh_ready"), xh_count[0])
                        V.scalar_tensor_tensor(xl[:, k, t], y[:, k, t], mod[:, l, 24 * w + k, c:c + 1],
                                               xh[:, k, t].bitcast(F32), ALU.add, ALU.subtract).then_inc(S("xl_ready"), 1)

            def low_of(src, n):
                for k in range(KT):
                    xh_count[0] += 1
                    dve.wait_ge(S("xh_ready"), xh_count[0])
                    V.tensor_tensor(xl[:, k, 0:n], src[:, k, 0:n], xh[:, k, 0:n].bitcast(F32), ALU.subtract)\
                        .then_inc(S("xl_ready"), 1)

            def add_normed(src, gain):
                for k in range(KT):
                    V.scalar_tensor_tensor(src[:, k, 0:SEQ], src[:, k, 0:SEQ], gain[:, k:k + 1], rstd[:, 0:SEQ],
                                           ALU.mult, ALU.mult).then_inc(S("post_scaled"), 1)
                    post[0] += 1
                for k in range(KT):
                    dve.wait_ge(S("post_scaled"), post[0] - KT + k + 1)
                    V.tensor_tensor(h[:, k, 0:SEQ], h[:, k, 0:SEQ], src[:, k, 0:SEQ], ALU.add).then_inc(S("h_ready"), 1)

            post = [0]

            def take(ph, n, dst, falling=False):
                def body(i):
                    for j in range(2):
                        pair_done(dve, ph, i, j)
                        src, to = ps[:, 2 * j:2 * j + 2, 0:n], dst[:, bass.ds(i * 4 + 2 * j, 2), 0:n]
                        if falling:
                            src = src.rearrange("p a (r c) -> p a r c", c=64)[:, :, :, ::-1]
                            to = to.rearrange("p a (r c) -> p a r c", c=64)
                        V.tensor_scalar(to, src, 1.0, None, ALU.mult).then_inc(bank_free, 1)
                run(dve, ph, body)

            def take_tokens(ph, tiles, dst):
                def body(i):
                    for j in range(2):
                        pair_done(dve, ph, i, j)
                        V.tensor_scalar(dst[:, :, bass.ds(i * 512 + 256 * j, 256)],
                                        ps[:, 2 * j:2 * j + tiles // 2, :].rearrange("p a (b c) -> p (a b) c", b=2),
                                        1.0, None, ALU.mult).then_inc(bank_free, 1)
                run(dve, ph, body)

            def take_gated(ph, n, l, w):
                def body(i):
                    for j in range(2):
                        pair_done(dve, ph, i, j)
                        for o in range(2):
                            for c in range(n // SEQ):
                                t = slice(c * SEQ, c * SEQ + SEQ)
                                k = i * 4 + (2 * j + o)
                                g = mod[:, l, bass.ds(i * 4 + (2 * j + o + 16 + 24 * w), 1), c:c + 1].rearrange("p a b -> p (a b)")
                                hk = h[:, bass.ds(k, 1), t].rearrange("p a b -> p (a b)")
                                ins = V.scalar_tensor_tensor(hk, ps[:, 2 * j + o, t], g, hk, ALU.mult, ALU.add)
                        ins.then_inc(bank_free, 1)
                run(dve, ph, body)

            def gate_up(ph, n, f0):
                def body(i):
                    for j in range(2):
                        dve.wait_ge(S("f_lo"), i * 2 + (f0 + j + 1))
                        dve.wait_ge(S("silu_ready"), i * 2 + (f0 + j + 1))
                        V.tensor_tensor(ft[:, j, 0:n], sil[:, j, 0:n], ps[:, 2 * j + 1, 0:n], ALU.mult).then_inc(bank_free, 1)
                        dve.wait_ge(S("f_hi"), i * 2 + (f0 + j + 1))
                        f1 = bass.ds(i * 2 + j, 1)
                        V.tensor_tensor(fl[n][:, f1, :].rearrange("p a b -> p (a b)"), ft[:, j, 0:n],
                                        fh[n][:, f1, :].rearrange("p a b -> p (a b)").bitcast(F32),
                                        ALU.subtract).then_inc(S("f_lo"), 1)
                run(dve, ph, body)

            recip("pre1", SEQ)
            scale_in(h, SEQ, par_ap("mix_pre"))
            take(PH["in_f"], SEQ, u)
            take_tokens(PH["in_v"], 2, vb)
            dve.wait_ge(S("ret_swap"), 32)
            dve.wait_ge(S("ret_in"), 32)
            V.tensor_tensor(u[:, 8:16, :], u[:, 8:16, :], rcs[:, 0:1, :].to_broadcast([P, 8, SEQ]), ALU.mult)
            link(V.tensor_tensor(sw[:], sw[:], rcs[:, 1:2, :].to_broadcast([P, 8, SEQ]), ALU.mult))
            V.tensor_tensor(u[:, 8:16, :], u[:, 8:16, :], sw[:], ALU.add).then_inc(S("ret_roped"), 1)
            for hd in range(RET_H):
                dve.wait_ge(S("ret_sc"), hd + 1)
                V.tensor_tensor(st[:, hd, :], ps[:, hd % 2, 0:384], dt_[:, hd, :], ALU.mult).then_inc(S("ret_s"), 1)
            dve.wait_ge(S("ret_sq"), 1)
            V.tensor_reduce(ssq[:], on[:].rearrange("p a b c -> p (a b) c"), AX_X, ALU.add).then_inc(S("ret_ssq"), 1)
            dve.wait_ge(S("ret_root"), 1)
            link(V.reciprocal(ssq[:], ssq[:]))
            V.tensor_tensor(on[:].rearrange("p a b c -> p (a b) c"),
                            ps[:, 2:4, :].rearrange("p a (b c) -> p (a b) c", c=P),
                            ssq[:].unsqueeze(2).to_broadcast([P, 8, P]), ALU.mult).then_inc(S("ret_on"), 1)
            dve.wait_ge(S("sig_ready"), 1)
            link(V.tensor_tensor(up[:, :, CONV_W - 1:], u[:, 0:4, :], u[:, 4:8, :], ALU.mult))
            for c in range(CONV_T):
                V.tensor_scalar(cy[:, c, :], up[:, c, 0:SEQ], par_ap("conv_w", c * CONV_W, 1), par_ap("conv_b", c, 1),
                                ALU.mult, ALU.add).then_inc(S("conv_tap"), 1)
            cw0 = PAT["conv_w"][0]
            with dve.Fori(1, CONV_W) as i:
                for c in range(CONV_T):
                    dve.wait_ge(S("conv_tap"), i * CONV_T + (c - CONV_T + 1))
                    V.scalar_tensor_tensor(cy[:, c, :], up[:, c, bass.ds(i, SEQ)], prm[:, bass.ds(i + (cw0 + c * CONV_W), 1)],
                                           cy[:, c, :], ALU.mult, ALU.add).then_inc(S("conv_tap"), 1)
            dve.wait_ge(S("conv_tap"), CONV_T * CONV_W)
            dve.wait_ge(S("ret_t"), 1)
            dve.wait_ge(S("gate_ready"), 1)
            V.tensor_tensor(mix[:, 4:8, :], ps[:, 0:2, :].rearrange("p a (b c) -> p (a b) c", b=2), u[:, 16:20, :], ALU.mult)\
                .then_inc(S("mix_ret"), KT)
            dve.wait_ge(S("ln_sum"), 1)
            for c in range(CONV_T):
                ins = V.scalar_tensor_tensor(cy[:, c, :], ps[:, 4, 0:SEQ], -1.0 / 512, cy[:, c, :], ALU.mult, ALU.add)
            ins.then_inc(S("dev_ready"), 1)
            dve.wait_ge(S("dev_ready"), 1)
            dve.wait_ge(S("ln_root"), 1)
            link(V.reciprocal(rstd[:, 0:SEQ], rstd[:, 0:SEQ]))
            V.tensor_tensor(cy[:], cy[:], rstd[:, 0:SEQ].unsqueeze(1).to_broadcast([P, CONV_T, SEQ]), ALU.mult)\
                .then_inc(S("ln_scaled"), 1)
            low_of(mix, SEQ)
            take(PH["out"], SEQ, y)
            recip("post1", SEQ)
            add_normed(y, par_ap("mix_post"))
            recip("fpre1", SEQ)
            scale_in(h, SEQ, par_ap("ffn_pre"))
            gate_up(PH["gu"], SEQ, 0)
            take(PH["dn"], SEQ, y)
            recip("fpost1", SEQ)
            add_normed(y, par_ap("ffn_post"))
            dve.wait_ge(S("p_hi"), 1)
            V.tensor_tensor(ptl[:], ptf[:], pth[:].bitcast(F32), ALU.subtract).then_inc(S("p_lo"), 1)
            low_of(h, SEQ)
            ph = PH["pp"]
            for pair in range(4):
                if pair < 3:
                    dve.wait_ge(S("pp_ready"), pair + 1)
                else:
                    dve.wait_ge(units_done, 2 * ph.step0 + 2 + SLOTS)
                b = 2 * (pair % 2)
                V.tensor_copy(ppo[:, 2 * pair:2 * pair + 2, :], ps[:, b:b + 2, 0:SEQ]).then_inc(bank_free, 1)

            def gated_e(i):
                ph = PH["pg"]
                for j in range(2):
                    dve.wait_ge(S("sigm_ready"), i * 2 + (j + 1))
                    pp2 = ppo[:, bass.ds(i * 4 + 2 * j, 2), :]
                    V.tensor_tensor(pp2, pp2, sil[:, j, :].rearrange("p (a b) -> p a b", a=2), ALU.mult).then_inc(bank_free, 1)
            run(dve, PH["pg"], gated_e)
            recip("ple1", SEQ)
            add_normed(ppo, par_ap("ple_post"))

            for l in range(2):
                n = NT if l == 0 else SEQ
                recip(f"m{l}", NT)
                modulate(l, 0, NT)
                if l == 0:
                    take(PH["q0"], NT, qk[:, 0, :, :])
                    take(PH["k0"], NT, qk[:, 1, :, :])
                    take_tokens(PH["v0"], 4, vv)
                    dve.wait_ge(S("rope_in"), 16)
                    dve.wait_ge(S("swap_in"), 8 * 16)

                    def roped(i, hh):
                        dve.wait_ge(S("s_ready"), i * 6 + (3 * hh + 3))
                        hd = bass.ds(i * 2 + hh, 1)
                        V.tensor_tensor(qkr[:, hh, :, 0:SEQ], qk[:, :, hd, 0:SEQ].rearrange("p m a b -> p m (a b)"),
                                        rope[:, 0:1, :].to_broadcast([P, 2, SEQ]), ALU.mult)
                        link(V.tensor_tensor(rtmp[:, hh, :, :], sww[:, :, hd, :].rearrange("p m a b -> p m (a b)"),
                                             rope[:, 1:2, :].to_broadcast([P, 2, SEQ]), ALU.mult))
                        V.tensor_tensor(qkr[:, hh, :, 0:SEQ], qkr[:, hh, :, 0:SEQ], rtmp[:, hh, :, :], ALU.add)\
                            .then_inc(S("qkr_ready"), 1)

                    def maxima(v, q, k3):
                        dve.wait_ge(S("s_ready"), v + 7)
                        src = ps[:, 2 * q:2 * q + 2, :]
                        if k3 < 2:
                            mx = sm[:, q, 12:14]
                            link(V.tensor_reduce(mx, src, AX_X, ALU.max))
                            V.tensor_scalar(sm[:, q, 0:2], mx, -0.125, None, ALU.mult).then_inc(S("s_max"), 1)
                        else:
                            mx = sm[:, q, 12:16]
                            link(V.tensor_reduce(mx.rearrange("p (t m) -> p m t", m=2),
                                                 src.rearrange("p m (t c) -> p m t c", t=2), AX_X, ALU.max))
                            V.tensor_scalar(sm[:, q, 0:4], mx, -0.125, None, ALU.mult).then_inc(S("s_max"), 1)

                    def combine(v, q, k3):
                        dve.wait_ge(S("e_ready"), v * 4 + 12)
                        tiles = 1 if k3 < 2 else 2
                        link(V.reciprocal(sm[:, q, 8:8 + 2 * tiles], sm[:, q, 4:4 + 2 * tiles]))
                        odd = sm[:, q, 8:8 + 2 * tiles].rearrange("p (t m) -> p t m", m=2)[:, :, 1]
                        link(V.tensor_scalar(odd, odd, lam4[:, 5:6], None, ALU.mult))
                        for t in range(tiles):
                            c = slice(0, 512) if k3 < 2 else slice(t * 256, t * 256 + 256)
                            ins = V.tensor_scalar(e2[:, q, 1, c], e2[:, q, 1, c], sm[:, q, 9 + 2 * t:10 + 2 * t], None, ALU.mult)
                        link(ins)
                        for t in range(tiles):
                            c = slice(0, 512) if k3 < 2 else slice(t * 256, t * 256 + 256)
                            ins = V.scalar_tensor_tensor(e2[:, q, 0, c], e2[:, q, 0, c], sm[:, q, 8 + 2 * t:9 + 2 * t],
                                                         e2[:, q, 1, c], ALU.mult, ALU.add)
                        ins.then_inc(S("p_ready"), 1)

                    def take_o(v, head, q, k3):
                        dve.wait_ge(S("pv_done"), v + 3)
                        t0, w = (k3, P) if k3 < 2 else (2, 2 * P)
                        V.tensor_scalar(qk[:, 0, bass.ds(head, 1), t0 * P:t0 * P + w].rearrange("p a b -> p (a b)"),
                                        ps[:, 6 + q, 0:w], 1.0, None, ALU.mult).then_inc(S("o_taken"), 1)

                    per = 2 + 6 * 4
                    with dve.Fori(0, DA_H // 2) as i:
                        link.begin(i, per)
                        for w in range(6):
                            if w == 0:
                                roped(i, 0)
                                roped(i, 1)
                            maxima(i * 6 + w, w % 2, w % 3)
                            if w:
                                combine(i * 6 + w - 1, (w - 1) % 2, (w - 1) % 3)
                            if w >= 2:
                                take_o(i * 6 + w - 2, i * 2 + (w - 2) // 3, w % 2, (w - 2) % 3)
                        combine(i * 6 + 5, 1, 2)
                        take_o(i * 6 + 4, i * 2 + 1, 0, 1)
                        take_o(i * 6 + 5, i * 2 + 1, 1, 2)
                    link.end(DA_H // 2)
                    for t in range(4):
                        dve.wait_ge(S("da_sq"), t + 1)
                        ins = V.tensor_reduce(ort[:, t, :], osq[:, t, :, :], AX_X, ALU.add)
                    ins.then_inc(S("da_ssq"), 1)
                    dve.wait_ge(S("da_root"), 1)
                    link(V.reciprocal(ort[:], ort[:]))
                    link(V.tensor_scalar(ort[:], ort[:], 1.0 - LAM_INIT, None, ALU.mult))
                    for t in range(4):
                        o_ = qk[:, 0, :, t * P:t * P + P]
                        V.tensor_tensor(o_, o_, ort[:, t, :].unsqueeze(2).to_broadcast([P, DA_H, P]), ALU.mult)\
                            .then_inc(S("da_scaled"), 1)
                    for t in range(4):
                        for b in range(2):
                            dve.wait_ge(S("oh_ready"), 2 * t + b + 1)
                            x_ = (slice(None), slice(4 * b, 4 * b + 4), slice(t * P, t * P + P))
                            V.scalar_tensor_tensor(xl[x_], ps[:, b + 2 * (t % 2), :].rearrange("p (a b) -> p a b", a=4),
                                                   par_ap("subln"), xh[x_].bitcast(F32), ALU.mult, ALU.subtract)\
                                .then_inc(S("ol_ready"), 1)
                else:
                    take(PH["q1"], SEQ, q1, falling=True)
                    take(PH["k1"], NT, k1)
                    dve.wait_ge(S("bias_in"), 16 * 16)
                    dve.wait_ge(S("mask_in"), 16)
                    for t in range(2):
                        V.tensor_tensor(bias[:, t, :, :], bias[:, t, :, :], mask[:].unsqueeze(1).to_broadcast([P, NA_H, SEQ]),
                                        ALU.add).then_inc(S("masked"), 1)
                    take_tokens(PH["v1"], 4, v1)
                    dve.wait_ge(S("masked"), 2)

                    def nscale(i, w):
                        q, t, r4 = w % 2, w % 2, w % 4
                        dve.wait_ge(S("ne_ready"), i * 8 + (w + 1))
                        dve.wait_ge(S("ns_ready"), i * 8 + (w + 9))
                        head = bass.ds(i * 4 + w // 2, 1)
                        V.scalar_tensor_tensor(s1[:, q, 0:SEQ], ps[:, q, 0:SEQ], 0.125,
                                               bias[:, t, head, :].rearrange("p a b -> p (a b)"), ALU.mult, ALU.add)
                        V.tensor_scalar(s1[:, q, SEQ:], ps[:, q, SEQ:], 0.125, None, ALU.mult).then_inc(S("ns_taken"), 1)
                        dve.wait_ge(S("ns_taken"), i * 8 + (w + 3))
                        link(V.tensor_reduce(sm1[:, r4, 0:1], s1[:, q, :], AX_X, ALU.max))
                        V.tensor_scalar(sm1[:, r4, 1:2], sm1[:, r4, 0:1], -1.0, None, ALU.mult).then_inc(S("ns_max"), 1)

                    def ntake(i, w):
                        q, t, r4 = w % 2, w % 2, w % 4
                        dve.wait_ge(S("npv_done"), i * 8 + (w + 3))
                        link(V.reciprocal(sm1[:, r4, 3:4], sm1[:, r4, 2:3]))
                        V.tensor_scalar(o1[:, t, bass.ds(i * 256 + (w // 2) * 64, 64)], ps[:, 6 + q, 0:64], sm1[:, r4, 3:4], None,
                                        ALU.mult).then_inc(S("no_taken"), 1)

                    with dve.Fori(0, KT // 2) as i:
                        link.begin(i, 16)
                        for w in range(8):
                            nscale(i, w)
                            if w >= 2:
                                ntake(i, w - 2)
                        ntake(i, 6)
                        ntake(i, 7)
                    link.end(KT // 2)
                    for t in range(2):
                        for b in range(2):
                            dve.wait_ge(S("oh_ready"), 8 + 2 * t + b + 1)
                            x_ = (slice(None), slice(4 * b, 4 * b + 4), slice(t * P, t * P + P))
                            V.tensor_tensor(xl[x_].rearrange("p a (r c) -> p a r c", c=64),
                                            ps[:, b + 2 * t, :].rearrange("p (a r c) -> p a r c", a=4, c=64)[:, :, :, ::-1],
                                            xh[x_].bitcast(F32).rearrange("p a (r c) -> p a r c", c=64), ALU.subtract).then_inc(S("nol_ready"), 1)
                take_gated(PH[f"wo{l}"], n, l, 0)
                recip(f"f{l}", n)
                modulate(l, 1, n)
                gate_up(PH[f"gu{l}"], n, FT * (l + 1))
                take_gated(PH[f"dn{l}"], n, l, 1)
            recip("final", SEQ)
            for k in range(KT):
                V.scalar_tensor_tensor(y[:, k, 0:SEQ], h[:, k, 0:SEQ], par_ap("final", k, 1), rstd[:, 0:SEQ], ALU.mult, ALU.mult)\
                    .then_inc(S("final_ready"), 1)


def tiles_of(w):
    k, n = w.shape
    w = w.reshape(k // 1024, 2, HALF, P, n // 256, 256)
    return np.ascontiguousarray(w.transpose(4, 0, 1, 3, 2, 5)).reshape(-1, P, HALF, 256)


def feature_tiles(v):
    return np.ascontiguousarray(v.T.reshape(-1, P, v.shape[0]).transpose(1, 0, 2))


def gate_up_tiles(g, u):
    both = np.stack([g.reshape(D, FT, P), u.reshape(D, FT, P)], axis=2)
    return tiles_of(both.reshape(D, 2 * FF))


def down_tiles(w):
    padded = np.zeros((3 * 1024, D), w.dtype)
    padded[:FF] = w
    return tiles_of(padded)


def shape_tables():
    f = np.float32
    tab = np.zeros((P, P + 2), f)
    tab[:, :P] = np.eye(P, dtype=f)
    for r_ in range(4):
        tab[r_, P + r_ % 2] = 1
    log_g = np.log(1.0 - 2.0 ** (-5.0 - np.arange(RET_H)))
    i = np.arange(SEQ)
    ret = np.zeros((P, RET_H * 384 + 2 * SEQ), f)
    for hd in range(RET_H):
        d = i[None, :] - i[:, None]
        full = np.where(d >= 0, np.exp(log_g[hd] * np.maximum(d, 0)), 0) * P ** -0.5
        ret[:, hd * 384:hd * 384 + 256] = full[0:P, :]
        ret[:, hd * 384 + 256:hd * 384 + 384] = full[P:, P:]
    freqs = f(10000.0) ** (-np.arange(64, dtype=f) / f(64))
    ang = np.arange(SEQ, dtype=f)[None, :] * np.concatenate([freqs, freqs])[:, None]
    ret[:, RET_H * 384:RET_H * 384 + SEQ] = np.cos(ang)
    ret[:, RET_H * 384 + SEQ:] = np.sin(ang) * np.where(np.arange(P) < 64, -1, 1)[:, None]
    fr = f(1.0) / (f(10000.0) ** (np.arange(0, 32, 2, dtype=f) / f(32)))
    pr, pc = (i // 64).astype(f), (i % 64).astype(f)
    ar, ac = fr[:, None] * pr[None, :], fr[:, None] * pc[None, :]
    half = np.concatenate([ar, ac, ar, ac])
    sign = np.where(np.arange(64) < 32, -1, 1)[:, None]
    rope_ = np.zeros((P, 2, SEQ), f)
    rope_[:, 0] = np.tile(np.cos(half), (2, 1))
    rope_[:, 1] = np.tile(np.sin(half) * sign, (2, 1))
    c = np.arange(64)
    start = np.clip(c - 8, 0, 48)
    inside = (c[None, :] >= start[:, None]) & (c[None, :] < start[:, None] + 16)
    mask_ = np.tile(np.where(inside, 0.0, NEG)[::-1], (2, 4)).astype(f)
    return tab, ret, rope_, mask_


def axial_order():
    one = np.concatenate([np.arange(0, 16), np.arange(32, 48), np.arange(16, 32), np.arange(48, 64)])
    return (np.arange(0, D, 64)[:, None] + one[None, :]).ravel()


def kernel(**inputs):
    import concourse.bacc as _bacc
    from concourse.bass_utils import run_bass_kernel_spmd as _run

    g = {k: np.asarray(v) for k, v in inputs.items()}
    w_in = g["w_in"][0]
    c = [w_in[:, 512 * k:512 * k + 512] for k in range(6)]
    w_in = np.concatenate([c[0], c[1], c[2], c[3], c[5], c[4]], axis=1)
    parts = [tiles_of(g["ada_w_2"][0]), tiles_of(g["ada_w_2"][1]), tiles_of(w_in), tiles_of(g["w_out"][0]),
             gate_up_tiles(g["w_ffn_gate"][0], g["w_ffn_up"][0]), down_tiles(g["w_ffn_down"][0]),
             g["w_ple_proj"][0].reshape(2, P, HALF, 256), tiles_of(g["w_ple_gate"][0])]
    for l in range(2):
        qkv = g["da_wqkv_2" if l == 0 else "na_wqkv_2"][0]
        q, k, v = qkv[:, :D], qkv[:, D:2 * D], qkv[:, 2 * D:]
        if l == 0:
            q, k = q[:, axial_order()], k[:, axial_order()]
        parts += [tiles_of(q), tiles_of(k), tiles_of(v), tiles_of(g["da_wo_2" if l == 0 else "na_wo_2"][0])]
        gu = g["ffn_w_gate_up_2"][l]
        parts += [gate_up_tiles(gu[:, :FF], gu[:, FF:]), down_tiles(g["ffn_w_down_2"][l])]
    wall = np.concatenate(parts)
    col = lambda v: v.reshape(-1, P).T
    cond = np.stack([col(g["c_2"][0]), col(g["c_ctx_2"])], axis=2).reshape(P, 2 * KT)
    conv_w = g["conv_dw_w"][0].T.reshape(CONV_T, P, CONV_W).transpose(1, 0, 2).reshape(P, -1)
    lam = np.concatenate([g["da_lambda_q1_2"][0], g["da_lambda_k1_2"][0], g["da_lambda_q2_2"][0], g["da_lambda_k2_2"][0]])
    vals = {"mix_pre": col(g["mix_pre_norm"][0]), "mix_post": col(g["mix_post_norm"][0]),
            "ffn_pre": col(g["ffn_pre_norm"][0]), "ffn_post": col(g["ffn_post_norm"][0]),
            "ple_post": col(g["ple_post_norm"][0]), "final": col(g["norm_final_2"]),
            "n_mix": col(g["norm_mix_2"].reshape(-1)), "n_ffn": col(g["norm_ffn_2"].reshape(-1)),
            "ada_b": col(g["ada_b_2"].reshape(-1)), "conv_w": conv_w, "conv_b": col(g["conv_dw_b"][0]),
            "ln_w": col(g["conv_ln_w"][0]), "ln_b": col(g["conv_ln_b"][0]), "cond": cond,
            "subln": g["da_subln_2"][0].reshape(P, 1), "lam": np.broadcast_to(lam, (P, 256))}
    par = np.concatenate([vals[name] for name, _ in PCOLS], axis=1)
    tab, ret, rope_, mask_ = shape_tables()
    xin = feature_tiles(np.concatenate([g["x"][0], g["ctx_2"][0]], axis=0))
    arrays = {"wall": wall, "xin": xin, "pin": feature_tiles(g["p"][0, 0]), "par": par, "tab": tab, "tab_ret": ret,
              "tab_rope": rope_, "tab_mask": mask_, "rpb": g["na_rpb_2"][0]}
    nc = _bacc.Bacc("TRN2", target_bir_lowering=False, num_devices=1)
    args = []
    for name in arrays:
        a = arrays[name] = np.ascontiguousarray(arrays[name])
        args.append(nc.dram_tensor(name, a.shape, mybir.dt.from_np(a.dtype), kind="ExternalInput").ap())
    args.append(nc.dram_tensor("out_0", (P, KT, SEQ), F32, kind="ExternalOutput").ap())
    build(nc, *args)
    r = _run(nc, [arrays], core_ids=[0])
    got = r.results[0]["out_0"]
    return np.ascontiguousarray(got.transpose(2, 1, 0).reshape(1, SEQ, D))
```

```python
from contextlib import ExitStack

import numpy as np

import concourse.bass as bass
from concourse import mybir

F32 = mybir.dt.float32
F32R = mybir.dt.float32r
BF16 = mybir.dt.bfloat16
ALU = mybir.AluOpType
ACT = mybir.ActivationFunctionType
AX_X = mybir.AxisListType.X

P = 128
D = 1024
KT = D // P
SEQ = 256
NT = 2 * SEQ
FF = 2816
FT = FF // P
EPS = 1e-6
HALF = 4
UNIT = HALF * 256
SLOTS = 4
CONV_W = 31
CONV_T = 4
RET_H = 4
DA_H = 8
NA_H = 16
LAM_INIT = 0.2
NEG = -1.0e37

PHASES = [("in_f", 10), ("in_v", 2), ("out", 4), ("gu", 22), ("dn", 12), ("pp", 1), ("pg", 4)]
for _l in range(2):
    PHASES += [(f"q{_l}", 4), (f"k{_l}", 4), (f"v{_l}", 4), (f"wo{_l}", 4), (f"gu{_l}", 22), (f"dn{_l}", 12)]


class Phase:

    def __init__(self, name, step0, steps, pair0):
        self.name, self.step0, self.steps, self.pair0 = name, step0, steps, pair0
        self.per_pair = 3 if name.startswith("dn") else 1
        self.body = 1 if name == "pp" else 2 * self.per_pair
        self.iters = steps // self.body
        self.pairs = 4 if name == "pp" else steps // self.per_pair


def plan():
    out, step, pair = {}, 0, 0
    for name, steps in PHASES:
        out[name] = ph = Phase(name, step, steps, pair)
        step += steps
        pair += ph.pairs
    return out, step


PH, STEPS = plan()
UNITS = 2 * STEPS
XL_COUNT = {"m0": 6 * KT, "f0": 8 * KT, "m1": 10 * KT, "f1": 11 * KT}
NORMS = ["pre1", "post1", "fpre1", "fpost1", "ple1", "m0", "f0", "m1", "f1", "final"]

PCOLS = [("mix_pre", KT), ("mix_post", KT), ("ffn_pre", KT), ("ffn_post", KT), ("ple_post", KT), ("final", KT),
         ("n_mix", 2 * KT), ("n_ffn", 2 * KT), ("ada_b", 96), ("conv_w", CONV_T * CONV_W), ("conv_b", CONV_T),
         ("ln_w", CONV_T), ("ln_b", CONV_T), ("subln", 1), ("lam", 256)]
PAT = {}
_at = 0
for _n, _w in PCOLS:
    PAT[_n] = (_at, _w)
    _at += _w
NPAR = _at
ADA_UNITS = 6 * D // P
ADA_SLOTS = 4
ADA_WOVEN = {}
_at = 0
for _n, _per, _slots in (("in_f", 1, 2), ("gu", 1, 2), ("dn", 4, 4), ("q0", 4, 4), ("k0", 4, 4), ("v0", 4, 4)):
    ADA_WOVEN[_n] = (_per, _slots, _at)
    _at += _per * PH[_n].pairs
assert _at == 2 * ADA_UNITS and ADA_WOVEN["q0"][2] == ADA_UNITS


def slot_tenants(name, s):
    n = 0
    for other, (per, slots, _) in ADA_WOVEN.items():
        if other == name:
            return n
        n += per * PH[other].pairs // slots if s < slots else 0


def build(nc, wall, wada, cond, xin, pin, par, tab, tab_ret, tab_rope, tab_mask, rpb, out):
    with ExitStack() as ctx:
        sems = {}

        def S(name):
            if name not in sems:
                sems[name] = ctx.enter_context(nc.semaphore(name))
            return sems[name]

        base = nc.sbuf_base
        base = (base + 31) // 32 * 32
        limit = nc.sbuf_usable_end
        arena_bytes = (limit - base) // 32 * 32
        ctx.enter_context(nc.sbuf_tensor("arena", [P, arena_bytes // 4], F32))
        cursor = [base]

        def at(name, shape, offset, dt=F32):
            size = 4 * int(np.prod(shape[1:]))
            assert offset + size <= base + arena_bytes, (name, offset + size - base - arena_bytes)
            return nc.alloc_sbuf_tensor_at(name, shape, dt, offset=offset)

        def sb(name, shape, dt=F32):
            o = cursor[0]
            cursor[0] = (o + 4 * int(np.prod(shape[1:])) + 31) // 32 * 32
            return at(name, shape, o, dt)

        class Region:

            def __init__(self, offset, size):
                self.o, self.end = offset, offset + size

            def take(self, name, shape, dt=F32):
                o = self.o
                self.o = (o + 4 * int(np.prod(shape[1:])) + 31) // 32 * 32
                assert self.o <= self.end, (name, self.o - self.end)
                return at(name, shape, o, dt)

        h = sb("h", [P, KT, NT])
        xs_at = cursor[0]
        xh = sb("xh", [P, KT, NT], F32R)
        xl = sb("xl", [P, KT, NT], F32R)
        y = sb("y", [P, KT, NT])
        y_at = cursor[0] - 4 * KT * NT
        raw = sb("raw", [P, SLOTS, HALF, 256])
        wh = sb("wh", [P, SLOTS, HALF, 256], F32R)
        wl = sb("wl", [P, SLOTS, HALF, 256], F32R)
        rstd = sb("rstd", [P, NT])
        prm = sb("prm", [P, NPAR])
        ones = sb("ones", [P, P])
        ident = sb("ident", [P, P])
        mod = sb("mod", [P, 2, 48, 2])
        gsc = sb("gsc", [P, 2, 2, KT, 2])
        lam4 = sb("lam4", [P, 8])
        eps = sb("eps", [P, 1])
        idle = sb("idle", [P, 1])
        big_at = cursor[0]
        BIG = 4 * FT * NT * 2
        assert big_at + BIG <= base + arena_bytes, big_at + BIG - base - arena_bytes

        sq = at("sq", [P, KT, NT], xs_at)
        fh = {SEQ: at("fh1", [P, FT, SEQ], big_at, F32R), NT: at("fh2", [P, FT, NT], big_at, F32R)}
        fl = {SEQ: at("fl1", [P, FT, SEQ], big_at + 4 * FT * SEQ, F32R),
              NT: at("fl2", [P, FT, NT], big_at + 4 * FT * NT, F32R)}
        sil = at("sil", [P, 2, NT], y_at)
        ft = at("ft", [P, 2, NT], y_at + 8 * NT)

        r = Region(big_at, BIG)
        u = r.take("u", [P, 20, SEQ])
        vb = r.take("vb", [P, 2, 512])
        up = r.take("up", [P, CONV_T, CONV_W - 1 + SEQ])
        cy = r.take("cy", [P, CONV_T, SEQ])
        sw = r.take("sw", [P, 8, SEQ])
        st = r.take("st", [P, RET_H, 384])
        on = r.take("on", [P, 2, RET_H, P])
        dt_ = r.take("dt_", [P, RET_H, 384])
        rcs = r.take("rcs", [P, 2, SEQ])
        ssq = r.take("ssq", [P, 8])
        csb = at("csb", [P, 2, D], big_at + BIG - 4 * D * (ADA_SLOTS + 2))
        ada = at("ada", [P, ADA_SLOTS, D], big_at + BIG - 4 * D * ADA_SLOTS)
        unread = nc.alloc_sbuf_tensor_at("unread", [P, 2, D], BF16, offset=big_at + BIG - 4 * D * (ADA_SLOTS + 3))
        assert r.o <= big_at + BIG - 4 * D * (ADA_SLOTS + 3)
        mix = at("mix", [P, KT, SEQ], y_at)
        r = Region(big_at, BIG)
        ptf = r.take("ptf", [P, 2, SEQ])
        pth = r.take("pth", [P, 2, SEQ], F32R)
        ptl = r.take("ptl", [P, 2, SEQ], F32R)
        ppo = r.take("ppo", [P, KT, SEQ])
        r = Region(big_at, BIG)
        qk = r.take("qk", [P, 2, KT, NT])
        vv = r.take("vv", [P, 4, D])
        rope = r.take("rope", [P, 2, SEQ])
        e2 = r.take("e2", [P, 2, 2, 512])
        pt = r.take("pt", [P, 2, 4, P])
        rtmp = r.take("rtmp", [P, 2, 2, SEQ])
        qkr = r.take("qkr", [P, 2, 2, NT])
        sm = r.take("sm", [P, 6, 16])
        ort = r.take("ort", [P, 4, DA_H])
        sww = at("sww", [P, 2, KT, SEQ], y_at)
        osq = at("osq", [P, 4, DA_H, P], y_at)
        r = Region(big_at, BIG)
        q1 = r.take("q1", [P, KT, SEQ])
        k1 = r.take("k1", [P, KT, NT])
        v1 = r.take("v1", [P, 4, D])
        bias = r.take("bias", [P, 2, NA_H, SEQ])
        e1 = r.take("e1", [P, 2, 512])
        pt1 = r.take("pt1", [P, 2, 4, P])
        sm1 = r.take("sm1", [P, 8, 8])
        qks = r.take("qks", [P, 2, SEQ + NT])
        o1 = at("o1", [P, 2, D], y_at)
        s1 = at("s1", [P, 2, 512], y_at + 8 * D)
        mask = at("mask", [P, SEQ], y_at + 12 * D)

        ps = ctx.enter_context(nc.psum_tensor("ps", [P, 8, 512], F32))

        def par_ap(name, a=0, n=None):
            o, w = PAT[name]
            n = w - a if n is None else n
            return prm[:, o + a:o + a + n]

        landed = [S(f"landed{k}") for k in range(SLOTS)]
        hi_ready, lo_ready = S("hi_ready"), S("lo_ready")
        units_done = S("units_done")
        ada_landed = [S(f"ada_landed{k}") for k in range(ADA_SLOTS)]
        ada_used = S("ada_used")
        bank_free = S("bank_free")

        def par_ap(name, a=0, n=None):
            o, w = PAT[name]
            n = w - a if n is None else n
            return prm[:, o + a:o + a + n]

        def run(eng, ph, body, peel=0):
            if ph.iters - peel > 1:
                with eng.Fori(0, ph.iters - peel) as i:
                    body(i)
            elif ph.iters - peel == 1:
                body(0)
            for i in range(ph.iters - peel, ph.iters):
                body(i)

        def pair_done(eng, ph, i, pair):
            eng.wait_ge(units_done, i * (2 * ph.body) + (2 * ph.step0 + 2 * ph.per_pair * (pair + 1) + SLOTS))

        def steps(eng, iters, per, depth, step):
            for w in range(per):
                step(0, w)
            with eng.Fori(1, iters) as i:
                for w in range(per):
                    step(i, w)
            for w in range(depth):
                step(iters, w)

        def live(i, w, iters, per):
            return not isinstance(i, int) or 0 <= i * per + w < iters * per

        def settled(eng):
            eng.wait_ge(S("x_in"), 16)

        class Link:

            def __init__(self, eng, name):
                self.eng, self.sem, self.n, self.off = eng, S(name), 0, 0

            def __call__(self, ins):
                self.n += 1
                ins.then_inc(self.sem, 1)
                self.eng.wait_ge(self.sem, self.off + self.n)

            def steps(self, iters, per, depth, links, step):

                def counted(i, w):
                    if not isinstance(i, int):
                        if w == 0:
                            self.n0, self.n = self.n, 0
                        self.off = i * links + (self.n0 - links)
                    step(i, w)
                    if not isinstance(i, int) and w == per - 1:
                        assert self.n == links, (self.n, links)
                        self.n, self.off = self.n0 + links * (iters - 1), 0

                steps(self.eng, iters, per, depth, counted)

        block = ctx.enter_context(nc.Block())

        @block.sync
        def _(sp):
            def load(u_, slot):
                sp.wait_ge(lo_ready, u_ + 1)
                sp.dma_start(raw[:, slot, :, :], wall[u_, :, :, :]).then_inc(landed[slot], 16)

            def load_ada(name, i, s):
                per, slots, a0 = ADA_WOVEN[name]
                n = 2 * per
                sp.wait_ge(ada_used, a0 + ADA_SLOTS)
                sp.wait_ge(ada_used, i * n + (a0 + s + 1 + ADA_SLOTS - slots))
                sp.dma_start(ada[:, s % slots, :], wada[i * n + (a0 + s), :, :]).then_inc(ada_landed[s % slots], 16)

            def stream(u0, u1, name=None):
                n = SLOTS if name is None else 4 * PH[name].per_pair
                a = 0 if name is None else 2 * ADA_WOVEN[name][0]
                with sp.Fori(0, (u1 - u0) // n) as i:
                    for s in range(n):
                        load(i * n + (u0 + s), (u0 + s) % SLOTS)
                        for s_ in range(s * a // n, (s + 1) * a // n):
                            load_ada(name, i, s_)
                for u_ in range(u0 + (u1 - u0) // n * n, u1):
                    load(u_, u_ % SLOTS)

            sp.dma_start(h[:], xin).then_inc(S("x_in"), 16)
            sp.dma_start(prm[:], par).then_inc(S("prm_in"), 16)
            sp.dma_start(csb[:], bass.AP(cond.tensor, 0, [[0, P], [D, 2], [1, D]])).then_inc(S("cond_in"), 16)
            sp.dma_start(ident[:], tab).then_inc(S("tab_in"), 16)
            sp.dma_start(dt_[:], tab_ret[:, 0:RET_H * 384].rearrange("p (a b) -> p a b", a=RET_H))\
                .then_inc(S("ret_in"), 16)
            sp.dma_start(rcs[:], tab_ret[:, RET_H * 384:].rearrange("p (a b) -> p a b", a=2))\
                .then_inc(S("ret_in"), 16)
            at_ = 0
            for name in ADA_WOVEN:
                if at_ < 2 * PH[name].step0:
                    stream(at_, 2 * PH[name].step0)
                at_ = 2 * (PH[name].step0 + PH[name].steps)
                stream(2 * PH[name].step0, at_, name)
            stream(at_, UNITS)
            sp.wait_ge(S("final_ready"), KT)
            sp.dma_start(out, y[:, :, 0:SEQ]).then_inc(S("stored"), 16)
            sp.wait_ge(S("stored"), 16)

        @block.gpsimd
        def _(pool):
            def low(u_, slot):
                pool.wait_ge(hi_ready, u_ + 1)
                nc.gpsimd.tensor_tensor(wl[:, slot, :, :], raw[:, slot, :, :], wh[:, slot, :, :].bitcast(F32),
                                        ALU.subtract).then_inc(lo_ready, 1)

            pool.sem_inc(lo_ready, SLOTS)
            nc.gpsimd.memset(eps[:], EPS).then_inc(S("consts"), 1)
            nc.gpsimd.memset(ones[:], 1.0).then_inc(S("consts"), 1)

            def lows(u0, u1):
                with pool.Fori(0, (u1 - u0) // SLOTS) as i:
                    for s in range(SLOTS):
                        low(i * SLOTS + (u0 + s), (u0 + s) % SLOTS)
                for u_ in range(u0 + (u1 - u0) // SLOTS * SLOTS, u1):
                    low(u_, u_ % SLOTS)

            ends = [2 * PH[f"wo{l}"].step0 + 2 for l in range(2)]
            lows(0, ends[0])
            pool.wait_ge(S("rope_in"), 16)
            pool.wait_ge(S("swap_in"), 8 * 16)
            pool.wait_ge(bank_free, PH["wo0"].pair0 + 2)
            with pool.Fori(0, DA_H // 2) as i:
                for hh in range(2):
                    pool.wait_ge(S("s_ready"), i * 6 + (3 * hh + 3))
                    hd = bass.ds(i * 2 + hh, 1)
                    nc.gpsimd.tensor_tensor(rtmp[:, hh, :, :], sww[:, :, hd, :].rearrange("p m a b -> p m (a b)"),
                                            rope[:, 1:2, :].to_broadcast([P, 2, SEQ]), ALU.mult)
                    nc.gpsimd.tensor_tensor(qkr[:, hh, :, 0:SEQ], qk[:, :, hd, 0:SEQ].rearrange("p m a b -> p m (a b)"),
                                            rope[:, 0:1, :].to_broadcast([P, 2, SEQ]), ALU.mult).then_inc(S("rope_mul"), 1)
                    pool.wait_ge(S("rope_mul"), i * 2 + (hh + 1))
                    nc.gpsimd.tensor_tensor(qkr[:, hh, :, 0:SEQ], qkr[:, hh, :, 0:SEQ], rtmp[:, hh, :, :], ALU.add)
                    nc.gpsimd.tensor_copy(qkr[:, hh, :, SEQ:NT], qk[:, :, hd, SEQ:NT].rearrange("p m a b -> p m (a b)"))\
                        .then_inc(S("qkr_ready"), 1)
            lows(ends[0], ends[1])
            pool.wait_ge(bank_free, PH["wo1"].pair0 + 2)
            with pool.Fori(0, KT // 2) as i:
                for b in range(2):
                    pool.wait_ge(S("ns_ready"), i * 8 + (4 * b + 4))
                    kt = bass.ds(i * 2 + b, 1)
                    nc.gpsimd.tensor_copy(qks[:, b, 0:SEQ], q1[:, kt, :].rearrange("p a b -> p (a b)"))
                    nc.gpsimd.tensor_copy(qks[:, b, SEQ:], k1[:, kt, :].rearrange("p a b -> p (a b)")).then_inc(S("qks_ready"), 1)
            lows(ends[1], UNITS)

        @block.scalar
        def _(act):
            def high(u_, n, slot):
                act.wait_ge(landed[slot], n * 16)
                act.wait_ge(units_done, u_ + 1)
                nc.scalar.activation(wh[:, slot, :, :], raw[:, slot, :, :], ACT.Copy).then_inc(hi_ready, 1)

            def high_step(ph, i, j):
                for half in range(2):
                    c = 2 * (ph.step0 + j + 1) + half
                    if isinstance(i, int) and c + 2 * ph.body * i >= UNITS:
                        return
                    high(i * (2 * ph.body) + c, i * (2 * ph.body // SLOTS) + (c // SLOTS + 1), c % SLOTS)

            def stream_only(ph, peel=0):
                def body(i):
                    for j in range(ph.body):
                        high_step(ph, i, j)
                run(act, ph, body, peel)

            def preload(func):
                nc.scalar.activation(idle[:], eps[:], func)

            def norm(name, src, n):
                for k in range(0, KT, 2):
                    nc.scalar.activation(sq[:, k:k + 2, 0:n], src[:, k:k + 2, 0:n], ACT.Square)\
                        .then_inc(S("sq_ready"), 1)
                preload(ACT.Sqrt)
                act.wait_ge(S("sum_ready"), NORMS.index(name) + 1)
                nc.scalar.activation(rstd[:, 0:n], ps[:, 4, 0:n], ACT.Sqrt, scale=1.0 / D, bias=eps[:, 0:1])\
                    .then_inc(S("root_ready"), 1)

            def split(sem, count0, src, n, scale=None):
                for k in range(KT):
                    act.wait_ge(S(sem), count0 + k + 1)
                    nc.scalar.activation(xh[:, k, 0:n], src[:, k, 0:n], ACT.Copy,
                                         scale=1.0 if scale is None else scale[:, k:k + 1]).then_inc(S("xh_ready"), 1)

            def split_shifted(count0, l, shift, n):
                for k in range(KT):
                    act.wait_ge(S("xr_ready"), count0 + k + 1)
                    for c in range(n // SEQ):
                        t = slice(c * SEQ, c * SEQ + SEQ)
                        nc.scalar.activation(xh[:, k, t], y[:, k, t], ACT.Identity,
                                             bias=mod[:, l, 8 * shift + k, c:c + 1]).then_inc(S("xh_ready"), 1)

            act.sem_inc(S("ne_ready"), 2)
            act.wait_ge(S("cond_in"), 16)
            nc.scalar.activation(csb[:], csb[:], ACT.Silu).then_inc(S("cond_ready"), 1)
            for u_ in range(2):
                high(u_, 1, u_)
            act.wait_ge(S("lam_dot"), 1)
            nc.scalar.activation(lam4[:, 2:4], lam4[:, 0:2], ACT.Exp).then_inc(S("lam_exp"), 1)

            act.wait_ge(S("x_in"), 16)
            act.wait_ge(S("consts"), 2)
            norm("pre1", h, SEQ)
            split("xr_ready", 0, y, SEQ, par_ap("mix_pre"))
            stream_only(PH["in_f"])
            act.wait_ge(bank_free, PH["in_v"].pair0 + 2)
            for half in range(2):
                a, b = slice(64 * half, 64 * half + 64), slice(64 - 64 * half, 128 - 64 * half)
                act.dma_start(sw[a, :, :], u[b, 8:16, :]).then_inc(S("ret_swap"), 16)
            stream_only(PH["in_v"])
            nc.scalar.activation(u[:, 4:8, :], u[:, 4:8, :], ACT.Sigmoid).then_inc(S("sig_ready"), 1)
            nc.scalar.activation(u[:, 16:20, :], u[:, 16:20, :], ACT.Silu).then_inc(S("gate_ready"), 1)
            act.wait_ge(S("ret_o"), 1)
            nc.scalar.activation(on[:], ps[:, 2:4, :].rearrange("p a (b c) -> p a b c", b=RET_H), ACT.Square)\
                .then_inc(S("ret_sq"), 1)
            act.wait_ge(S("ret_ssq"), 1)
            nc.scalar.activation(ssq[:], ssq[:], ACT.Sqrt, scale=1.0 / P, bias=eps[:, 0:1]).then_inc(S("ret_root"), 1)
            act.wait_ge(S("dev_ready"), 1)
            nc.scalar.activation(sq[:, 0:4, 0:SEQ], cy[:], ACT.Square).then_inc(S("dev_sq"), 1)
            act.wait_ge(S("ln_sum"), 2)
            nc.scalar.activation(rstd[:, 0:SEQ], ps[:, 5, 0:SEQ], ACT.Sqrt, scale=1.0 / 512, bias=eps[:, 0:1])\
                .then_inc(S("ln_root"), 1)
            act.wait_ge(S("ln_scaled"), 1)
            for c in range(CONV_T):
                nc.scalar.activation(mix[:, c, :], cy[:, c, :], ACT.Silu, scale=par_ap("ln_w", c, 1),
                                     bias=par_ap("ln_b", c, 1)).then_inc(S("mix_conv"), 1)
            act.wait_ge(S("mix_conv"), CONV_T)
            split("mix_ret", 0, mix, SEQ)
            stream_only(PH["out"])
            act.wait_ge(bank_free, PH["gu"].pair0 + 2)
            norm("post1", y, SEQ)
            act.wait_ge(S("h_ready"), KT)
            norm("fpre1", h, SEQ)
            split("xr_ready", KT, y, SEQ, par_ap("ffn_pre"))

            def gate_up(ph, n, f0):
                def body(i):
                    for j in range(2):
                        high_step(ph, i, j)
                        pair_done(act, ph, i, j)
                        act.wait_ge(S("f_lo"), i * 2 + (f0 + j + 1))
                        nc.scalar.activation(sil[:, j, 0:n], ps[:, 2 * j, 0:n], ACT.Silu).then_inc(S("silu_ready"), 1)
                        act.wait_ge(bank_free, i * 2 + (ph.pair0 + j + 3))
                        settled(act)
                        nc.scalar.activation(fh[n][:, i * 2 + j, :], ft[:, j, 0:n], ACT.Copy).then_inc(S("f_hi"), 1)
                preload(ACT.Silu)
                run(act, ph, body)

            gate_up(PH["gu"], SEQ, 0)
            stream_only(PH["dn"])
            act.wait_ge(bank_free, PH["pp"].pair0 + 2)
            act.dma_start(ptf[:], pin).then_inc(S("p_in"), 16)
            norm("fpost1", y, SEQ)
            act.wait_ge(S("p_in"), 16)
            nc.scalar.activation(pth[:], ptf[:], ACT.Copy).then_inc(S("p_hi"), 1)
            high_step(PH["pp"], 0, 0)
            split("h_ready", KT, h, SEQ)

            def gate_e(i):
                ph = PH["pg"]
                for j in range(2):
                    high_step(ph, i, j)
                    pair_done(act, ph, i, j)
                    act.wait_ge(bank_free, i * 2 + (ph.pair0 + j + 1))
                    nc.scalar.activation(sil[:, j, :].rearrange("p (a b) -> p a b", a=2),
                                         ps[:, 2 * j:2 * j + 2, 0:SEQ], ACT.Sigmoid).then_inc(S("sigm_ready"), 1)
            preload(ACT.Sigmoid)
            run(act, PH["pg"], gate_e)
            act.wait_ge(bank_free, PH["q0"].pair0 + 2)
            norm("ple1", ppo, SEQ)
            act.wait_ge(S("h_ready"), 3 * KT)
            act.dma_start(rope[:], tab_rope).then_inc(S("rope_in"), 16)

            for l in range(2):
                norm(f"m{l}", h, NT)
                split_shifted((2 + 2 * l) * KT, l, 0, NT)
                stream_only(PH[f"q{l}"])
                if l == 1:
                    act.wait_ge(S("xl_ready"), XL_COUNT["m1"])
                    act.dma_start(mask[:], tab_mask).then_inc(S("mask_in"), 16)
                    for t in range(2):
                        for rr in range(2):
                            row0 = 2 * t + rr
                            for kr in range(4):
                                src = bass.AP(rpb.tensor, (kr + 7 - row0) * 31 + 15 - 63, [[1, 64], [15 * 31, NA_H], [1, 64]])
                                act.dma_start(bias[64 * rr:64 * rr + 64, t, :, 64 * kr:64 * kr + 64], src)\
                                    .then_inc(S("bias_in"), 16)
                stream_only(PH[f"k{l}"])
                if l == 0:
                    act.wait_ge(bank_free, PH["v0"].pair0 + 2)
                    for b in range(4):
                        src, dst = slice(32 * b, 32 * b + 32), slice(32 * (b ^ 1), 32 * (b ^ 1) + 32)
                        for m in range(2):
                            act.dma_start(sww[dst, m, :, :], qk[src, m, :, 0:SEQ]).then_inc(S("swap_in"), 16)
                stream_only(PH[f"v{l}"])
                preload(ACT.Exp)
                if l == 0:
                    def exps(v, q, k3, r6):
                        act.wait_ge(S("pt_psum"), v + 1)
                        for m in range(2):
                            act.wait_ge(S("s_max"), v + 1)
                            for t in range(1 if k3 < 2 else 2):
                                c = slice(0, 512) if k3 < 2 else slice(t * 256, t * 256 + 256)
                                nc.scalar.activation(e2[:, q, m, c], ps[:, 2 * q + m, c], ACT.Exp, scale=0.125,
                                                     bias=sm[:, r6, 2 * t + m:2 * t + m + 1],
                                                     accum_out=sm[:, r6, 4 + 2 * t + m:5 + 2 * t + m])\
                                    .then_inc(S("e_ready"), 2 if k3 < 2 else 1)

                    def probs(v, q):
                        act.wait_ge(S("pt_psum"), v + 3)
                        act.wait_ge(S("pv_done"), v + 1)
                        nc.scalar.activation(pt[:, q, :, :], ps[:, 4 + q, :].rearrange("p (a b) -> p a b", a=4), ACT.Copy)\
                            .then_inc(S("pt_ready"), 1)

                    act.wait_ge(bank_free, PH["wo0"].pair0 + 2)
                    def take_o(v, head, q, k3, r6):
                        for t in range(1 if k3 < 2 else 2):
                            act.wait_ge(S("pv_done"), v + 3)
                            settled(act)
                            ins = nc.scalar.activation(qk[:, 0, head, (k3 + t) * P:(k3 + t) * P + P], ps[:, 6 + q, t * P:t * P + P],
                                                       ACT.Copy, scale=sm[:, r6, 8 + 2 * t:9 + 2 * t])
                        ins.then_inc(S("o_taken"), 1)

                    def step(i, w):
                        if live(i, w - 4, DA_H // 2, 6):
                            u_ = w - 4
                            take_o(i * 6 + u_, i * 2 + u_ // 3, u_ % 2, u_ % 3, u_ % 6)
                        if live(i, w - 2, DA_H // 2, 6):
                            probs(i * 6 + (w - 2), w % 2)
                        if live(i, w, DA_H // 2, 6):
                            exps(i * 6 + w, w % 2, w % 3, w)

                    steps(act, DA_H // 2, 6, 4, step)
                    act.wait_ge(S("o_taken"), 2 + 3 * DA_H)
                    for t in range(4):
                        nc.scalar.activation(osq[:, t, :, :], qk[:, 0, :, t * P:t * P + P], ACT.Square)\
                            .then_inc(S("da_sq"), 1)
                    act.wait_ge(S("da_ssq"), 1)
                    nc.scalar.activation(ort[:], ort[:], ACT.Sqrt, scale=1.0 / P, bias=eps[:, 0:1]).then_inc(S("da_root"), 1)
                    for t in range(4):
                        for b in range(2):
                            act.wait_ge(S("o_t"), 2 * t + b + 1)
                            nc.scalar.activation(xh[:, 4 * b:4 * b + 4, t * P:t * P + P],
                                                 ps[:, b + 2 * (t % 2), :].rearrange("p (a b) -> p a b", a=4), ACT.Copy,
                                                 scale=par_ap("subln")).then_inc(S("oh_ready"), 1)
                else:
                    def nprobs(v, q):
                        act.wait_ge(S("npt_psum"), v + 3)
                        act.wait_ge(S("npv_done"), v + 1)
                        nc.scalar.activation(pt1[:, q, :, :], ps[:, 4 + q, :].rearrange("p (a b) -> p a b", a=4), ACT.Copy)\
                            .then_inc(S("npt_ready"), 1)

                    act.wait_ge(bank_free, PH["wo1"].pair0 + 2)
                    def step(i, w):
                        if live(i, w - 2, KT // 2, 8):
                            nprobs(i * 8 + (w - 2), w % 2)
                        if live(i, w, KT // 2, 8):
                            q = w % 2
                            act.wait_ge(S("npt_psum"), i * 8 + (w + 1))
                            act.wait_ge(S("ns_max"), i * 8 + (w + 1))
                            nc.scalar.activation(e1[:, q, :], s1[:, q, :], ACT.Exp, bias=sm1[:, w, 1:2],
                                                 accum_out=sm1[:, w, 2:3]).then_inc(S("ne_ready"), 1)

                    steps(act, KT // 2, 8, 2, step)
                    for t in range(2):
                        for b in range(2):
                            act.wait_ge(S("no_t"), 2 * t + b + 1)
                            nc.scalar.activation(xh[:, 4 * b:4 * b + 4, t * P:t * P + P].rearrange("p a (r c) -> p a r c", c=64),
                                                 ps[:, b + 2 * t, :].rearrange("p (a r c) -> p a r c", a=4, c=64)[:, :, :, ::-1],
                                                 ACT.Copy)\
                                .then_inc(S("oh_ready"), 1)
                n = NT if l == 0 else SEQ
                stream_only(PH[f"wo{l}"])
                act.wait_ge(bank_free, PH[f"gu{l}"].pair0 + 2)
                norm(f"f{l}", h, n)
                split_shifted((3 + 2 * l) * KT, l, 3, n)
                gate_up(PH[f"gu{l}"], n, FT * (l + 1))
                stream_only(PH[f"dn{l}"], peel=l)
                act.wait_ge(bank_free, PH[f"dn{l}"].pair0 + PH[f"dn{l}"].pairs + 2)
            norm("final", h, SEQ)

        @block.tensor
        def _(pe):
            def unit_ready(ph, i, j, half):
                c = 2 * (ph.step0 + j) + half
                pe.wait_ge(lo_ready, i * (2 * ph.body) + (c + 1 + SLOTS))
                return c % SLOTS

            def banks_ready(ph, i, pair):
                pe.wait_ge(bank_free, i * 2 + (ph.pair0 + pair + 1))

            def three(o, wa, wb, xa, xb, start, stop):
                nc.tensor.matmul(o, wa, xa, start=start, stop=False)
                nc.tensor.matmul(o, wa, xb, start=False, stop=False)
                return nc.tensor.matmul(o, wb, xa, start=False, stop=stop)

            def features(ph, n, a=xh, b=xl, ktiles=KT):
                def body(i):
                    for j in range(ph.body):
                        pair = j // ph.per_pair
                        if j % ph.per_pair == 0:
                            banks_ready(ph, i, pair)
                        for half in range(2):
                            slot = unit_ready(ph, i, j, half)
                            k0 = 2 * HALF * (j % ph.per_pair) + HALF * half
                            for o in range(2):
                                c = slice(o * P, o * P + P)
                                for kk in range(min(HALF, ktiles - k0)):
                                    k = k0 + kk
                                    mm = three(ps[:, 2 * pair + o, 0:n], wh[:, slot, kk, c], wl[:, slot, kk, c],
                                               a[:, k, 0:n], b[:, k, 0:n], k == 0, k == ktiles - 1)
                            mm.then_inc(units_done, 1)
                run(pe, ph, body)

            def tokens(ph, tiles):
                def body(i):
                    for j in range(2):
                        banks_ready(ph, i, j)
                        for half in range(2):
                            slot = unit_ready(ph, i, j, half)
                            for t in range(tiles):
                                o = ps[:, 2 * j + t // 2, (t % 2) * 256:(t % 2) * 256 + 256]
                                for kk in range(HALF):
                                    k = HALF * half + kk
                                    xa, xb = xh[:, k, t * P:t * P + P], xl[:, k, t * P:t * P + P]
                                    s0, s1_ = k == 0 and t % 2 == 0, k == KT - 1
                                    nc.tensor.matmul(o, xa, wh[:, slot, kk, :], start=s0, stop=False, skip_group_check=True)
                                    nc.tensor.matmul(o, xb, wh[:, slot, kk, :], start=False, stop=False, skip_group_check=True)
                                    mm = nc.tensor.matmul(o, xa, wl[:, slot, kk, :], start=False, stop=s1_,
                                                          skip_group_check=True)
                            mm.then_inc(units_done, 1)
                run(pe, ph, body)

            def norm_sum(name, n):
                m = NORMS.index(name)
                if m:
                    pe.wait_ge(S("root_ready"), m)
                for k in range(KT):
                    if k % 2 == 0:
                        pe.wait_ge(S("sq_ready"), 4 * m + k // 2 + 1)
                    mm = nc.tensor.matmul(ps[:, 4, 0:n], ones[:], sq[:, k, 0:n], start=k == 0, stop=k == KT - 1)
                mm.then_inc(S("sum_ready"), 1)

            pe.sem_inc(units_done, SLOTS)
            for name, n in (("s_ready", 6), ("pt_psum", 2), ("pv_done", 2), ("ns_ready", 8),
                            ("npt_psum", 2), ("npv_done", 2)):
                pe.sem_inc(S(name), n)
            pe.wait_ge(S("consts"), 2)
            pe.wait_ge(S("tab_in"), 16)

            norm_sum("pre1", SEQ)
            pe.wait_ge(S("xl_ready"), KT)
            features(PH["in_f"], SEQ)
            tokens(PH["in_v"], 2)
            pe.wait_ge(S("ret_roped"), 1)
            pe.wait_ge(bank_free, PH["out"].pair0 + 2)
            for hd in range(RET_H):
                b = hd % 2
                if hd >= 2:
                    pe.wait_ge(S("ret_s"), hd - 1)
                q_, k_ = u[:, 8 + hd, :], u[:, 12 + hd, :]
                nc.tensor.matmul(ps[:, b, 0:256], k_[:, 0:P], q_, start=True, stop=True)
                nc.tensor.matmul(ps[:, b, 256:384], k_[:, P:256], q_[:, P:256], start=True, stop=True)\
                    .then_inc(S("ret_sc"), 1)
            for hd in range(RET_H):
                pe.wait_ge(S("ret_s"), hd + 1)
                c = slice(hd * P, hd * P + P)
                nc.tensor.matmul(ps[:, 2, c], st[:, hd, 0:P], vb[:, 0, c], start=True, stop=True)
                nc.tensor.matmul(ps[:, 3, c], st[:, hd, P:256], vb[:, 0, c], start=True, stop=False)
                mm = nc.tensor.matmul(ps[:, 3, c], st[:, hd, 256:384], vb[:, 1, c], start=False, stop=True)
            mm.then_inc(S("ret_o"), 1)
            pe.wait_ge(S("ret_on"), 1)
            for hd in range(RET_H):
                for t in range(2):
                    mm = nc.tensor.transpose(ps[:, hd // 2, (hd % 2) * 256 + t * P:(hd % 2) * 256 + t * P + P],
                                             on[:, t, hd, :], ident[:])
            mm.then_inc(S("ret_t"), 1)
            pe.wait_ge(S("conv_tap"), CONV_T * CONV_W)
            for c in range(CONV_T):
                mm = nc.tensor.matmul(ps[:, 4, 0:SEQ], ones[:], cy[:, c, :], start=c == 0, stop=c == CONV_T - 1)
            mm.then_inc(S("ln_sum"), 1)
            pe.wait_ge(S("dev_sq"), 1)
            for c in range(CONV_T):
                mm = nc.tensor.matmul(ps[:, 5, 0:SEQ], ones[:], sq[:, c, 0:SEQ], start=c == 0, stop=c == CONV_T - 1)
            mm.then_inc(S("ln_sum"), 1)
            pe.wait_ge(S("xl_ready"), 2 * KT)
            features(PH["out"], SEQ)
            norm_sum("post1", SEQ)
            norm_sum("fpre1", SEQ)
            pe.wait_ge(S("xl_ready"), 3 * KT)
            features(PH["gu"], SEQ)
            pe.wait_ge(S("f_lo"), 2 + FT)
            features(PH["dn"], SEQ, fh[SEQ], fl[SEQ], FT)
            norm_sum("fpost1", SEQ)
            ph = PH["pp"]
            pe.wait_ge(S("p_lo"), 1)
            slots = [unit_ready(ph, 0, 0, half) for half in range(2)]
            flat = [(wh[:, s, :, :].rearrange("p a b -> p (a b)"), wl[:, s, :, :].rearrange("p a b -> p (a b)")) for s in slots]
            for pair in range(4):
                pe.wait_ge(bank_free, ph.pair0 + pair + 1)
                for o in range(2 * pair, 2 * pair + 2):
                    for k in range(2):
                        mm = three(ps[:, 2 * (pair % 2) + o % 2, 0:SEQ], flat[k][0][:, o * P:o * P + P],
                                   flat[k][1][:, o * P:o * P + P], pth[:, k, :], ptl[:, k, :], k == 0, k == 1)
                if pair < 3:
                    mm.then_inc(S("pp_ready"), 1)
            mm.then_inc(units_done, 2)
            pe.wait_ge(S("xl_ready"), 4 * KT)
            features(PH["pg"], SEQ)
            norm_sum("ple1", SEQ)

            for l in range(2):
                n = NT if l == 0 else SEQ
                norm_sum(f"m{l}", NT)
                pe.wait_ge(S("xl_ready"), XL_COUNT[f"m{l}"])
                features(PH[f"q{l}"], n)
                features(PH[f"k{l}"], NT)
                tokens(PH[f"v{l}"], 4)
                pe.wait_ge(bank_free, PH[f"wo{l}"].pair0 + 2)
                if l == 0:
                    def scores(v, hh, k3, q):
                        pe.wait_ge(S("e_ready"), v * 4 + 4)
                        for m in range(2):
                            rows = slice(64 * m, 64 * m + 64)
                            if k3 < 2:
                                mm = nc.tensor.matmul(ps[:, 2 * q + m, :], qkr[rows, hh, 0, k3 * P:k3 * P + P],
                                                      qkr[rows, hh, 1, :], start=True, stop=True)
                            else:
                                for t in range(2):
                                    mm = nc.tensor.matmul(ps[:, 2 * q + m, t * 256:t * 256 + 256],
                                                          qkr[rows, hh, 0, SEQ + t * P:SEQ + t * P + P],
                                                          qkr[rows, hh, 1, SEQ:NT], start=True, stop=True)
                        mm.then_inc(S("s_ready"), 1)

                    def turn(v, q):
                        pe.wait_ge(S("p_ready"), v + 1)
                        pe.wait_ge(S("pt_ready"), v + 1)
                        for t in range(4):
                            mm = nc.tensor.transpose(ps[:, 4 + q, t * P:t * P + P], e2[:, q, 0, t * P:t * P + P], ident[:])
                        mm.then_inc(S("pt_psum"), 1)

                    def values(v, head, k3, q):
                        pe.wait_ge(S("pt_ready"), v + 3)
                        pe.wait_ge(S("o_taken"), v + 1)
                        for t in range(1 if k3 < 2 else 2):
                            for c in range(4 if k3 < 2 else 2):
                                mm = nc.tensor.matmul(ps[:, 6 + q, t * P:t * P + P], pt[:, q, 2 * t + c, :],
                                                      vv[:, c if k3 < 2 else 2 + c, bass.ds(head * P, P)], start=c == 0,
                                                      stop=c == (3 if k3 < 2 else 1))
                        mm.then_inc(S("pv_done"), 1)

                    def step(i, w):
                        if live(i, w, DA_H // 2, 6):
                            if w % 3 == 0:
                                pe.wait_ge(S("qkr_ready"), i * 2 + (w // 3 + 1))
                            scores(i * 6 + w, w // 3, w % 3, w % 2)
                        if live(i, w - 2, DA_H // 2, 6):
                            turn(i * 6 + (w - 2), w % 2)
                        if live(i, w - 3, DA_H // 2, 6):
                            values(i * 6 + (w - 3), i * 2 + (w - 3) // 3, w % 3, (w - 3) % 2)

                    steps(pe, DA_H // 2, 6, 3, step)
                    for t in range(4):
                        pe.wait_ge(S("da_scaled"), t + 1)
                        for b in range(2):
                            if t >= 2:
                                pe.wait_ge(S("ol_ready"), 2 * (t - 2) + b + 1)
                            for hd in range(4):
                                mm = nc.tensor.transpose(ps[:, b + 2 * (t % 2), hd * P:hd * P + P],
                                                         qk[:, 0, 4 * b + hd, t * P:t * P + P], ident[:])
                            mm.then_inc(S("o_t"), 1)
                    pe.wait_ge(S("ol_ready"), 8)
                else:
                    def nturn(v, q):
                        pe.wait_ge(S("ne_ready"), v + 3)
                        pe.wait_ge(S("npt_ready"), v + 1)
                        for c in range(4):
                            mm = nc.tensor.transpose(ps[:, 4 + q, c * P:c * P + P], e1[:, q, c * P:c * P + P], ident[:])
                        mm.then_inc(S("npt_psum"), 1)

                    def nvalues(v, tile, hh, q):
                        pe.wait_ge(S("npt_ready"), v + 3)
                        pe.wait_ge(S("no_taken"), v + 1)
                        for c in range(4):
                            mm = nc.tensor.matmul(ps[:, 6 + q, 0:64], pt1[:, q, c, :],
                                                  v1[:, c, bass.ds(tile * P + hh * 64, 64)], start=c == 0, stop=c == 3)
                        mm.then_inc(S("npv_done"), 1)

                    def step(i, w):
                        if live(i, w, KT // 2, 8):
                            hh, t, b, q = w // 2 % 2, w % 2, w // 4, w % 2
                            if w % 4 == 0:
                                pe.wait_ge(S("qks_ready"), i * 2 + (b + 1))
                            pe.wait_ge(S("ns_taken"), i * 8 + (w + 1))
                            rows = slice(64 * hh, 64 * hh + 64)
                            nc.tensor.matmul(ps[:, q, :], qks[rows, b, t * P:t * P + P], qks[rows, b, SEQ:],
                                             start=True, stop=True).then_inc(S("ns_ready"), 1)
                        if live(i, w - 2, KT // 2, 8):
                            nturn(i * 8 + (w - 2), w % 2)
                        if live(i, w - 3, KT // 2, 8):
                            nvalues(i * 8 + (w - 3), i * 2 + (w - 3) // 4, (w - 3) // 2 % 2, (w - 3) % 2)

                    steps(pe, KT // 2, 8, 3, step)
                    pe.wait_ge(S("no_taken"), 2 + 2 * NA_H)
                    for t in range(2):
                        for b in range(2):
                            for hd in range(4):
                                c = (4 * b + hd) * P
                                mm = nc.tensor.transpose(ps[:, b + 2 * t, hd * P:hd * P + P], o1[:, t, c:c + P], ident[:])
                            mm.then_inc(S("no_t"), 1)
                    pe.wait_ge(S("nol_ready"), 4)
                features(PH[f"wo{l}"], n)
                norm_sum(f"f{l}", n)
                pe.wait_ge(S("xl_ready"), XL_COUNT[f"f{l}"])
                features(PH[f"gu{l}"], n)
                pe.wait_ge(S("f_lo"), 2 + FT * (l + 2))
                features(PH[f"dn{l}"], n, fh[n], fl[n], FT)
            norm_sum("final", SEQ)

        @block.vector
        def _(dve):
            link = Link(dve, "dve_link")
            V = nc.vector

            for name, n in (("ada_used", ADA_SLOTS), ("bank_free", 2), ("f_lo", 2), ("e_ready", 8), ("pt_ready", 2), ("o_taken", 2),
                            ("npt_ready", 2), ("no_taken", 2), ("ns_taken", 2)):
                dve.sem_inc(S(name), n)
            V.memset(up[:, :, 0:CONV_W - 1], 0.0)
            dve.wait_ge(S("prm_in"), 16)
            for m in range(2):
                V.tensor_tensor(y[:, m, 0:64], par_ap("lam", 128 * m, 64), par_ap("lam", 128 * m + 64, 64), ALU.mult)\
                    .then_inc(S("lam_mul"), 1)
            dve.wait_ge(S("lam_mul"), 2)
            V.tensor_reduce(lam4[:, 0:2], y[:, 0:2, 0:64], AX_X, ALU.add).then_inc(S("lam_dot"), 1)

            dve.wait_ge(S("lam_exp"), 1)
            link(V.tensor_tensor(lam4[:, 4:5], lam4[:, 3:4], lam4[:, 2:3], ALU.subtract))
            link(V.tensor_scalar(lam4[:, 5:6], lam4[:, 4:5], -LAM_INIT, None, ALU.add))

            xl_count, xh_count, xr_count = [0], [0], [0]

            def recip(name, n):
                dve.wait_ge(S("root_ready"), NORMS.index(name) + 1)
                link(V.reciprocal(rstd[:, 0:n], rstd[:, 0:n]))

            def scale_in(src, n, gain):
                for k in range(KT):
                    V.tensor_tensor(y[:, k, 0:n], src[:, k, 0:n], rstd[:, 0:n], ALU.mult).then_inc(S("xr_ready"), 1)
                xr_count[0] += KT
                for k in range(KT):
                    xh_count[0] += 1
                    dve.wait_ge(S("xh_ready"), xh_count[0])
                    V.scalar_tensor_tensor(xl[:, k, 0:n], y[:, k, 0:n], gain[:, k:k + 1], xh[:, k, 0:n].bitcast(F32),
                                           ALU.mult, ALU.subtract).then_inc(S("xl_ready"), 1)

            def modulate(l, w, n):
                parts = [slice(c * SEQ, c * SEQ + SEQ) for c in range(n // SEQ)]
                for k in range(KT):
                    for c, t in enumerate(parts):
                        ins = V.scalar_tensor_tensor(y[:, k, t], h[:, k, t], gsc[:, l, w, k, c:c + 1], rstd[:, t],
                                                     ALU.mult, ALU.mult)
                    ins.then_inc(S("xr_ready"), 1)
                for k in range(KT):
                    for c, t in enumerate(parts):
                        xh_count[0] += 1
                        dve.wait_ge(S("xh_ready"), xh_count[0])
                        V.scalar_tensor_tensor(xl[:, k, t], y[:, k, t], mod[:, l, 24 * w + k, c:c + 1],
                                               xh[:, k, t].bitcast(F32), ALU.add, ALU.subtract).then_inc(S("xl_ready"), 1)

            def condition(ph, i, j):
                if ph.name not in ADA_WOVEN:
                    return
                per, slots, a0 = ADA_WOVEN[ph.name]
                for s in range(per * j, per * j + per):
                    l, first = a0 // ADA_UNITS, a0 % ADA_UNITS
                    dve.wait_ge(ada_landed[s % slots],
                                i * (16 * 2 * per // slots) + 16 * (slot_tenants(ph.name, s % slots) + s // slots + 1))
                    for c in range(2):
                        dve.wait_ge(ada_used, i * (2 * per) + (a0 + s + ADA_SLOTS))
                        ins = V.scalar_tensor_tensor(unread[:, c, :], ada[:, s % slots, :], 1.0, csb[:, c, :],
                                                     ALU.mult, ALU.mult,
                                                     accum_out=mod[:, l, bass.ds(i * (2 * per) + (first + s), 1), c])
                    ins.then_inc(ada_used, 1)

            def modulation(l):
                dve.wait_ge(ada_used, (l + 1) * ADA_UNITS + ADA_SLOTS)
                bias_ = par_ap("ada_b", l * ADA_UNITS, ADA_UNITS)
                link(V.tensor_tensor(mod[:, l, :, :], mod[:, l, :, :],
                                     bias_.unsqueeze(2).to_broadcast([P, ADA_UNITS, 2]), ALU.add))
                for w, name in enumerate(("n_mix", "n_ffn")):
                    V.scalar_tensor_tensor(gsc[:, l, w, :, :], mod[:, l, 8 + 24 * w:16 + 24 * w, :], 1.0,
                                           par_ap(name, l * KT, KT).unsqueeze(2).to_broadcast([P, KT, 2]),
                                           ALU.add, ALU.mult).then_inc(S("gsc_ready"), 1)
                dve.wait_ge(S("gsc_ready"), 2 * (l + 1))

            def low_of(src, n):
                for k in range(KT):
                    xh_count[0] += 1
                    dve.wait_ge(S("xh_ready"), xh_count[0])
                    V.tensor_tensor(xl[:, k, 0:n], src[:, k, 0:n], xh[:, k, 0:n].bitcast(F32), ALU.subtract)\
                        .then_inc(S("xl_ready"), 1)

            def add_normed(src, gain):
                for k in range(KT):
                    V.scalar_tensor_tensor(src[:, k, 0:SEQ], src[:, k, 0:SEQ], gain[:, k:k + 1], rstd[:, 0:SEQ],
                                           ALU.mult, ALU.mult).then_inc(S("post_scaled"), 1)
                    post[0] += 1
                for k in range(KT):
                    dve.wait_ge(S("post_scaled"), post[0] - KT + k + 1)
                    V.tensor_tensor(h[:, k, 0:SEQ], h[:, k, 0:SEQ], src[:, k, 0:SEQ], ALU.add).then_inc(S("h_ready"), 1)

            post = [0]

            def take(ph, n, dst, falling=False):
                def body(i):
                    for j in range(2):
                        condition(ph, i, j)
                        pair_done(dve, ph, i, j)
                        src, to = ps[:, 2 * j:2 * j + 2, 0:n], dst[:, bass.ds(i * 4 + 2 * j, 2), 0:n]
                        if falling:
                            src = src.rearrange("p a (r c) -> p a r c", c=64)[:, :, :, ::-1]
                            to = to.rearrange("p a (r c) -> p a r c", c=64)
                        V.tensor_scalar(to, src, 1.0, None, ALU.mult).then_inc(bank_free, 1)
                run(dve, ph, body)

            def take_tokens(ph, tiles, dst):
                def body(i):
                    for j in range(2):
                        condition(ph, i, j)
                        pair_done(dve, ph, i, j)
                        V.tensor_scalar(dst[:, :, bass.ds(i * 512 + 256 * j, 256)],
                                        ps[:, 2 * j:2 * j + tiles // 2, :].rearrange("p a (b c) -> p (a b) c", b=2),
                                        1.0, None, ALU.mult).then_inc(bank_free, 1)
                run(dve, ph, body)

            def take_gated(ph, n, l, w):
                def body(i):
                    for j in range(2):
                        pair_done(dve, ph, i, j)
                        for o in range(2):
                            for c in range(n // SEQ):
                                t = slice(c * SEQ, c * SEQ + SEQ)
                                k = i * 4 + (2 * j + o)
                                g = mod[:, l, bass.ds(i * 4 + (2 * j + o + 16 + 24 * w), 1), c:c + 1].rearrange("p a b -> p (a b)")
                                hk = h[:, bass.ds(k, 1), t].rearrange("p a b -> p (a b)")
                                ins = V.scalar_tensor_tensor(hk, ps[:, 2 * j + o, t], g, hk, ALU.mult, ALU.add)
                        ins.then_inc(bank_free, 1)
                run(dve, ph, body)

            def gate_up(ph, n, f0):
                def body(i):
                    for j in range(2):
                        condition(ph, i, j)
                        dve.wait_ge(S("f_lo"), i * 2 + (f0 + j + 1))
                        dve.wait_ge(S("silu_ready"), i * 2 + (f0 + j + 1))
                        V.tensor_tensor(ft[:, j, 0:n], sil[:, j, 0:n], ps[:, 2 * j + 1, 0:n], ALU.mult).then_inc(bank_free, 1)
                        dve.wait_ge(S("f_hi"), i * 2 + (f0 + j + 1))
                        f1 = bass.ds(i * 2 + j, 1)
                        V.tensor_tensor(fl[n][:, f1, :].rearrange("p a b -> p (a b)"), ft[:, j, 0:n],
                                        fh[n][:, f1, :].rearrange("p a b -> p (a b)").bitcast(F32),
                                        ALU.subtract).then_inc(S("f_lo"), 1)
                run(dve, ph, body)

            dve.wait_ge(S("cond_ready"), 1)
            recip("pre1", SEQ)
            scale_in(h, SEQ, par_ap("mix_pre"))
            take(PH["in_f"], SEQ, u)
            take_tokens(PH["in_v"], 2, vb)
            dve.wait_ge(S("ret_swap"), 32)
            dve.wait_ge(S("ret_in"), 32)
            V.tensor_tensor(u[:, 8:16, :], u[:, 8:16, :], rcs[:, 0:1, :].to_broadcast([P, 8, SEQ]), ALU.mult)
            link(V.tensor_tensor(sw[:], sw[:], rcs[:, 1:2, :].to_broadcast([P, 8, SEQ]), ALU.mult))
            V.tensor_tensor(u[:, 8:16, :], u[:, 8:16, :], sw[:], ALU.add).then_inc(S("ret_roped"), 1)
            for hd in range(RET_H):
                dve.wait_ge(S("ret_sc"), hd + 1)
                V.tensor_tensor(st[:, hd, :], ps[:, hd % 2, 0:384], dt_[:, hd, :], ALU.mult).then_inc(S("ret_s"), 1)
            dve.wait_ge(S("ret_sq"), 1)
            V.tensor_reduce(ssq[:], on[:].rearrange("p a b c -> p (a b) c"), AX_X, ALU.add).then_inc(S("ret_ssq"), 1)
            dve.wait_ge(S("ret_root"), 1)
            link(V.reciprocal(ssq[:], ssq[:]))
            V.tensor_tensor(on[:].rearrange("p a b c -> p (a b) c"),
                            ps[:, 2:4, :].rearrange("p a (b c) -> p (a b) c", c=P),
                            ssq[:].unsqueeze(2).to_broadcast([P, 8, P]), ALU.mult).then_inc(S("ret_on"), 1)
            dve.wait_ge(S("sig_ready"), 1)
            link(V.tensor_tensor(up[:, :, CONV_W - 1:], u[:, 0:4, :], u[:, 4:8, :], ALU.mult))
            for c in range(CONV_T):
                V.tensor_scalar(cy[:, c, :], up[:, c, 0:SEQ], par_ap("conv_w", c * CONV_W, 1), par_ap("conv_b", c, 1),
                                ALU.mult, ALU.add).then_inc(S("conv_tap"), 1)
            cw0 = PAT["conv_w"][0]
            with dve.Fori(1, CONV_W) as i:
                for c in range(CONV_T):
                    dve.wait_ge(S("conv_tap"), i * CONV_T + (c - CONV_T + 1))
                    V.scalar_tensor_tensor(cy[:, c, :], up[:, c, bass.ds(i, SEQ)], prm[:, bass.ds(i + (cw0 + c * CONV_W), 1)],
                                           cy[:, c, :], ALU.mult, ALU.add).then_inc(S("conv_tap"), 1)
            dve.wait_ge(S("conv_tap"), CONV_T * CONV_W)
            dve.wait_ge(S("ret_t"), 1)
            dve.wait_ge(S("gate_ready"), 1)
            V.tensor_tensor(mix[:, 4:8, :], ps[:, 0:2, :].rearrange("p a (b c) -> p (a b) c", b=2), u[:, 16:20, :], ALU.mult)\
                .then_inc(S("mix_ret"), KT)
            dve.wait_ge(S("ln_sum"), 1)
            for c in range(CONV_T):
                ins = V.scalar_tensor_tensor(cy[:, c, :], ps[:, 4, 0:SEQ], -1.0 / 512, cy[:, c, :], ALU.mult, ALU.add)
            ins.then_inc(S("dev_ready"), 1)
            dve.wait_ge(S("dev_ready"), 1)
            dve.wait_ge(S("ln_root"), 1)
            link(V.reciprocal(rstd[:, 0:SEQ], rstd[:, 0:SEQ]))
            V.tensor_tensor(cy[:], cy[:], rstd[:, 0:SEQ].unsqueeze(1).to_broadcast([P, CONV_T, SEQ]), ALU.mult)\
                .then_inc(S("ln_scaled"), 1)
            low_of(mix, SEQ)
            take(PH["out"], SEQ, y)
            recip("post1", SEQ)
            add_normed(y, par_ap("mix_post"))
            recip("fpre1", SEQ)
            scale_in(h, SEQ, par_ap("ffn_pre"))
            gate_up(PH["gu"], SEQ, 0)
            take(PH["dn"], SEQ, y)
            recip("fpost1", SEQ)
            add_normed(y, par_ap("ffn_post"))
            dve.wait_ge(S("p_hi"), 1)
            V.tensor_tensor(ptl[:], ptf[:], pth[:].bitcast(F32), ALU.subtract).then_inc(S("p_lo"), 1)
            low_of(h, SEQ)
            ph = PH["pp"]
            for pair in range(4):
                if pair < 3:
                    dve.wait_ge(S("pp_ready"), pair + 1)
                else:
                    dve.wait_ge(units_done, 2 * ph.step0 + 2 + SLOTS)
                b = 2 * (pair % 2)
                V.tensor_copy(ppo[:, 2 * pair:2 * pair + 2, :], ps[:, b:b + 2, 0:SEQ]).then_inc(bank_free, 1)

            def gated_e(i):
                ph = PH["pg"]
                for j in range(2):
                    dve.wait_ge(S("sigm_ready"), i * 2 + (j + 1))
                    pp2 = ppo[:, bass.ds(i * 4 + 2 * j, 2), :]
                    V.tensor_tensor(pp2, pp2, sil[:, j, :].rearrange("p (a b) -> p a b", a=2), ALU.mult).then_inc(bank_free, 1)
            run(dve, PH["pg"], gated_e)
            recip("ple1", SEQ)
            add_normed(ppo, par_ap("ple_post"))

            for l in range(2):
                n = NT if l == 0 else SEQ
                modulation(l)
                recip(f"m{l}", NT)
                modulate(l, 0, NT)
                if l == 0:
                    take(PH["q0"], NT, qk[:, 0, :, :])
                    take(PH["k0"], NT, qk[:, 1, :, :])
                    take_tokens(PH["v0"], 4, vv)
                    dve.wait_ge(bank_free, PH["wo0"].pair0 + 2)

                    def maxima(v, q, k3, r6):
                        dve.wait_ge(S("s_ready"), v + 7)
                        src = ps[:, 2 * q:2 * q + 2, :]
                        if k3 < 2:
                            mx = sm[:, r6, 12:14]
                            link(V.tensor_reduce(mx, src, AX_X, ALU.max))
                            V.tensor_scalar(sm[:, r6, 0:2], mx, -0.125, None, ALU.mult).then_inc(S("s_max"), 1)
                        else:
                            mx = sm[:, r6, 12:16]
                            link(V.tensor_reduce(mx.rearrange("p (t m) -> p m t", m=2),
                                                 src.rearrange("p m (t c) -> p m t c", t=2), AX_X, ALU.max))
                            V.tensor_scalar(sm[:, r6, 0:4], mx, -0.125, None, ALU.mult).then_inc(S("s_max"), 1)

                    def combine(v, q, k3, r6):
                        dve.wait_ge(S("e_ready"), v * 4 + 12)
                        tiles = 1 if k3 < 2 else 2
                        sums = sm[:, r6, 4:4 + 2 * tiles].rearrange("p (t m) -> p t m", m=2)
                        inv = sm[:, r6, 8:8 + 2 * tiles].rearrange("p (t m) -> p t m", m=2)
                        link(V.reciprocal(inv, sums))
                        link(V.scalar_tensor_tensor(inv[:, :, 1], sums[:, :, 0], lam4[:, 5:6], inv[:, :, 1], ALU.mult, ALU.mult))
                        for t in range(tiles):
                            c = slice(0, 512) if k3 < 2 else slice(t * 256, t * 256 + 256)
                            ins = V.scalar_tensor_tensor(e2[:, q, 0, c], e2[:, q, 1, c], sm[:, r6, 9 + 2 * t:10 + 2 * t],
                                                         e2[:, q, 0, c], ALU.mult, ALU.add)
                        ins.then_inc(S("p_ready"), 1)

                    def step(i, w):
                        if live(i, w - 1, DA_H // 2, 6):
                            combine(i * 6 + (w - 1), (w - 1) % 2, (w - 1) % 3, (w - 1) % 6)
                        if live(i, w, DA_H // 2, 6):
                            maxima(i * 6 + w, w % 2, w % 3, w)

                    link.steps(DA_H // 2, 6, 1, 18, step)
                    for t in range(4):
                        dve.wait_ge(S("da_sq"), t + 1)
                        ins = V.tensor_reduce(ort[:, t, :], osq[:, t, :, :], AX_X, ALU.add)
                    ins.then_inc(S("da_ssq"), 1)
                    dve.wait_ge(S("da_root"), 1)
                    link(V.reciprocal(ort[:], ort[:]))
                    link(V.tensor_scalar(ort[:], ort[:], 1.0 - LAM_INIT, None, ALU.mult))
                    for t in range(4):
                        o_ = qk[:, 0, :, t * P:t * P + P]
                        V.tensor_tensor(o_, o_, ort[:, t, :].unsqueeze(2).to_broadcast([P, DA_H, P]), ALU.mult)\
                            .then_inc(S("da_scaled"), 1)
                    for t in range(4):
                        for b in range(2):
                            dve.wait_ge(S("oh_ready"), 2 * t + b + 1)
                            x_ = (slice(None), slice(4 * b, 4 * b + 4), slice(t * P, t * P + P))
                            V.scalar_tensor_tensor(xl[x_], ps[:, b + 2 * (t % 2), :].rearrange("p (a b) -> p a b", a=4),
                                                   par_ap("subln"), xh[x_].bitcast(F32), ALU.mult, ALU.subtract)\
                                .then_inc(S("ol_ready"), 1)
                else:
                    take(PH["q1"], SEQ, q1, falling=True)
                    take(PH["k1"], NT, k1)
                    dve.wait_ge(S("bias_in"), 16 * 16)
                    dve.wait_ge(S("mask_in"), 16)
                    for t in range(2):
                        V.tensor_tensor(bias[:, t, :, :], bias[:, t, :, :], mask[:].unsqueeze(1).to_broadcast([P, NA_H, SEQ]),
                                        ALU.add).then_inc(S("masked"), 1)
                    take_tokens(PH["v1"], 4, v1)
                    dve.wait_ge(S("masked"), 2)

                    def nscale(i, w):
                        q, t, r8 = w % 2, w % 2, w
                        dve.wait_ge(S("ne_ready"), i * 8 + (w + 1))
                        dve.wait_ge(S("ns_ready"), i * 8 + (w + 9))
                        head = bass.ds(i * 4 + w // 2, 1)
                        V.scalar_tensor_tensor(s1[:, q, 0:SEQ], ps[:, q, 0:SEQ], 0.125,
                                               bias[:, t, head, :].rearrange("p a b -> p (a b)"), ALU.mult, ALU.add)
                        V.tensor_scalar(s1[:, q, SEQ:], ps[:, q, SEQ:], 0.125, None, ALU.mult).then_inc(S("ns_taken"), 1)
                        dve.wait_ge(S("ns_taken"), i * 8 + (w + 3))
                        link(V.tensor_reduce(sm1[:, r8, 0:1], s1[:, q, :], AX_X, ALU.max))
                        V.tensor_scalar(sm1[:, r8, 1:2], sm1[:, r8, 0:1], -1.0, None, ALU.mult).then_inc(S("ns_max"), 1)

                    def ntake(i, w):
                        q, t, r8 = w % 2, w % 2, w % 8
                        dve.wait_ge(S("npv_done"), i * 8 + (w + 3))
                        link(V.reciprocal(sm1[:, r8, 3:4], sm1[:, r8, 2:3]))
                        V.tensor_scalar(o1[:, t, bass.ds(i * 256 + (w // 2) * 64, 64)], ps[:, 6 + q, 0:64], sm1[:, r8, 3:4], None,
                                        ALU.mult).then_inc(S("no_taken"), 1)

                    def step(i, w):
                        if live(i, w - 4, KT // 2, 8):
                            ntake(i, w - 4)
                        if live(i, w, KT // 2, 8):
                            nscale(i, w)

                    link.steps(KT // 2, 8, 4, 16, step)
                    for t in range(2):
                        for b in range(2):
                            dve.wait_ge(S("oh_ready"), 8 + 2 * t + b + 1)
                            x_ = (slice(None), slice(4 * b, 4 * b + 4), slice(t * P, t * P + P))
                            V.tensor_tensor(xl[x_].rearrange("p a (r c) -> p a r c", c=64),
                                            ps[:, b + 2 * t, :].rearrange("p (a r c) -> p a r c", a=4, c=64)[:, :, :, ::-1],
                                            xh[x_].bitcast(F32).rearrange("p a (r c) -> p a r c", c=64), ALU.subtract).then_inc(S("nol_ready"), 1)
                take_gated(PH[f"wo{l}"], n, l, 0)
                recip(f"f{l}", n)
                modulate(l, 1, n)
                gate_up(PH[f"gu{l}"], n, FT * (l + 1))
                take_gated(PH[f"dn{l}"], n, l, 1)
            recip("final", SEQ)
            for k in range(KT):
                V.scalar_tensor_tensor(y[:, k, 0:SEQ], h[:, k, 0:SEQ], par_ap("final", k, 1), rstd[:, 0:SEQ], ALU.mult, ALU.mult)\
                    .then_inc(S("final_ready"), 1)


def tiles_of(w):
    k, n = w.shape
    w = w.reshape(k // 1024, 2, HALF, P, n // 256, 256)
    return np.ascontiguousarray(w.transpose(4, 0, 1, 3, 2, 5)).reshape(-1, P, HALF, 256)


def feature_tiles(v):
    return np.ascontiguousarray(v.T.reshape(-1, P, v.shape[0]).transpose(1, 0, 2))


def gate_up_tiles(g, u):
    both = np.stack([g.reshape(D, FT, P), u.reshape(D, FT, P)], axis=2)
    return tiles_of(both.reshape(D, 2 * FF))


def down_tiles(w):
    padded = np.zeros((3 * 1024, D), w.dtype)
    padded[:FF] = w
    return tiles_of(padded)


def shape_tables():
    f = np.float32
    tab = np.eye(P, dtype=f)
    log_g = np.log(1.0 - 2.0 ** (-5.0 - np.arange(RET_H)))
    i = np.arange(SEQ)
    ret = np.zeros((P, RET_H * 384 + 2 * SEQ), f)
    for hd in range(RET_H):
        d = i[None, :] - i[:, None]
        full = np.where(d >= 0, np.exp(log_g[hd] * np.maximum(d, 0)), 0) * P ** -0.5
        ret[:, hd * 384:hd * 384 + 256] = full[0:P, :]
        ret[:, hd * 384 + 256:hd * 384 + 384] = full[P:, P:]
    freqs = f(10000.0) ** (-np.arange(64, dtype=f) / f(64))
    ang = np.arange(SEQ, dtype=f)[None, :] * np.concatenate([freqs, freqs])[:, None]
    ret[:, RET_H * 384:RET_H * 384 + SEQ] = np.cos(ang)
    ret[:, RET_H * 384 + SEQ:] = np.sin(ang) * np.where(np.arange(P) < 64, -1, 1)[:, None]
    fr = f(1.0) / (f(10000.0) ** (np.arange(0, 32, 2, dtype=f) / f(32)))
    pr, pc = (i // 64).astype(f), (i % 64).astype(f)
    ar, ac = fr[:, None] * pr[None, :], fr[:, None] * pc[None, :]
    half = np.concatenate([ar, ac, ar, ac])
    sign = np.where(np.arange(64) < 32, -1, 1)[:, None]
    rope_ = np.zeros((P, 2, SEQ), f)
    rope_[:, 0] = np.tile(np.cos(half), (2, 1))
    rope_[:, 1] = np.tile(np.sin(half) * sign, (2, 1))
    c = np.arange(64)
    start = np.clip(c - 8, 0, 48)
    inside = (c[None, :] >= start[:, None]) & (c[None, :] < start[:, None] + 16)
    mask_ = np.tile(np.where(inside, 0.0, NEG)[::-1], (2, 4)).astype(f)
    return tab, ret, rope_, mask_


def axial_order():
    one = np.concatenate([np.arange(0, 16), np.arange(32, 48), np.arange(16, 32), np.arange(48, 64)])
    return (np.arange(0, D, 64)[:, None] + one[None, :]).ravel()


def kernel(**inputs):
    import concourse.bacc as _bacc
    from concourse.bass_utils import run_bass_kernel_spmd as _run

    g = {k: np.asarray(v) for k, v in inputs.items()}
    w_in = g["w_in"][0]
    c = [w_in[:, 512 * k:512 * k + 512] for k in range(6)]
    w_in = np.concatenate([c[0], c[1], c[2], c[3], c[5], c[4]], axis=1)
    parts = [tiles_of(w_in), tiles_of(g["w_out"][0]),
             gate_up_tiles(g["w_ffn_gate"][0], g["w_ffn_up"][0]), down_tiles(g["w_ffn_down"][0]),
             g["w_ple_proj"][0].reshape(2, P, HALF, 256), tiles_of(g["w_ple_gate"][0])]
    for l in range(2):
        qkv = g["da_wqkv_2" if l == 0 else "na_wqkv_2"][0]
        q, k, v = qkv[:, :D], qkv[:, D:2 * D], qkv[:, 2 * D:]
        if l == 0:
            q, k = q[:, axial_order()], k[:, axial_order()]
        parts += [tiles_of(q), tiles_of(k), tiles_of(v), tiles_of(g["da_wo_2" if l == 0 else "na_wo_2"][0])]
        gu = g["ffn_w_gate_up_2"][l]
        parts += [gate_up_tiles(gu[:, :FF], gu[:, FF:]), down_tiles(g["ffn_w_down_2"][l])]
    wall = np.concatenate(parts)
    wada = g["ada_w_2"].transpose(0, 2, 1).reshape(2 * ADA_UNITS, P, D)
    col = lambda v: v.reshape(-1, P).T
    cond = np.stack([g["c_2"][0], g["c_ctx_2"]])
    conv_w = g["conv_dw_w"][0].T.reshape(CONV_T, P, CONV_W).transpose(1, 0, 2).reshape(P, -1)
    lam = np.concatenate([g["da_lambda_q1_2"][0], g["da_lambda_k1_2"][0], g["da_lambda_q2_2"][0], g["da_lambda_k2_2"][0]])
    vals = {"mix_pre": col(g["mix_pre_norm"][0]), "mix_post": col(g["mix_post_norm"][0]),
            "ffn_pre": col(g["ffn_pre_norm"][0]), "ffn_post": col(g["ffn_post_norm"][0]),
            "ple_post": col(g["ple_post_norm"][0]), "final": col(g["norm_final_2"]),
            "n_mix": col(g["norm_mix_2"].reshape(-1)), "n_ffn": col(g["norm_ffn_2"].reshape(-1)),
            "ada_b": col(g["ada_b_2"].reshape(-1)), "conv_w": conv_w, "conv_b": col(g["conv_dw_b"][0]),
            "ln_w": col(g["conv_ln_w"][0]), "ln_b": col(g["conv_ln_b"][0]),
            "subln": g["da_subln_2"][0].reshape(P, 1), "lam": np.broadcast_to(lam, (P, 256))}
    par = np.concatenate([vals[name] for name, _ in PCOLS], axis=1)
    tab, ret, rope_, mask_ = shape_tables()
    xin = feature_tiles(np.concatenate([g["x"][0], g["ctx_2"][0]], axis=0))
    arrays = {"wall": wall, "wada": wada, "cond": cond, "xin": xin, "pin": feature_tiles(g["p"][0, 0]), "par": par, "tab": tab, "tab_ret": ret,
              "tab_rope": rope_, "tab_mask": mask_, "rpb": g["na_rpb_2"][0]}
    nc = _bacc.Bacc("TRN2", target_bir_lowering=False, num_devices=1)
    args = []
    for name in arrays:
        a = arrays[name] = np.ascontiguousarray(arrays[name])
        args.append(nc.dram_tensor(name, a.shape, mybir.dt.from_np(a.dtype), kind="ExternalInput").ap())
    args.append(nc.dram_tensor("out_0", (P, KT, SEQ), F32, kind="ExternalOutput").ap())
    build(nc, *args)
    r = _run(nc, [arrays], core_ids=[0])
    got = r.results[0]["out_0"]
    return np.ascontiguousarray(got.transpose(2, 1, 0).reshape(1, SEQ, D))
```

```python
from contextlib import ExitStack

import numpy as np

import concourse.bass as bass
from concourse import mybir

F32 = mybir.dt.float32
F32R = mybir.dt.float32r
BF16 = mybir.dt.bfloat16
ALU = mybir.AluOpType
ACT = mybir.ActivationFunctionType
AX_X = mybir.AxisListType.X

P = 128
D = 1024
KT = D // P
SEQ = 256
NT = 2 * SEQ
FF = 2816
FT = FF // P
EPS = 1e-6
HALF = 4
SLOTS = 4
CONV_W = 31
CONV_T = 4
RET_H = 4
DA_H = 8
NA_H = 16
LAM_INIT = 0.2
NEG = -1.0e37

PHASES = [("in_u", 4), ("in_f", 6), ("in_v", 2), ("out", 4), ("gu", 22), ("dn", 12), ("pp", 1), ("pg", 4)]
for _l in range(2):
    PHASES += [(f"q{_l}", 4), (f"k{_l}", 4), (f"v{_l}", 4), (f"wo{_l}", 4), (f"gu{_l}", 22), (f"dn{_l}", 12)]


class Phase:

    def __init__(self, name, step0, steps, pair0):
        self.name, self.step0, self.steps, self.pair0 = name, step0, steps, pair0
        self.per_pair = 3 if name.startswith("dn") else 1
        self.body = 1 if name == "pp" else 2 * self.per_pair
        self.iters = steps // self.body
        self.pairs = 4 if name == "pp" else steps // self.per_pair


def plan():
    out, step, pair = {}, 0, 0
    for name, steps in PHASES:
        out[name] = ph = Phase(name, step, steps, pair)
        step += steps
        pair += ph.pairs
    return out, step


PH, STEPS = plan()
UNITS = 2 * STEPS
XL_COUNT = {"m0": 6 * KT, "f0": 8 * KT, "m1": 10 * KT, "f1": 11 * KT}
SUMMED = {"post1": "out", "fpost1": "dn", "ple1": "pg", "f0": "wo0", "m1": "dn0", "f1": "wo1", "final": "dn1"}
NORMS = ["pre1", "post1", "fpre1", "fpost1", "c0", "ple1", "m0", "f0", "m1", "f1", "final"]

PCOLS = [("mix_pre", KT), ("mix_post", KT), ("ffn_pre", KT), ("ffn_post", KT), ("ple_post", KT), ("final", KT),
         ("n_mix", 2 * KT), ("n_ffn", 2 * KT), ("ada_b", 96), ("conv_w", CONV_T * CONV_W), ("conv_b", CONV_T),
         ("ln_w", CONV_T), ("ln_b", CONV_T), ("subln", 1), ("lam", 256)]
PAT = {}
_at = 0
for _n, _w in PCOLS:
    PAT[_n] = (_at, _w)
    _at += _w
NPAR = _at
ADA_UNITS = 6 * D // P
ADA_SLOTS = 4
ADA_WOVEN = {"in_u": (3, 3, 0, 6)}
_at = 6
for _n, _per, _slots in (("out", 1, 2), ("gu", 1, 2), ("dn", 4, 4), ("pg", 2, 4), ("q0", 4, 4), ("k0", 3, 3), ("v0", 3, 3)):
    ADA_WOVEN[_n] = (_per, _slots, _at, _per * PH[_n].pairs)
    _at += _per * PH[_n].pairs
assert _at == 2 * ADA_UNITS and ADA_WOVEN["pg"][2] >= ADA_UNITS


def last_tenant(name, s):
    last = None
    for other, (_, slots, a0, units) in ADA_WOVEN.items():
        if other == name:
            return last
        if s < slots:
            last = max(a for a in range(a0, a0 + units) if (a - a0) % slots == s)


def slot_tenants(name, s):
    n = 0
    for other, (_, slots, _, units) in ADA_WOVEN.items():
        if other == name:
            return n
        n += units // slots if s < slots else 0


def build(nc, wall, wada, cond, xin, pin, par, tab, tab_ret, tab_rope, tab_mask, rpb, out):
    with ExitStack() as ctx:
        sems = {}

        def S(name):
            if name not in sems:
                sems[name] = ctx.enter_context(nc.semaphore(name))
            return sems[name]

        base = nc.sbuf_base
        base = (base + 31) // 32 * 32
        limit = nc.sbuf_usable_end
        arena_bytes = (limit - base) // 32 * 32
        ctx.enter_context(nc.sbuf_tensor("arena", [P, arena_bytes // 4], F32))
        cursor = [base]

        def at(name, shape, offset, dt=F32):
            size = 4 * int(np.prod(shape[1:]))
            assert offset + size <= base + arena_bytes, (name, offset + size - base - arena_bytes)
            return nc.alloc_sbuf_tensor_at(name, shape, dt, offset=offset)

        def sb(name, shape, dt=F32):
            o = cursor[0]
            cursor[0] = (o + 4 * int(np.prod(shape[1:])) + 31) // 32 * 32
            return at(name, shape, o, dt)

        class Region:

            def __init__(self, offset, size):
                self.o, self.end = offset, offset + size

            def take(self, name, shape, dt=F32):
                o = self.o
                self.o = (o + 4 * int(np.prod(shape[1:])) + 31) // 32 * 32
                assert self.o <= self.end, (name, self.o - self.end)
                return at(name, shape, o, dt)

        h = sb("h", [P, KT, NT])
        xs_at = cursor[0]
        xh = sb("xh", [P, KT, NT], F32R)
        xl = sb("xl", [P, KT, NT], F32R)
        y = sb("y", [P, KT, NT])
        y_at = cursor[0] - 4 * KT * NT
        raw = sb("raw", [P, SLOTS, HALF, 256])
        wh = sb("wh", [P, SLOTS, HALF, 256], F32R)
        wl = sb("wl", [P, SLOTS, HALF, 256], F32R)
        rstd = sb("rstd", [P, NT])
        prm = sb("prm", [P, NPAR])
        ones = sb("ones", [P, P])
        ident = sb("ident", [P, P])
        mod = sb("mod", [P, 2, 48, 2])
        gsc = sb("gsc", [P, 2, 2, KT, 2])
        lam4 = sb("lam4", [P, 8])
        eps = sb("eps", [P, 1])
        idle = sb("idle", [P, 1])
        big_at = cursor[0]
        BIG = 4 * FT * NT * 2
        assert big_at + BIG <= base + arena_bytes, big_at + BIG - base - arena_bytes

        sq = at("sq", [P, KT, NT], xs_at)
        fh = {SEQ: at("fh1", [P, FT, SEQ], big_at, F32R), NT: at("fh2", [P, FT, NT], big_at, F32R)}
        fl = {SEQ: at("fl1", [P, FT, SEQ], big_at + 4 * FT * SEQ, F32R),
              NT: at("fl2", [P, FT, NT], big_at + 4 * FT * NT, F32R)}
        sil = at("sil", [P, 2, NT], y_at)
        ft = at("ft", [P, 2, NT], y_at + 8 * NT)

        r = Region(big_at, BIG)
        u = r.take("u", [P, 16, SEQ])
        vb = r.take("vb", [P, 2, 512])
        up = r.take("up", [P, CONV_T, CONV_W - 1 + SEQ])
        cy = r.take("cy", [P, CONV_T, SEQ])
        sw = r.take("sw", [P, 8, SEQ])
        st = r.take("st", [P, RET_H, 384])
        on = r.take("on", [P, 2, RET_H, P])
        dt_ = r.take("dt_", [P, RET_H, 384])
        rcs = r.take("rcs", [P, 2, SEQ])
        ssq = r.take("ssq", [P, 8])
        csb = at("csb", [P, 2, D], big_at + BIG - 4 * D * (ADA_SLOTS + 2))
        ada = at("ada", [P, ADA_SLOTS, D], big_at + BIG - 4 * D * ADA_SLOTS)
        unread = nc.alloc_sbuf_tensor_at("unread", [P, D], BF16, offset=big_at + BIG - 4 * D * (ADA_SLOTS + 2) - 2 * D)
        assert r.o <= big_at + BIG - 4 * D * (ADA_SLOTS + 2) - 2 * D
        mix = at("mix", [P, KT, SEQ], y_at)
        r = Region(big_at, BIG)
        ptf = r.take("ptf", [P, 2, SEQ])
        pth = r.take("pth", [P, 2, SEQ], F32R)
        ptl = r.take("ptl", [P, 2, SEQ], F32R)
        ppo = r.take("ppo", [P, KT, SEQ])
        r = Region(big_at, BIG)
        qk = r.take("qk", [P, 2, KT, NT])
        vv = r.take("vv", [P, 4, D])
        rope = r.take("rope", [P, 2, SEQ])
        qkr = r.take("qkr", [P, 2, 2, NT])
        rtmp = r.take("rtmp", [P, 2, 2, SEQ])
        e2 = r.take("e2", [P, 2, 2, 512])
        pt = r.take("pt", [P, 2, 4, P])
        sm = r.take("sm", [P, 6, 16])
        osq = r.take("osq", [P, 2, P])
        ort = r.take("ort", [P, 4, DA_H])
        sww = at("sww", [P, 2, KT, SEQ], y_at)
        r = Region(big_at, BIG)
        q1 = r.take("q1", [P, KT, SEQ])
        k1 = r.take("k1", [P, KT, NT])
        v1 = r.take("v1", [P, 4, D])
        bias = r.take("bias", [P, 2, NA_H, SEQ])
        e1 = r.take("e1", [P, 2, 512])
        pt1 = r.take("pt1", [P, 2, 4, P])
        sm1 = r.take("sm1", [P, 8, 8])
        qks = r.take("qks", [P, 2, SEQ + NT])
        o1 = at("o1", [P, 2, D], y_at)
        mask = at("mask", [P, SEQ], y_at + 12 * D)

        ps = ctx.enter_context(nc.psum_tensor("ps", [P, 8, 512], F32))

        landed = [S(f"landed{k}") for k in range(SLOTS)]
        hi_ready, lo_ready = S("hi_ready"), S("lo_ready")
        units_done = S("units_done")
        ada_landed = [S(f"ada_landed{k}") for k in range(ADA_SLOTS)]
        ada_used = S("ada_used")
        bank_free = S("bank_free")

        def par_ap(name, a=0, n=None):
            o, w = PAT[name]
            n = w - a if n is None else n
            return prm[:, o + a:o + a + n]

        def run(eng, ph, body, peel=0):
            if ph.iters - peel > 1:
                with eng.Fori(0, ph.iters - peel) as i:
                    body(i)
            elif ph.iters - peel == 1:
                body(0)
            for i in range(ph.iters - peel, ph.iters):
                body(i)

        def pair_done(eng, ph, i, pair):
            eng.wait_ge(units_done, i * (2 * ph.body) + (2 * ph.step0 + 2 * ph.per_pair * (pair + 1) + SLOTS))

        def steps(eng, iters, per, depth, step):
            for w in range(per):
                step(0, w)
            with eng.Fori(1, iters) as i:
                for w in range(per):
                    step(i, w)
            for w in range(depth):
                step(iters, w)

        def live(i, w, iters, per):
            return not isinstance(i, int) or 0 <= i * per + w < iters * per

        def square_sums(name, n):
            if n == SEQ:
                return sq[:, 0:2, SEQ:NT], sq[:, 2, SEQ:NT]
            home = sq if name == "m1" else y
            return home[:, 0:2, :], home[:, 2, :]

        def settled(eng):
            eng.wait_ge(S("x_in"), 16)

        class Link:

            def __init__(self, eng, name):
                self.eng, self.sem, self.n, self.off = eng, S(name), 0, 0

            def __call__(self, ins):
                self.n += 1
                ins.then_inc(self.sem, 1)
                self.eng.wait_ge(self.sem, self.off + self.n)

            def steps(self, iters, per, depth, links, step):

                def counted(i, w):
                    if not isinstance(i, int):
                        if w == 0:
                            self.n0, self.n = self.n, 0
                        self.off = i * links + (self.n0 - links)
                    step(i, w)
                    if not isinstance(i, int) and w == per - 1:
                        assert self.n == links, (self.n, links)
                        self.n, self.off = self.n0 + links * (iters - 1), 0

                steps(self.eng, iters, per, depth, counted)

        block = ctx.enter_context(nc.Block())

        @block.sync
        def _(sp):
            def load(u_, slot):
                sp.wait_ge(lo_ready, u_ + 1)
                sp.dma_start(raw[:, slot, :, :], wall[u_, :, :, :]).then_inc(landed[slot], 16)

            def load_ada(name, i, s):
                per, slots, a0, _ = ADA_WOVEN[name]
                n = 2 * per
                if s < slots and last_tenant(name, s) is not None:
                    sp.wait_ge(ada_used, last_tenant(name, s) + 1 + ADA_SLOTS)
                sp.wait_ge(ada_used, i * n + (a0 + s + 1 + ADA_SLOTS - slots))
                sp.dma_start(ada[:, s % slots, :], wada[i * n + (a0 + s), :, :]).then_inc(ada_landed[s % slots], 16)

            def stream(u0, u1, name=None):
                n = SLOTS if name is None else 4 * PH[name].per_pair
                a = 0 if name is None else 2 * ADA_WOVEN[name][0]
                if u1 - u0 >= n:
                    with sp.Fori(0, (u1 - u0) // n) as i:
                        for s in range(n):
                            load(i * n + (u0 + s), (u0 + s) % SLOTS)
                            for s_ in range(s * a // n, (s + 1) * a // n):
                                load_ada(name, i, s_)
                for u_ in range(u0 + (u1 - u0) // n * n, u1):
                    load(u_, u_ % SLOTS)

            sp.dma_start(h[:, :, 0:SEQ], xin[:, :, 0:SEQ]).then_inc(S("x_in"), 16)
            sp.dma_start(csb[:], bass.AP(cond.tensor, 0, [[0, P], [D, 2], [1, D]])).then_inc(S("cond_in"), 16)
            for s in range(2):
                load(s, s)
            sp.dma_start(prm[:], par).then_inc(S("prm_in"), 16)
            sp.dma_start(ident[:], tab).then_inc(S("tab_in"), 16)
            sp.dma_start(dt_[:], tab_ret[:, 0:RET_H * 384].rearrange("p (a b) -> p a b", a=RET_H))\
                .then_inc(S("ret_in"), 16)
            sp.dma_start(rcs[:], tab_ret[:, RET_H * 384:].rearrange("p (a b) -> p a b", a=2))\
                .then_inc(S("ret_in"), 16)
            for u_ in range(2, 2 * PH["in_u"].steps):
                load(u_, u_ % SLOTS)
                if u_ >= 2:
                    load_ada("in_u", 0, u_ - 2)
            sp.dma_start(h[:, :, SEQ:NT], xin[:, :, SEQ:NT]).then_inc(S("ctx_in"), 16)
            at_ = 2 * PH["in_u"].steps
            for name in list(ADA_WOVEN)[1:]:
                if at_ < 2 * PH[name].step0:
                    stream(at_, 2 * PH[name].step0)
                at_ = 2 * (PH[name].step0 + PH[name].steps)
                stream(2 * PH[name].step0, at_, name)
            stream(at_, UNITS)
            for k in range(0, KT, 4):
                sp.wait_ge(S("final_ready"), k + 4)
                sp.dma_start(out[:, k:k + 4, :], y[:, k:k + 4, 0:SEQ]).then_inc(S("stored"), 16)
            sp.wait_ge(S("stored"), 32)

        @block.gpsimd
        def _(pool):
            def low(u_, slot):
                pool.wait_ge(hi_ready, u_ + 1)
                nc.gpsimd.tensor_tensor(wl[:, slot, :, :], raw[:, slot, :, :], wh[:, slot, :, :].bitcast(F32),
                                        ALU.subtract).then_inc(lo_ready, 1)

            pool.sem_inc(lo_ready, SLOTS)
            nc.gpsimd.memset(eps[:], EPS).then_inc(S("consts"), 1)
            nc.gpsimd.memset(ones[:], 1.0).then_inc(S("consts"), 1)

            def lows(u0, u1):
                with pool.Fori(0, (u1 - u0) // SLOTS) as i:
                    for s in range(SLOTS):
                        low(i * SLOTS + (u0 + s), (u0 + s) % SLOTS)
                for u_ in range(u0 + (u1 - u0) // SLOTS * SLOTS, u1):
                    low(u_, u_ % SLOTS)

            ends = [2 * PH[f"wo{l}"].step0 for l in range(2)]
            first = 2 * PH["out"].step0
            lows(0, first)
            pool.wait_ge(S("ret_swap"), 32)
            pool.wait_ge(S("ret_in"), 32)
            for part, tiles in enumerate((slice(0, 4), slice(4, 6))):
                w = tiles.stop - tiles.start
                at_u = u[:, 4 + tiles.start:4 + tiles.stop, :]
                nc.gpsimd.tensor_tensor(sw[:, tiles, :], sw[:, tiles, :], rcs[:, 1:2, :].to_broadcast([P, w, SEQ]), ALU.mult)
                nc.gpsimd.tensor_tensor(at_u, at_u, rcs[:, 0:1, :].to_broadcast([P, w, SEQ]), ALU.mult)\
                    .then_inc(S("ret_mul"), 1)
                pool.wait_ge(S("ret_mul"), part + 1)
                nc.gpsimd.tensor_tensor(at_u, at_u, sw[:, tiles, :], ALU.add).then_inc(S("ret_roped"), 1)
            lows(first, ends[0])
            pool.wait_ge(S("rope_in"), 16)
            pool.wait_ge(S("swap_in"), 8 * 16)
            pool.wait_ge(bank_free, PH["v0"].pair0 + 2)
            with pool.Fori(0, DA_H // 2) as i:
                for hh in range(2):
                    pool.wait_ge(S("s_ready"), i * 6 + (3 * hh + 3))
                    hd = bass.ds(i * 2 + hh, 1)
                    nc.gpsimd.tensor_tensor(rtmp[:, hh, :, :], sww[:, :, hd, :].rearrange("p m a b -> p m (a b)"),
                                            rope[:, 1:2, :].to_broadcast([P, 2, SEQ]), ALU.mult)
                    nc.gpsimd.tensor_tensor(qkr[:, hh, :, 0:SEQ], qk[:, :, hd, 0:SEQ].rearrange("p m a b -> p m (a b)"),
                                            rope[:, 0:1, :].to_broadcast([P, 2, SEQ]), ALU.mult).then_inc(S("rope_mul"), 1)
                    pool.wait_ge(S("rope_mul"), i * 2 + (hh + 1))
                    nc.gpsimd.tensor_tensor(qkr[:, hh, :, 0:SEQ], qkr[:, hh, :, 0:SEQ], rtmp[:, hh, :, :], ALU.add)
                    nc.gpsimd.tensor_copy(qkr[:, hh, :, SEQ:NT], qk[:, :, hd, SEQ:NT].rearrange("p m a b -> p m (a b)"))\
                        .then_inc(S("qkr_ready"), 1)
            lows(ends[0], ends[1])
            pool.wait_ge(bank_free, PH["v1"].pair0 + 2)
            with pool.Fori(0, KT // 2) as i:
                for b in range(2):
                    pool.wait_ge(S("ns_ready"), i * 8 + (4 * b + 4))
                    kt = bass.ds(i * 2 + b, 1)
                    nc.gpsimd.tensor_copy(qks[:, b, 0:SEQ], q1[:, kt, :].rearrange("p a b -> p (a b)"))
                    nc.gpsimd.tensor_copy(qks[:, b, SEQ:], k1[:, kt, :].rearrange("p a b -> p (a b)")).then_inc(S("qks_ready"), 1)
            lows(ends[1], UNITS)

        @block.scalar
        def _(act):
            def high(u_, n, slot):
                act.wait_ge(landed[slot], n * 16)
                act.wait_ge(units_done, u_ + 1)
                nc.scalar.activation(wh[:, slot, :, :], raw[:, slot, :, :], ACT.Copy).then_inc(hi_ready, 1)

            def high_step(ph, i, j):
                for half in range(2):
                    c = 2 * (ph.step0 + j + 1) + half
                    if isinstance(i, int) and c + 2 * ph.body * i >= UNITS:
                        return
                    high(i * (2 * ph.body) + c, i * (2 * ph.body // SLOTS) + (c // SLOTS + 1), c % SLOTS)

            def stream_only(ph, peel=0):
                def body(i):
                    for j in range(ph.body):
                        high_step(ph, i, j)
                run(act, ph, body, peel)

            preloads = [0]

            def preload(func):
                if preloads[0]:
                    act.wait_ge(S("preloaded"), preloads[0])
                nc.scalar.activation(idle[:], eps[:], func).then_inc(S("preloaded"), 1)
                preloads[0] += 1

            def root(name, n, t0=0):
                preload(ACT.Sqrt)
                act.wait_ge(S("sum_ready"), NORMS.index(name) + 1)
                nc.scalar.activation(rstd[:, t0:n], ps[:, 4, t0:n], ACT.Sqrt, scale=1.0 / D, bias=eps[:, 0:1])\
                    .then_inc(S("root_ready"), 1)

            def norm(name, src, n, h_count=None, t0=0):
                for k in range(KT):
                    if h_count is not None:
                        act.wait_ge(S("h_ready"), h_count + k + 1)
                    nc.scalar.activation(sq[:, k, t0:n], src[:, k, t0:n], ACT.Square).then_inc(S("sq_ready"), 1)
                root(name, n, t0)

            def split(sem, count0, src, n, scale=None):
                for k in range(KT):
                    act.wait_ge(S(sem), count0 + k + 1)
                    nc.scalar.activation(xh[:, k, 0:n], src[:, k, 0:n], ACT.Copy,
                                         scale=1.0 if scale is None else scale[:, k:k + 1]).then_inc(S("xh_ready"), 1)

            def split_shifted(count0, l, shift, n):
                for k in range(KT):
                    act.wait_ge(S("xr_ready"), count0 + k + 1)
                    for c in range(n // SEQ):
                        t = slice(c * SEQ, c * SEQ + SEQ)
                        nc.scalar.activation(xh[:, k, t], y[:, k, t], ACT.Identity,
                                             bias=mod[:, l, 8 * shift + k, c:c + 1]).then_inc(S("xh_ready"), 1)

            for name in ("ne_ready", "osq_done"):
                act.sem_inc(S(name), 2)

            act.wait_ge(S("x_in"), 16)
            for k in range(KT):
                nc.scalar.activation(sq[:, k, 0:SEQ], h[:, k, 0:SEQ], ACT.Square).then_inc(S("sq_ready"), 1)
            act.wait_ge(S("cond_in"), 16)
            nc.scalar.activation(csb[:], csb[:], ACT.Silu).then_inc(S("cond_ready"), 1)
            act.wait_ge(S("consts"), 2)
            root("pre1", SEQ)
            for u_ in range(2):
                high(u_, 1, u_)
            split("xr_ready", 0, y, SEQ, par_ap("mix_pre"))
            def take(ph, i, j, dst, src, func):
                pair_done(act, ph, i, j)
                act.wait_ge(bank_free, i * 2 + (ph.pair0 + j + 2))
                settled(act)
                nc.scalar.activation(dst, src, func).then_inc(bank_free, 1)

            for j in range(2):
                high_step(PH["in_u"], 0, j)
                if j == 0:
                    preload(ACT.Sigmoid)
                take(PH["in_u"], 0, j, u[:, 2 * j:2 * j + 2, :], ps[:, 2 * j:2 * j + 2, 0:SEQ], ACT.Sigmoid)
            for j in range(2):
                high_step(PH["in_u"], 1, j)

            def take_qkg(i):
                gate = isinstance(i, int)
                if gate:
                    act.wait_ge(bank_free, PH["in_f"].pair0 + 4 + 2)
                    for half in range(2):
                        a, b = slice(64 * half, 64 * half + 64), slice(64 - 64 * half, 128 - 64 * half)
                        act.dma_start(sw[a, :, :], u[b, 4:12, :]).then_inc(S("ret_swap"), 16)
                for j in range(2):
                    high_step(PH["in_f"], i, j)
                    take(PH["in_f"], i, j, u[:, bass.ds(i * 4 + (2 * j + 4), 2), :], ps[:, 2 * j:2 * j + 2, 0:SEQ],
                         ACT.Silu if gate else ACT.Copy)

            run(act, PH["in_f"], take_qkg, peel=1)
            for j in range(2):
                high_step(PH["in_v"], 0, j)
                take(PH["in_v"], 0, j, vb[:, :, 256 * j:256 * j + 256],
                     ps[:, 2 * j:2 * j + 1, :].rearrange("p a (b c) -> p (a b) c", b=2), ACT.Copy)
            act.wait_ge(S("lam_dot"), 1)
            nc.scalar.activation(lam4[:, 2:4], lam4[:, 0:2], ACT.Exp).then_inc(S("lam_exp"), 1)
            preload(ACT.Sqrt)
            act.wait_ge(S("dev_ready"), 1)
            nc.scalar.activation(sq[:, 0:4, 0:SEQ], cy[:], ACT.Square).then_inc(S("dev_sq"), 1)
            act.wait_ge(S("ret_o"), 1)
            nc.scalar.activation(on[:], ps[:, 2:4, :].rearrange("p a (b c) -> p a b c", b=RET_H), ACT.Square)\
                .then_inc(S("ret_sq"), 1)
            act.wait_ge(S("ret_ssq"), 1)
            nc.scalar.activation(ssq[:], ssq[:], ACT.Sqrt, scale=1.0 / P, bias=eps[:, 0:1]).then_inc(S("ret_root"), 1)
            act.wait_ge(S("ln_sum"), 2)
            nc.scalar.activation(rstd[:, 0:SEQ], ps[:, 5, 0:SEQ], ACT.Sqrt, scale=1.0 / 512, bias=eps[:, 0:1])\
                .then_inc(S("ln_root"), 1)
            preload(ACT.Silu)
            act.wait_ge(S("ln_scaled"), 1)
            for c in range(CONV_T):
                nc.scalar.activation(mix[:, c, :], cy[:, c, :], ACT.Silu, scale=par_ap("ln_w", c, 1),
                                     bias=par_ap("ln_b", c, 1)).then_inc(S("mix_conv"), 1)
                act.wait_ge(S("mix_conv"), c + 1)
                nc.scalar.activation(xh[:, c, 0:SEQ], mix[:, c, :], ACT.Copy).then_inc(S("xh_ready"), 1)
            act.wait_ge(S("mix_ret"), 1)
            for c in range(CONV_T, KT):
                nc.scalar.activation(xh[:, c, 0:SEQ], mix[:, c, :], ACT.Copy).then_inc(S("xh_ready"), 1)
            stream_only(PH["out"])
            root("post1", SEQ)
            norm("fpre1", h, SEQ, 0)
            split("xr_ready", KT, y, SEQ, par_ap("ffn_pre"))

            def gate_up(ph, n, f0):
                def body(i):
                    for j in range(2):
                        high_step(ph, i, j)
                        pair_done(act, ph, i, j)
                        act.wait_ge(S("f_lo"), i * 2 + (f0 + j + 1))
                        nc.scalar.activation(sil[:, j, 0:n], ps[:, 2 * j, 0:n], ACT.Silu).then_inc(S("silu_ready"), 1)
                        act.wait_ge(bank_free, i * 2 + (ph.pair0 + j + 3))
                        settled(act)
                        nc.scalar.activation(fh[n][:, i * 2 + j, :], ft[:, j, 0:n], ACT.Copy).then_inc(S("f_hi"), 1)
                preload(ACT.Silu)
                run(act, ph, body)

            gate_up(PH["gu"], SEQ, 0)
            stream_only(PH["dn"])
            act.wait_ge(bank_free, PH["pp"].pair0 + 2)
            act.dma_start(ptf[:], pin).then_inc(S("p_in"), 16)
            root("fpost1", SEQ)
            act.wait_ge(S("ctx_in"), 16)
            norm("c0", h, NT, t0=SEQ)
            act.wait_ge(S("p_in"), 16)
            nc.scalar.activation(pth[:], ptf[:], ACT.Copy).then_inc(S("p_hi"), 1)
            high_step(PH["pp"], 0, 0)
            split("h_ready", KT, h, SEQ)

            def gate_e(i):
                ph = PH["pg"]
                for j in range(2):
                    high_step(ph, i, j)
                    pair_done(act, ph, i, j)
                    act.wait_ge(bank_free, i * 2 + (ph.pair0 + j + 1))
                    nc.scalar.activation(sil[:, j, :].rearrange("p (a b) -> p a b", a=2),
                                         ps[:, 2 * j:2 * j + 2, 0:SEQ], ACT.Sigmoid).then_inc(S("sigm_ready"), 1)
            preload(ACT.Sigmoid)
            run(act, PH["pg"], gate_e)
            root("ple1", SEQ)
            act.dma_start(rope[:], tab_rope).then_inc(S("rope_in"), 16)

            for l in range(2):
                if l == 0:
                    norm("m0", h, SEQ, 2 * KT)
                else:
                    root("m1", NT)
                split_shifted((2 + 2 * l) * KT, l, 0, NT)
                stream_only(PH[f"q{l}"])
                if l == 1:
                    act.wait_ge(S("xl_ready"), XL_COUNT["m1"])
                    act.dma_start(mask[:], tab_mask).then_inc(S("mask_in"), 16)
                    for t in range(2):
                        for rr in range(2):
                            row0 = 2 * t + rr
                            for kr in range(4):
                                src = bass.AP(rpb.tensor, (kr + 7 - row0) * 31 + 15 - 63, [[1, 64], [15 * 31, NA_H], [1, 64]])
                                act.dma_start(bias[64 * rr:64 * rr + 64, t, :, 64 * kr:64 * kr + 64], src)\
                                    .then_inc(S("bias_in"), 16)
                stream_only(PH[f"k{l}"])
                if l == 0:
                    act.wait_ge(bank_free, PH["v0"].pair0 + 2)
                    for b in range(4):
                        src, dst = slice(32 * b, 32 * b + 32), slice(32 * (b ^ 1), 32 * (b ^ 1) + 32)
                        for m in range(2):
                            act.dma_start(sww[dst, m, :, :], qk[src, m, :, 0:SEQ]).then_inc(S("swap_in"), 16)
                stream_only(PH[f"v{l}"])
                preload(ACT.Exp)
                if l == 0:
                    def exps(v, q, k3, r6):
                        act.wait_ge(S("pt_psum"), v + 1)
                        for m in range(2):
                            act.wait_ge(S("s_max"), v + 1)
                            for t in range(1 if k3 < 2 else 2):
                                c = slice(0, 512) if k3 < 2 else slice(t * 256, t * 256 + 256)
                                nc.scalar.activation(e2[:, q, m, c], ps[:, 2 * q + m, c], ACT.Exp, scale=0.125,
                                                     bias=sm[:, r6, 2 * t + m:2 * t + m + 1],
                                                     accum_out=sm[:, r6, 4 + 2 * t + m:5 + 2 * t + m])\
                                    .then_inc(S("e_ready"), 2 if k3 < 2 else 1)

                    def probs(v, q):
                        act.wait_ge(S("pt_psum"), v + 3)
                        act.wait_ge(S("pv_done"), v + 1)
                        nc.scalar.activation(pt[:, q, :, :], ps[:, 4 + q, :].rearrange("p (a b) -> p a b", a=4), ACT.Copy)\
                            .then_inc(S("pt_ready"), 1)

                    act.wait_ge(bank_free, PH["wo0"].pair0 + 2)
                    def take_o(v, head, q, k3, r6):
                        for t in range(1 if k3 < 2 else 2):
                            act.wait_ge(S("pv_done"), v + 3)
                            act.wait_ge(S("osq_done"), head * 4 + (k3 + t + 1))
                            settled(act)
                            nc.scalar.activation(osq[:, (k3 + t) % 2, :], ps[:, 6 + q, t * P:t * P + P], ACT.Square,
                                                 scale=sm[:, r6, 8 + 2 * t:9 + 2 * t],
                                                 accum_out=ort[:, k3 + t, bass.ds(head, 1)]).then_inc(S("osq_done"), 1)
                            settled(act)
                            ins = nc.scalar.activation(qk[:, 0, head, (k3 + t) * P:(k3 + t) * P + P], ps[:, 6 + q, t * P:t * P + P],
                                                       ACT.Copy, scale=sm[:, r6, 8 + 2 * t:9 + 2 * t])
                        ins.then_inc(S("o_taken"), 1)

                    def step(i, w):
                        if live(i, w - 4, DA_H // 2, 6):
                            u_ = w - 4
                            take_o(i * 6 + u_, i * 2 + u_ // 3, u_ % 2, u_ % 3, u_ % 6)
                        if live(i, w - 2, DA_H // 2, 6):
                            probs(i * 6 + (w - 2), w % 2)
                        if live(i, w, DA_H // 2, 6):
                            exps(i * 6 + w, w % 2, w % 3, w)

                    steps(act, DA_H // 2, 6, 4, step)
                    act.wait_ge(S("o_taken"), 2 + 3 * DA_H)
                    nc.scalar.activation(ort[:], ort[:], ACT.Sqrt, scale=1.0 / P, bias=eps[:, 0:1]).then_inc(S("da_root"), 1)
                    for t in range(4):
                        for b in range(2):
                            act.wait_ge(S("o_t"), 2 * t + b + 1)
                            nc.scalar.activation(xh[:, 4 * b:4 * b + 4, t * P:t * P + P],
                                                 ps[:, b + 2 * (t % 2), :].rearrange("p (a b) -> p a b", a=4), ACT.Copy,
                                                 scale=par_ap("subln")).then_inc(S("oh_ready"), 1)
                else:
                    def nprobs(v, q):
                        act.wait_ge(S("npt_psum"), v + 3)
                        act.wait_ge(S("npv_done"), v + 1)
                        nc.scalar.activation(pt1[:, q, :, :], ps[:, 4 + q, :].rearrange("p (a b) -> p a b", a=4), ACT.Copy)\
                            .then_inc(S("npt_ready"), 1)

                    act.wait_ge(bank_free, PH["wo1"].pair0 + 2)
                    def step(i, w):
                        if live(i, w - 2, KT // 2, 8):
                            nprobs(i * 8 + (w - 2), w % 2)
                        if live(i, w, KT // 2, 8):
                            q = w % 2
                            act.wait_ge(S("npt_psum"), i * 8 + (w + 1))
                            act.wait_ge(S("ns_max"), i * 8 + (w + 1))
                            nc.scalar.activation(e1[:, q, :], ps[:, q, :], ACT.Exp, bias=sm1[:, w, 1:2],
                                                 accum_out=sm1[:, w, 2:3]).then_inc(S("ne_ready"), 1)

                    steps(act, KT // 2, 8, 2, step)
                    for t in range(2):
                        for b in range(2):
                            act.wait_ge(S("no_t"), 2 * t + b + 1)
                            nc.scalar.activation(xh[:, 4 * b:4 * b + 4, t * P:t * P + P].rearrange("p a (r c) -> p a r c", c=64),
                                                 ps[:, b + 2 * t, :].rearrange("p (a r c) -> p a r c", a=4, c=64)[:, :, :, ::-1],
                                                 ACT.Copy)\
                                .then_inc(S("oh_ready"), 1)
                n = NT if l == 0 else SEQ
                stream_only(PH[f"wo{l}"])
                root(f"f{l}", n)
                split_shifted((3 + 2 * l) * KT, l, 3, n)
                gate_up(PH[f"gu{l}"], n, FT * (l + 1))
                stream_only(PH[f"dn{l}"], peel=l)
            root("final", SEQ)

        @block.tensor
        def _(pe):
            def unit_ready(ph, i, j, half):
                c = 2 * (ph.step0 + j) + half
                pe.wait_ge(lo_ready, i * (2 * ph.body) + (c + 1 + SLOTS))
                return c % SLOTS

            def banks_ready(ph, i, pair):
                pe.wait_ge(bank_free, i * 2 + (ph.pair0 + pair + 1))

            def three(o, wa, wb, xa, xb, start, stop):
                nc.tensor.matmul(o, wa, xa, start=start, stop=False)
                nc.tensor.matmul(o, wa, xb, start=False, stop=False)
                return nc.tensor.matmul(o, wb, xa, start=False, stop=stop)

            def features(ph, n, a=xh, b=xl, ktiles=KT, fresh=None):
                def body(i):
                    for j in range(ph.body):
                        pair = j // ph.per_pair
                        if j % ph.per_pair == 0:
                            banks_ready(ph, i, pair)
                        for half in range(2):
                            slot = unit_ready(ph, i, j, half)
                            k0 = 2 * HALF * (j % ph.per_pair) + HALF * half
                            for o in range(2):
                                c = slice(o * P, o * P + P)
                                for kk in range(min(HALF, ktiles - k0)):
                                    k = k0 + kk
                                    if fresh and o == 0 and pair == 0:
                                        sem, n0, each = fresh
                                        pe.wait_ge(S(sem), n0 + each * (k + 1))
                                    mm = three(ps[:, 2 * pair + o, 0:n], wh[:, slot, kk, c], wl[:, slot, kk, c],
                                               a[:, k, 0:n], b[:, k, 0:n], k == 0, k == ktiles - 1)
                            mm.then_inc(units_done, 1)
                run(pe, ph, body)

            def tokens(ph, tiles):
                def body(i):
                    for j in range(2):
                        banks_ready(ph, i, j)
                        for half in range(2):
                            slot = unit_ready(ph, i, j, half)
                            for t in range(tiles):
                                o = ps[:, 2 * j + t // 2, (t % 2) * 256:(t % 2) * 256 + 256]
                                for kk in range(HALF):
                                    k = HALF * half + kk
                                    xa, xb = xh[:, k, t * P:t * P + P], xl[:, k, t * P:t * P + P]
                                    s0, s1_ = k == 0 and t % 2 == 0, k == KT - 1
                                    nc.tensor.matmul(o, xa, wh[:, slot, kk, :], start=s0, stop=False, skip_group_check=True)
                                    nc.tensor.matmul(o, xb, wh[:, slot, kk, :], start=False, stop=False, skip_group_check=True)
                                    mm = nc.tensor.matmul(o, xa, wl[:, slot, kk, :], start=False, stop=s1_,
                                                          skip_group_check=True)
                            mm.then_inc(units_done, 1)
                run(pe, ph, body)

            def norm_sum(name, n, t0=0):
                m = NORMS.index(name)
                if m:
                    pe.wait_ge(S("root_ready"), m)
                if name in SUMMED:
                    pe.wait_ge(S("acc_ready"), 9 * list(SUMMED).index(name) + 9)
                    mm = nc.tensor.matmul(ps[:, 4, 0:n], ones[:], square_sums(name, n)[1], start=True, stop=True)
                else:
                    tiles = sum(KT for other in NORMS[:m] if other not in SUMMED)
                    for k in range(KT):
                        pe.wait_ge(S("sq_ready"), tiles + k + 1)
                        mm = nc.tensor.matmul(ps[:, 4, t0:n], ones[:], sq[:, k, t0:n], start=k == 0, stop=k == KT - 1)
                mm.then_inc(S("sum_ready"), 1)

            pe.sem_inc(units_done, SLOTS)
            for name, n in (("s_ready", 6), ("pt_psum", 2), ("pv_done", 2), ("ns_ready", 8),
                            ("npt_psum", 2), ("npv_done", 2)):
                pe.sem_inc(S(name), n)
            pe.wait_ge(S("consts"), 2)

            norm_sum("pre1", SEQ)
            features(PH["in_u"], SEQ, fresh=("xl_ready", 0, 1))
            features(PH["in_f"], SEQ)
            tokens(PH["in_v"], 2)
            pe.wait_ge(S("tab_in"), 16)
            pe.wait_ge(S("ret_roped"), 2)
            pe.wait_ge(bank_free, PH["out"].pair0 + 2)
            for hd in range(RET_H):
                b = hd % 2
                if hd >= 2:
                    pe.wait_ge(S("ret_k_roped"), 1)
                    pe.wait_ge(S("ret_s"), hd - 1)
                q_, k_ = u[:, 4 + hd, :], u[:, 8 + hd, :]
                nc.tensor.matmul(ps[:, b, 0:256], k_[:, 0:P], q_, start=True, stop=True)
                nc.tensor.matmul(ps[:, b, 256:384], k_[:, P:256], q_[:, P:256], start=True, stop=True)\
                    .then_inc(S("ret_sc"), 1)
            pe.wait_ge(S("conv_tap"), CONV_T * CONV_W)
            for c in range(CONV_T):
                mm = nc.tensor.matmul(ps[:, 4, 0:SEQ], ones[:], cy[:, c, :], start=c == 0, stop=c == CONV_T - 1)
            mm.then_inc(S("ln_sum"), 1)
            for hd in range(RET_H):
                pe.wait_ge(S("ret_s"), hd + 1)
                c = slice(hd * P, hd * P + P)
                nc.tensor.matmul(ps[:, 2, c], st[:, hd, 0:P], vb[:, 0, c], start=True, stop=True)
                nc.tensor.matmul(ps[:, 3, c], st[:, hd, P:256], vb[:, 0, c], start=True, stop=False)
                mm = nc.tensor.matmul(ps[:, 3, c], st[:, hd, 256:384], vb[:, 1, c], start=False, stop=True)
            mm.then_inc(S("ret_o"), 1)
            pe.wait_ge(S("dev_sq"), 1)
            for c in range(CONV_T):
                mm = nc.tensor.matmul(ps[:, 5, 0:SEQ], ones[:], sq[:, c, 0:SEQ], start=c == 0, stop=c == CONV_T - 1)
            mm.then_inc(S("ln_sum"), 1)
            pe.wait_ge(S("ret_on"), 1)
            for hd in range(RET_H):
                for t in range(2):
                    mm = nc.tensor.transpose(ps[:, hd // 2, (hd % 2) * 256 + t * P:(hd % 2) * 256 + t * P + P],
                                             on[:, t, hd, :], ident[:])
            mm.then_inc(S("ret_t"), 1)
            features(PH["out"], SEQ, fresh=("xl_ready", KT, 1))
            norm_sum("post1", SEQ)
            norm_sum("fpre1", SEQ)
            features(PH["gu"], SEQ, fresh=("xl_ready", 2 * KT, 1))
            features(PH["dn"], SEQ, fh[SEQ], fl[SEQ], FT, fresh=("f_lo", 2, 1))
            norm_sum("fpost1", SEQ)
            norm_sum("c0", NT, SEQ)
            ph = PH["pp"]
            pe.wait_ge(S("p_lo"), 1)
            slots = [unit_ready(ph, 0, 0, half) for half in range(2)]
            flat = [(wh[:, s, :, :].rearrange("p a b -> p (a b)"), wl[:, s, :, :].rearrange("p a b -> p (a b)")) for s in slots]
            for pair in range(4):
                pe.wait_ge(bank_free, ph.pair0 + pair + 1)
                for o in range(2 * pair, 2 * pair + 2):
                    for k in range(2):
                        mm = three(ps[:, 2 * (pair % 2) + o % 2, 0:SEQ], flat[k][0][:, o * P:o * P + P],
                                   flat[k][1][:, o * P:o * P + P], pth[:, k, :], ptl[:, k, :], k == 0, k == 1)
                if pair < 3:
                    mm.then_inc(S("pp_ready"), 1)
            mm.then_inc(units_done, 2)
            features(PH["pg"], SEQ, fresh=("xl_ready", 3 * KT, 1))
            norm_sum("ple1", SEQ)

            for l in range(2):
                n = NT if l == 0 else SEQ
                norm_sum(f"m{l}", NT if l else SEQ)
                features(PH[f"q{l}"], n, fresh=("xl_ready", XL_COUNT[f"m{l}"] - 2 * KT, 2))
                features(PH[f"k{l}"], NT)
                tokens(PH[f"v{l}"], 4)
                pe.wait_ge(bank_free, PH[f"wo{l}"].pair0 + 2)
                if l == 0:
                    def scores(v, hh, k3, q):
                        pe.wait_ge(S("e_ready"), v * 4 + 4)
                        for m in range(2):
                            rows = slice(64 * m, 64 * m + 64)
                            if k3 < 2:
                                mm = nc.tensor.matmul(ps[:, 2 * q + m, :], qkr[rows, hh, 0, k3 * P:k3 * P + P],
                                                      qkr[rows, hh, 1, :], start=True, stop=True)
                            else:
                                for t in range(2):
                                    mm = nc.tensor.matmul(ps[:, 2 * q + m, t * 256:t * 256 + 256],
                                                          qkr[rows, hh, 0, SEQ + t * P:SEQ + t * P + P],
                                                          qkr[rows, hh, 1, SEQ:NT], start=True, stop=True)
                        mm.then_inc(S("s_ready"), 1)

                    def turn(v, q):
                        pe.wait_ge(S("p_ready"), v + 1)
                        pe.wait_ge(S("pt_ready"), v + 1)
                        for t in range(4):
                            mm = nc.tensor.transpose(ps[:, 4 + q, t * P:t * P + P], e2[:, q, 0, t * P:t * P + P], ident[:])
                        mm.then_inc(S("pt_psum"), 1)

                    def values(v, head, k3, q):
                        pe.wait_ge(S("pt_ready"), v + 3)
                        pe.wait_ge(S("o_taken"), v + 1)
                        for t in range(1 if k3 < 2 else 2):
                            for c in range(4 if k3 < 2 else 2):
                                mm = nc.tensor.matmul(ps[:, 6 + q, t * P:t * P + P], pt[:, q, 2 * t + c, :],
                                                      vv[:, c if k3 < 2 else 2 + c, bass.ds(head * P, P)], start=c == 0,
                                                      stop=c == (3 if k3 < 2 else 1))
                        mm.then_inc(S("pv_done"), 1)

                    def step(i, w):
                        if live(i, w, DA_H // 2, 6):
                            if w % 3 == 0:
                                pe.wait_ge(S("qkr_ready"), i * 2 + (w // 3 + 1))
                            scores(i * 6 + w, w // 3, w % 3, w % 2)
                        if live(i, w - 2, DA_H // 2, 6):
                            turn(i * 6 + (w - 2), w % 2)
                        if live(i, w - 3, DA_H // 2, 6):
                            values(i * 6 + (w - 3), i * 2 + (w - 3) // 3, w % 3, (w - 3) % 2)

                    steps(pe, DA_H // 2, 6, 3, step)
                    for t in range(4):
                        pe.wait_ge(S("da_scaled"), t + 1)
                        for b in range(2):
                            if t >= 2:
                                pe.wait_ge(S("ol_ready"), 2 * (t - 2) + b + 1)
                            for hd in range(4):
                                mm = nc.tensor.transpose(ps[:, b + 2 * (t % 2), hd * P:hd * P + P],
                                                         qk[:, 0, 4 * b + hd, t * P:t * P + P], ident[:])
                            mm.then_inc(S("o_t"), 1)
                    pe.wait_ge(S("ol_ready"), 8)
                else:
                    def nturn(v, q):
                        pe.wait_ge(S("ne_ready"), v + 3)
                        pe.wait_ge(S("npt_ready"), v + 1)
                        for c in range(4):
                            mm = nc.tensor.transpose(ps[:, 4 + q, c * P:c * P + P], e1[:, q, c * P:c * P + P], ident[:])
                        mm.then_inc(S("npt_psum"), 1)

                    def nvalues(v, tile, q):
                        pe.wait_ge(S("npt_ready"), v + 3)
                        pe.wait_ge(S("no_taken"), v + 1)
                        for c in range(4):
                            mm = nc.tensor.matmul(ps[:, 6 + q, 0:P], pt1[:, q, c, :],
                                                  v1[:, c, bass.ds(tile * P, P)], start=c == 0, stop=c == 3)
                        mm.then_inc(S("npv_done"), 1)

                    def step(i, w):
                        if live(i, w, KT // 2, 8):
                            hh, t, b, q = w // 2 % 2, w % 2, w // 4, w % 2
                            if w % 4 == 0:
                                pe.wait_ge(S("qks_ready"), i * 2 + (b + 1))
                            pe.wait_ge(S("ne_ready"), i * 8 + (w + 1))
                            rows = slice(64 * hh, 64 * hh + 64)
                            nc.tensor.matmul(ps[:, q, :], qks[rows, b, t * P:t * P + P], qks[rows, b, SEQ:],
                                             start=True, stop=True).then_inc(S("ns_ready"), 1)
                        if live(i, w - 2, KT // 2, 8):
                            nturn(i * 8 + (w - 2), w % 2)
                        if live(i, w - 3, KT // 2, 8):
                            nvalues(i * 8 + (w - 3), i * 2 + (w - 3) // 4, (w - 3) % 2)

                    steps(pe, KT // 2, 8, 3, step)
                    pe.wait_ge(S("no_taken"), 2 + 2 * NA_H)
                    for t in range(2):
                        for b in range(2):
                            for hd in range(4):
                                c = (4 * b + hd) * P
                                mm = nc.tensor.transpose(ps[:, b + 2 * t, hd * P:hd * P + P], o1[:, t, c:c + P], ident[:])
                            mm.then_inc(S("no_t"), 1)
                    pe.wait_ge(S("nol_ready"), 4)
                features(PH[f"wo{l}"], n)
                norm_sum(f"f{l}", n)
                features(PH[f"gu{l}"], n, fresh=("xl_ready", XL_COUNT[f"f{l}"] - n // SEQ * KT, n // SEQ))
                features(PH[f"dn{l}"], n, fh[n], fl[n], FT, fresh=("f_lo", 2 + FT * (l + 1), 1))
            norm_sum("final", SEQ)

        @block.vector
        def _(dve):
            link = Link(dve, "dve_link")
            V = nc.vector

            for name, n in (("ada_used", ADA_SLOTS), ("bank_free", 2), ("f_lo", 2), ("e_ready", 8), ("pt_ready", 2), ("o_taken", 2),
                            ("npt_ready", 2), ("no_taken", 2)):
                dve.sem_inc(S(name), n)
            V.memset(up[:, :, 0:CONV_W - 1], 0.0)
            dve.wait_ge(S("prm_in"), 16)
            for m in range(2):
                V.tensor_tensor(y[:, m, 0:64], par_ap("lam", 128 * m, 64), par_ap("lam", 128 * m + 64, 64), ALU.mult)\
                    .then_inc(S("lam_mul"), 1)
            dve.wait_ge(S("lam_mul"), 2)
            V.tensor_reduce(lam4[:, 0:2], y[:, 0:2, 0:64], AX_X, ALU.add).then_inc(S("lam_dot"), 1)


            xh_count = [0]

            def recip(name, n, t0=0):
                dve.wait_ge(S("root_ready"), NORMS.index(name) + 1)
                link(V.reciprocal(rstd[:, t0:n], rstd[:, t0:n]))

            def lagged(first, then, lag):
                for k in range(KT + lag):
                    if k < KT:
                        first(k)
                    if k >= lag:
                        then(k - lag)

            def scale_in(src, n, gain):
                def scaled(k):
                    V.tensor_tensor(y[:, k, 0:n], src[:, k, 0:n], rstd[:, 0:n], ALU.mult).then_inc(S("xr_ready"), 1)

                def low(k):
                    xh_count[0] += 1
                    dve.wait_ge(S("xh_ready"), xh_count[0])
                    V.scalar_tensor_tensor(xl[:, k, 0:n], y[:, k, 0:n], gain[:, k:k + 1], xh[:, k, 0:n].bitcast(F32),
                                           ALU.mult, ALU.subtract).then_inc(S("xl_ready"), 1)

                lagged(scaled, low, 2)

            def modulate(l, w, n):
                parts = [slice(c * SEQ, c * SEQ + SEQ) for c in range(n // SEQ)]

                def scaled(k):
                    for c, t in enumerate(parts):
                        ins = V.scalar_tensor_tensor(y[:, k, t], h[:, k, t], gsc[:, l, w, k, c:c + 1], rstd[:, t],
                                                     ALU.mult, ALU.mult)
                    ins.then_inc(S("xr_ready"), 1)

                def low(k):
                    for c, t in enumerate(parts):
                        xh_count[0] += 1
                        dve.wait_ge(S("xh_ready"), xh_count[0])
                        V.scalar_tensor_tensor(xl[:, k, t], y[:, k, t], mod[:, l, 24 * w + k, c:c + 1],
                                               xh[:, k, t].bitcast(F32), ALU.add, ALU.subtract).then_inc(S("xl_ready"), 1)

                lagged(scaled, low, 2)

            mod_flat = mod[:].rearrange("p l t c -> p (l t) c")

            def condition(ph, i, j):
                if ph.name not in ADA_WOVEN:
                    return
                per, slots, a0, _ = ADA_WOVEN[ph.name]
                for s in range(per * j, per * j + per):
                    dve.wait_ge(ada_landed[s % slots],
                                i * (16 * 2 * per // slots) + 16 * (slot_tenants(ph.name, s % slots) + s // slots + 1))
                    at_ = bass.ds(i * (2 * per) + (a0 + s), 1)
                    dve.wait_ge(ada_used, i * (2 * per) + (a0 + s + ADA_SLOTS))
                    V.scalar_tensor_tensor(unread[:], ada[:, s % slots, :], 1.0, csb[:, 0, :], ALU.mult, ALU.mult,
                                           accum_out=mod_flat[:, at_, 0]).then_inc(S("ada_half"), 1)
                    dve.wait_ge(S("ada_half"), i * (2 * per) + (a0 + s + 1))
                    ins = V.scalar_tensor_tensor(unread[:], ada[:, s % slots, :], 1.0, csb[:, 1, :], ALU.mult, ALU.mult,
                                                 accum_out=mod_flat[:, at_, 1])
                    ins.then_inc(ada_used, 1)

            def modulation(l):
                dve.wait_ge(ada_used, (l + 1) * ADA_UNITS + ADA_SLOTS)
                bias_ = par_ap("ada_b", l * ADA_UNITS, ADA_UNITS)
                link(V.tensor_tensor(mod[:, l, :, :], mod[:, l, :, :],
                                     bias_.unsqueeze(2).to_broadcast([P, ADA_UNITS, 2]), ALU.add))
                for w, name in enumerate(("n_mix", "n_ffn")):
                    V.scalar_tensor_tensor(gsc[:, l, w, :, :], mod[:, l, 8 + 24 * w:16 + 24 * w, :], 1.0,
                                           par_ap(name, l * KT, KT).unsqueeze(2).to_broadcast([P, KT, 2]),
                                           ALU.add, ALU.mult).then_inc(S("gsc_ready"), 1)
                dve.wait_ge(S("gsc_ready"), 2 * (l + 1))

            def low_of(src, n):
                for k in range(KT):
                    xh_count[0] += 1
                    dve.wait_ge(S("xh_ready"), xh_count[0])
                    V.tensor_tensor(xl[:, k, 0:n], src[:, k, 0:n], xh[:, k, 0:n].bitcast(F32), ALU.subtract)\
                        .then_inc(S("xl_ready"), 1)

            def add_normed(src, gain):
                def scaled(k):
                    V.scalar_tensor_tensor(src[:, k, 0:SEQ], src[:, k, 0:SEQ], gain[:, k:k + 1], rstd[:, 0:SEQ],
                                           ALU.mult, ALU.mult).then_inc(S("post_scaled"), 1)

                def add(k):
                    post[0] += 1
                    dve.wait_ge(S("post_scaled"), post[0])
                    V.tensor_tensor(h[:, k, 0:SEQ], h[:, k, 0:SEQ], src[:, k, 0:SEQ], ALU.add).then_inc(S("h_ready"), 1)

                lagged(scaled, add, 1)

            def clear_sums(name, n):
                if name is not None:
                    V.memset(square_sums(name, n)[1], 0.0).then_inc(S("acc_ready"), 1)

            def add_squares(name, n, ph, i, j, src):
                if name is None:
                    return
                m = list(SUMMED).index(name)
                new, acc = square_sums(name, n)
                dve.wait_ge(bank_free, i * 2 + (ph.pair0 + j + 3))
                dve.wait_ge(S("acc_ready"), i * 4 + (9 * m + 2 * j + 1))
                V.tensor_tensor(new, src, src, ALU.mult).then_inc(S("sq_new"), 1)
                dve.wait_ge(S("sq_new"), i * 2 + (4 * m + j + 1))
                V.tensor_tensor(acc, acc, new[:, 0, :], ALU.add).then_inc(S("acc_ready"), 1)
                dve.wait_ge(S("acc_ready"), i * 4 + (9 * m + 2 * j + 2))
                V.tensor_tensor(acc, acc, new[:, 1, :], ALU.add).then_inc(S("acc_ready"), 1)

            post = [0]

            def take(ph, n, dst, falling=False, norm=None, scale=1.0):
                def body(i):
                    for j in range(2):
                        condition(ph, i, j)
                        pair_done(dve, ph, i, j)
                        src, to = ps[:, 2 * j:2 * j + 2, 0:n], dst[:, bass.ds(i * 4 + 2 * j, 2), 0:n]
                        if falling:
                            src = src.rearrange("p a (r c) -> p a r c", c=64)[:, :, :, ::-1]
                            to = to.rearrange("p a (r c) -> p a r c", c=64)
                        V.tensor_scalar(to, src, scale, None, ALU.mult).then_inc(bank_free, 1)
                        add_squares(norm, n, ph, i, j, to)
                clear_sums(norm, n)
                run(dve, ph, body)

            def take_tokens(ph, tiles, dst):
                def body(i):
                    for j in range(2):
                        condition(ph, i, j)
                        pair_done(dve, ph, i, j)
                        V.tensor_scalar(dst[:, :, bass.ds(i * 512 + 256 * j, 256)],
                                        ps[:, 2 * j:2 * j + tiles // 2, :].rearrange("p a (b c) -> p (a b) c", b=2),
                                        1.0, None, ALU.mult).then_inc(bank_free, 1)
                run(dve, ph, body)

            def take_gated(ph, n, l, w, norm):
                def body(i):
                    for j in range(2):
                        pair_done(dve, ph, i, j)
                        for o in range(2):
                            for c in range(n // SEQ):
                                t = slice(c * SEQ, c * SEQ + SEQ)
                                k = i * 4 + (2 * j + o)
                                g = mod[:, l, bass.ds(i * 4 + (2 * j + o + 16 + 24 * w), 1), c:c + 1].rearrange("p a b -> p (a b)")
                                hk = h[:, bass.ds(k, 1), t].rearrange("p a b -> p (a b)")
                                ins = V.scalar_tensor_tensor(hk, ps[:, 2 * j + o, t], g, hk, ALU.mult, ALU.add)
                        ins.then_inc(bank_free, 1)
                        add_squares(norm, n, ph, i, j, h[:, bass.ds(i * 4 + 2 * j, 2), 0:n])
                clear_sums(norm, n)
                run(dve, ph, body)

            def gate_up(ph, n, f0):
                def body(i):
                    for j in range(2):
                        condition(ph, i, j)
                        dve.wait_ge(S("f_lo"), i * 2 + (f0 + j + 1))
                        dve.wait_ge(S("silu_ready"), i * 2 + (f0 + j + 1))
                        V.tensor_tensor(ft[:, j, 0:n], sil[:, j, 0:n], ps[:, 2 * j + 1, 0:n], ALU.mult).then_inc(bank_free, 1)
                        dve.wait_ge(S("f_hi"), i * 2 + (f0 + j + 1))
                        f1 = bass.ds(i * 2 + j, 1)
                        V.tensor_tensor(fl[n][:, f1, :].rearrange("p a b -> p (a b)"), ft[:, j, 0:n],
                                        fh[n][:, f1, :].rearrange("p a b -> p (a b)").bitcast(F32),
                                        ALU.subtract).then_inc(S("f_lo"), 1)
                run(dve, ph, body)

            recip("pre1", SEQ)
            scale_in(h, SEQ, par_ap("mix_pre"))
            dve.wait_ge(S("cond_ready"), 1)
            ph = PH["in_u"]
            for j in range(2):
                condition(ph, 0, j)
            for j in range(2):
                pair_done(dve, ph, 1, j)
                dve.wait_ge(bank_free, ph.pair0 + 4 + j)
                V.tensor_tensor(up[:, 2 * j:2 * j + 2, CONV_W - 1:], ps[:, 2 * j:2 * j + 2, 0:SEQ], u[:, 2 * j:2 * j + 2, :],
                                ALU.mult).then_inc(bank_free, 1)
            dve.wait_ge(bank_free, ph.pair0 + 4 + 2)
            for c in range(CONV_T):
                V.tensor_scalar(cy[:, c, :], up[:, c, 0:SEQ], par_ap("conv_w", c * CONV_W, 1), par_ap("conv_b", c, 1),
                                ALU.mult, ALU.add).then_inc(S("conv_tap"), 1)
            cw0 = PAT["conv_w"][0]
            with dve.Fori(1, CONV_W) as i:
                for c in range(CONV_T):
                    dve.wait_ge(S("conv_tap"), i * CONV_T + (c - CONV_T + 1))
                    V.scalar_tensor_tensor(cy[:, c, :], up[:, c, bass.ds(i, SEQ)], prm[:, bass.ds(i + (cw0 + c * CONV_W), 1)],
                                           cy[:, c, :], ALU.mult, ALU.add).then_inc(S("conv_tap"), 1)
            dve.wait_ge(S("conv_tap"), CONV_T * CONV_W)
            dve.wait_ge(S("ret_swap"), 32)
            dve.wait_ge(S("ret_in"), 32)
            V.tensor_tensor(u[:, 10:12, :], u[:, 10:12, :], rcs[:, 0:1, :].to_broadcast([P, 2, SEQ]), ALU.mult)
            link(V.tensor_tensor(sw[:, 6:8, :], sw[:, 6:8, :], rcs[:, 1:2, :].to_broadcast([P, 2, SEQ]), ALU.mult))
            V.tensor_tensor(u[:, 10:12, :], u[:, 10:12, :], sw[:, 6:8, :], ALU.add).then_inc(S("ret_k_roped"), 1)
            for hd in range(RET_H):
                dve.wait_ge(S("ret_sc"), hd + 1)
                V.tensor_tensor(st[:, hd, :], ps[:, hd % 2, 0:384], dt_[:, hd, :], ALU.mult).then_inc(S("ret_s"), 1)
            dve.wait_ge(S("ln_sum"), 1)
            for c in range(CONV_T):
                ins = V.scalar_tensor_tensor(cy[:, c, :], ps[:, 4, 0:SEQ], -1.0 / 512, cy[:, c, :], ALU.mult, ALU.add)
            ins.then_inc(S("dev_ready"), 1)
            dve.wait_ge(S("ret_sq"), 1)
            V.tensor_reduce(ssq[:], on[:].rearrange("p a b c -> p (a b) c"), AX_X, ALU.add).then_inc(S("ret_ssq"), 1)
            dve.wait_ge(S("ret_root"), 1)
            link(V.reciprocal(ssq[:], ssq[:]))
            V.tensor_tensor(on[:].rearrange("p a b c -> p (a b) c"),
                            ps[:, 2:4, :].rearrange("p a (b c) -> p (a b) c", c=P),
                            ssq[:].unsqueeze(2).to_broadcast([P, 8, P]), ALU.mult).then_inc(S("ret_on"), 1)
            dve.wait_ge(S("lam_exp"), 1)
            link(V.tensor_tensor(lam4[:, 4:5], lam4[:, 3:4], lam4[:, 2:3], ALU.subtract))
            link(V.tensor_scalar(lam4[:, 5:6], lam4[:, 4:5], -LAM_INIT, None, ALU.add))
            dve.wait_ge(S("dev_ready"), 1)
            dve.wait_ge(S("ln_root"), 1)
            link(V.reciprocal(rstd[:, 0:SEQ], rstd[:, 0:SEQ]))
            V.tensor_tensor(cy[:], cy[:], rstd[:, 0:SEQ].unsqueeze(1).to_broadcast([P, CONV_T, SEQ]), ALU.mult)\
                .then_inc(S("ln_scaled"), 1)
            dve.wait_ge(S("ret_t"), 1)
            V.tensor_tensor(mix[:, 4:8, :], ps[:, 0:2, :].rearrange("p a (b c) -> p (a b) c", b=2), u[:, 12:16, :], ALU.mult)\
                .then_inc(S("mix_ret"), 1)
            low_of(mix, SEQ)
            take(PH["out"], SEQ, y, norm="post1")
            recip("post1", SEQ)
            add_normed(y, par_ap("mix_post"))
            recip("fpre1", SEQ)
            scale_in(h, SEQ, par_ap("ffn_pre"))
            gate_up(PH["gu"], SEQ, 0)
            take(PH["dn"], SEQ, y, norm="fpost1")
            recip("fpost1", SEQ)
            add_normed(y, par_ap("ffn_post"))
            recip("c0", NT, SEQ)
            dve.wait_ge(S("p_hi"), 1)
            V.tensor_tensor(ptl[:], ptf[:], pth[:].bitcast(F32), ALU.subtract).then_inc(S("p_lo"), 1)
            low_of(h, SEQ)
            ph = PH["pp"]
            for pair in range(4):
                if pair < 3:
                    dve.wait_ge(S("pp_ready"), pair + 1)
                else:
                    dve.wait_ge(units_done, 2 * ph.step0 + 2 + SLOTS)
                b = 2 * (pair % 2)
                V.tensor_copy(ppo[:, 2 * pair:2 * pair + 2, :], ps[:, b:b + 2, 0:SEQ]).then_inc(bank_free, 1)

            def gated_e(i):
                ph = PH["pg"]
                for j in range(2):
                    condition(ph, i, j)
                    dve.wait_ge(S("sigm_ready"), i * 2 + (j + 1))
                    pp2 = ppo[:, bass.ds(i * 4 + 2 * j, 2), :]
                    V.tensor_tensor(pp2, pp2, sil[:, j, :].rearrange("p (a b) -> p a b", a=2), ALU.mult).then_inc(bank_free, 1)
                    add_squares("ple1", SEQ, ph, i, j, pp2)
            clear_sums("ple1", SEQ)
            run(dve, PH["pg"], gated_e)
            recip("ple1", SEQ)
            add_normed(ppo, par_ap("ple_post"))

            for l in range(2):
                n = NT if l == 0 else SEQ
                modulation(l)
                recip(f"m{l}", NT if l else SEQ)
                modulate(l, 0, NT)
                if l == 0:
                    take(PH["q0"], NT, qk[:, 0, :, :])
                    take(PH["k0"], NT, qk[:, 1, :, :])
                    take_tokens(PH["v0"], 4, vv)
                    dve.wait_ge(bank_free, PH["wo0"].pair0 + 2)

                    def maxima(v, q, k3, r6):
                        dve.wait_ge(S("s_ready"), v + 7)
                        src = ps[:, 2 * q:2 * q + 2, :]
                        if k3 < 2:
                            mx = sm[:, r6, 12:14]
                            link(V.tensor_reduce(mx, src, AX_X, ALU.max))
                            V.tensor_scalar(sm[:, r6, 0:2], mx, -0.125, None, ALU.mult).then_inc(S("s_max"), 1)
                        else:
                            mx = sm[:, r6, 12:16]
                            link(V.tensor_reduce(mx.rearrange("p (t m) -> p m t", m=2),
                                                 src.rearrange("p m (t c) -> p m t c", t=2), AX_X, ALU.max))
                            V.tensor_scalar(sm[:, r6, 0:4], mx, -0.125, None, ALU.mult).then_inc(S("s_max"), 1)

                    def combine(v, q, k3, r6):
                        dve.wait_ge(S("e_ready"), v * 4 + 12)
                        tiles = 1 if k3 < 2 else 2
                        sums = sm[:, r6, 4:4 + 2 * tiles].rearrange("p (t m) -> p t m", m=2)
                        inv = sm[:, r6, 8:8 + 2 * tiles].rearrange("p (t m) -> p t m", m=2)
                        link(V.reciprocal(inv, sums))
                        link(V.scalar_tensor_tensor(inv[:, :, 1], sums[:, :, 0], lam4[:, 5:6], inv[:, :, 1], ALU.mult, ALU.mult))
                        for t in range(tiles):
                            c = slice(0, 512) if k3 < 2 else slice(t * 256, t * 256 + 256)
                            ins = V.scalar_tensor_tensor(e2[:, q, 0, c], e2[:, q, 1, c], sm[:, r6, 9 + 2 * t:10 + 2 * t],
                                                         e2[:, q, 0, c], ALU.mult, ALU.add)
                        ins.then_inc(S("p_ready"), 1)

                    def step(i, w):
                        if live(i, w - 1, DA_H // 2, 6):
                            combine(i * 6 + (w - 1), (w - 1) % 2, (w - 1) % 3, (w - 1) % 6)
                        if live(i, w, DA_H // 2, 6):
                            maxima(i * 6 + w, w % 2, w % 3, w)

                    link.steps(DA_H // 2, 6, 1, 18, step)
                    dve.wait_ge(S("da_root"), 1)
                    link(V.reciprocal(ort[:], ort[:]))
                    link(V.tensor_scalar(ort[:], ort[:], 1.0 - LAM_INIT, None, ALU.mult))
                    for t in range(4):
                        o_ = qk[:, 0, :, t * P:t * P + P]
                        V.tensor_tensor(o_, o_, ort[:, t, :].unsqueeze(2).to_broadcast([P, DA_H, P]), ALU.mult)\
                            .then_inc(S("da_scaled"), 1)
                    for t in range(4):
                        for b in range(2):
                            dve.wait_ge(S("oh_ready"), 2 * t + b + 1)
                            x_ = (slice(None), slice(4 * b, 4 * b + 4), slice(t * P, t * P + P))
                            V.scalar_tensor_tensor(xl[x_], ps[:, b + 2 * (t % 2), :].rearrange("p (a b) -> p a b", a=4),
                                                   par_ap("subln"), xh[x_].bitcast(F32), ALU.mult, ALU.subtract)\
                                .then_inc(S("ol_ready"), 1)
                else:
                    take(PH["q1"], SEQ, q1, falling=True, scale=0.125)
                    take(PH["k1"], NT, k1)
                    dve.wait_ge(S("bias_in"), 16 * 16)
                    dve.wait_ge(S("mask_in"), 16)
                    for t in range(2):
                        V.tensor_tensor(bias[:, t, :, :], bias[:, t, :, :], mask[:].unsqueeze(1).to_broadcast([P, NA_H, SEQ]),
                                        ALU.add).then_inc(S("masked"), 1)
                    take_tokens(PH["v1"], 4, v1)
                    dve.wait_ge(S("masked"), 2)

                    def nmax(i, w):
                        q, t, r8 = w % 2, w % 2, w
                        dve.wait_ge(S("ns_ready"), i * 8 + (w + 9))
                        head = bass.ds(i * 4 + w // 2, 1)
                        link(V.tensor_tensor(ps[:, q, 0:SEQ], ps[:, q, 0:SEQ], bias[:, t, head, :].rearrange("p a b -> p (a b)"),
                                             ALU.add))
                        link(V.tensor_reduce(sm1[:, r8, 0:1], ps[:, q, :], AX_X, ALU.max))
                        V.tensor_scalar(sm1[:, r8, 1:2], sm1[:, r8, 0:1], -1.0, None, ALU.mult).then_inc(S("ns_max"), 1)

                    def ntake(i, w):
                        q, t, r8, hh = w % 2, w % 2, w % 8, w // 2 % 2
                        dve.wait_ge(S("npv_done"), i * 8 + (w + 3))
                        link(V.reciprocal(sm1[:, r8, 3:4], sm1[:, r8, 2:3]))
                        V.tensor_scalar(o1[:, t, bass.ds(i * 256 + (w // 2) * 64, 64)], ps[:, 6 + q, hh * 64:hh * 64 + 64], sm1[:, r8, 3:4], None,
                                        ALU.mult).then_inc(S("no_taken"), 1)

                    def step(i, w):
                        if live(i, w - 4, KT // 2, 8):
                            ntake(i, w - 4)
                        if live(i, w, KT // 2, 8):
                            nmax(i, w)

                    link.steps(KT // 2, 8, 4, 24, step)
                    for t in range(2):
                        for b in range(2):
                            dve.wait_ge(S("oh_ready"), 8 + 2 * t + b + 1)
                            x_ = (slice(None), slice(4 * b, 4 * b + 4), slice(t * P, t * P + P))
                            V.tensor_tensor(xl[x_].rearrange("p a (r c) -> p a r c", c=64),
                                            ps[:, b + 2 * t, :].rearrange("p (a r c) -> p a r c", a=4, c=64)[:, :, :, ::-1],
                                            xh[x_].bitcast(F32).rearrange("p a (r c) -> p a r c", c=64), ALU.subtract).then_inc(S("nol_ready"), 1)
                take_gated(PH[f"wo{l}"], n, l, 0, f"f{l}")
                recip(f"f{l}", n)
                modulate(l, 1, n)
                gate_up(PH[f"gu{l}"], n, FT * (l + 1))
                take_gated(PH[f"dn{l}"], n, l, 1, ("m1", "final")[l])
            recip("final", SEQ)
            for k in range(KT):
                V.scalar_tensor_tensor(y[:, k, 0:SEQ], h[:, k, 0:SEQ], par_ap("final", k, 1), rstd[:, 0:SEQ], ALU.mult, ALU.mult)\
                    .then_inc(S("final_ready"), 1)


def tiles_of(w):
    k, n = w.shape
    w = w.reshape(k // 1024, 2, HALF, P, n // 256, 256)
    return np.ascontiguousarray(w.transpose(4, 0, 1, 3, 2, 5)).reshape(-1, P, HALF, 256)


def feature_tiles(v):
    return np.ascontiguousarray(v.T.reshape(-1, P, v.shape[0]).transpose(1, 0, 2))


def gate_up_tiles(g, u):
    both = np.stack([g.reshape(D, FT, P), u.reshape(D, FT, P)], axis=2)
    return tiles_of(both.reshape(D, 2 * FF))


def down_tiles(w):
    padded = np.zeros((3 * 1024, D), w.dtype)
    padded[:FF] = w
    return tiles_of(padded)


def shape_tables():
    f = np.float32
    tab = np.eye(P, dtype=f)
    log_g = np.log(1.0 - 2.0 ** (-5.0 - np.arange(RET_H)))
    i = np.arange(SEQ)
    ret = np.zeros((P, RET_H * 384 + 2 * SEQ), f)
    for hd in range(RET_H):
        d = i[None, :] - i[:, None]
        full = np.where(d >= 0, np.exp(log_g[hd] * np.maximum(d, 0)), 0) * P ** -0.5
        ret[:, hd * 384:hd * 384 + 256] = full[0:P, :]
        ret[:, hd * 384 + 256:hd * 384 + 384] = full[P:, P:]
    freqs = f(10000.0) ** (-np.arange(64, dtype=f) / f(64))
    ang = np.arange(SEQ, dtype=f)[None, :] * np.concatenate([freqs, freqs])[:, None]
    ret[:, RET_H * 384:RET_H * 384 + SEQ] = np.cos(ang)
    ret[:, RET_H * 384 + SEQ:] = np.sin(ang) * np.where(np.arange(P) < 64, -1, 1)[:, None]
    fr = f(1.0) / (f(10000.0) ** (np.arange(0, 32, 2, dtype=f) / f(32)))
    pr, pc = (i // 64).astype(f), (i % 64).astype(f)
    ar, ac = fr[:, None] * pr[None, :], fr[:, None] * pc[None, :]
    half = np.concatenate([ar, ac, ar, ac])
    sign = np.where(np.arange(64) < 32, -1, 1)[:, None]
    rope_ = np.zeros((P, 2, SEQ), f)
    rope_[:, 0] = np.tile(np.cos(half), (2, 1))
    rope_[:, 1] = np.tile(np.sin(half) * sign, (2, 1))
    c = np.arange(64)
    start = np.clip(c - 8, 0, 48)
    inside = (c[None, :] >= start[:, None]) & (c[None, :] < start[:, None] + 16)
    mask_ = np.tile(np.where(inside, 0.0, NEG)[::-1], (2, 4)).astype(f)
    return tab, ret, rope_, mask_


def axial_order():
    one = np.concatenate([np.arange(0, 16), np.arange(32, 48), np.arange(16, 32), np.arange(48, 64)])
    return (np.arange(0, D, 64)[:, None] + one[None, :]).ravel()


def kernel(**inputs):
    import concourse.bacc as _bacc
    from concourse.bass_utils import run_bass_kernel_spmd as _run

    g = {k: np.asarray(v) for k, v in inputs.items()}
    w_in = g["w_in"][0]
    c = [w_in[:, 512 * k:512 * k + 512] for k in range(6)]
    w_in = np.concatenate([c[1], c[0], c[2], c[3], c[5], c[4]], axis=1)
    parts = [tiles_of(w_in), tiles_of(g["w_out"][0]),
             gate_up_tiles(g["w_ffn_gate"][0], g["w_ffn_up"][0]), down_tiles(g["w_ffn_down"][0]),
             g["w_ple_proj"][0].reshape(2, P, HALF, 256), tiles_of(g["w_ple_gate"][0])]
    for l in range(2):
        qkv = g["da_wqkv_2" if l == 0 else "na_wqkv_2"][0]
        q, k, v = qkv[:, :D], qkv[:, D:2 * D], qkv[:, 2 * D:]
        if l == 0:
            q, k = q[:, axial_order()], k[:, axial_order()]
        parts += [tiles_of(q), tiles_of(k), tiles_of(v), tiles_of(g["da_wo_2" if l == 0 else "na_wo_2"][0])]
        gu = g["ffn_w_gate_up_2"][l]
        parts += [gate_up_tiles(gu[:, :FF], gu[:, FF:]), down_tiles(g["ffn_w_down_2"][l])]
    wall = np.concatenate(parts)
    wada = g["ada_w_2"].transpose(0, 2, 1).reshape(2 * ADA_UNITS, P, D)
    col = lambda v: v.reshape(-1, P).T
    cond = np.stack([g["c_2"][0], g["c_ctx_2"]])
    conv_w = g["conv_dw_w"][0].T.reshape(CONV_T, P, CONV_W).transpose(1, 0, 2).reshape(P, -1)
    lam = np.concatenate([g["da_lambda_q1_2"][0], g["da_lambda_k1_2"][0], g["da_lambda_q2_2"][0], g["da_lambda_k2_2"][0]])
    vals = {"mix_pre": col(g["mix_pre_norm"][0]), "mix_post": col(g["mix_post_norm"][0]),
            "ffn_pre": col(g["ffn_pre_norm"][0]), "ffn_post": col(g["ffn_post_norm"][0]),
            "ple_post": col(g["ple_post_norm"][0]), "final": col(g["norm_final_2"]),
            "n_mix": col(g["norm_mix_2"].reshape(-1)), "n_ffn": col(g["norm_ffn_2"].reshape(-1)),
            "ada_b": col(g["ada_b_2"].reshape(-1)), "conv_w": conv_w, "conv_b": col(g["conv_dw_b"][0]),
            "ln_w": col(g["conv_ln_w"][0]), "ln_b": col(g["conv_ln_b"][0]),
            "subln": g["da_subln_2"][0].reshape(P, 1), "lam": np.broadcast_to(lam, (P, 256))}
    par = np.concatenate([vals[name] for name, _ in PCOLS], axis=1)
    tab, ret, rope_, mask_ = shape_tables()
    xin = feature_tiles(np.concatenate([g["x"][0], g["ctx_2"][0]], axis=0))
    arrays = {"wall": wall, "wada": wada, "cond": cond, "xin": xin, "pin": feature_tiles(g["p"][0, 0]), "par": par, "tab": tab, "tab_ret": ret,
              "tab_rope": rope_, "tab_mask": mask_, "rpb": g["na_rpb_2"][0]}
    nc = _bacc.Bacc("TRN2", target_bir_lowering=False, num_devices=1)
    args = []
    for name in arrays:
        a = arrays[name] = np.ascontiguousarray(arrays[name])
        args.append(nc.dram_tensor(name, a.shape, mybir.dt.from_np(a.dtype), kind="ExternalInput").ap())
    args.append(nc.dram_tensor("out_0", (P, KT, SEQ), F32, kind="ExternalOutput").ap())
    build(nc, *args)
    r = _run(nc, [arrays], core_ids=[0])
    got = r.results[0]["out_0"]
    return np.ascontiguousarray(got.transpose(2, 1, 0).reshape(1, SEQ, D))
```
